# Optimizing a Trainium2 kernel written in Bass

```python
import math
import jax, jax.numpy as jnp
from jax import lax
import numpy as np

D_MODEL = 1024
BATCH = 1
SEQ = 256
DEPTH = 1

GRID_W = 64
CTX_LEN = 256

GDN_DK = 128
GDN_DV = 128
GDN_HEADS = (D_MODEL // 2) // GDN_DV
GDN_QK = GDN_HEADS * GDN_DK
GDN_WIDTH = GDN_HEADS * GDN_DV
CONV_W = 5
RET_DK = 128
RET_DV = 128
RET_HEADS = (D_MODEL // 2) // RET_DV
RET_QK = RET_HEADS * RET_DK
RET_WIDTH = RET_HEADS * RET_DV
MIX_WIDTH = GDN_WIDTH + RET_WIDTH
CHUNK = 64
ROPE_THETA = 10000.0
IN_SIZES = (GDN_QK, GDN_QK, GDN_WIDTH, GDN_WIDTH, 2 * GDN_HEADS, 2 * GDN_HEADS,
            RET_QK, RET_QK, RET_WIDTH, RET_WIDTH)
IN_WIDTH = sum(IN_SIZES)
N_EXPERTS = 64
TOP_K = 8
N_GROUPS = 8
TOPK_GROUPS = 4
EXPERT_FF = 256
SHARED_FF = 256
ROUTED_SCALE = 2.5
DEEPNORM_ALPHA = (2 * DEPTH) ** 0.25
DEEPNORM_BETA = (8 * DEPTH) ** -0.25
LN_EPS = 1e-6

kernel_name = 'hybrid_gdn_retention_moe_deepnorm_dit'

def _layernorm(x, g=None, b=None):
    xf = x.astype(jnp.float32)
    mu = xf.mean(-1, keepdims=True)
    var = jnp.square(xf - mu).mean(-1, keepdims=True)
    y = (xf - mu) * lax.rsqrt(var + LN_EPS)
    if g is not None:
        y = y * g.astype(jnp.float32) + b.astype(jnp.float32)
    return y.astype(x.dtype)

def _rmsnorm(x, g):
    xf = x.astype(jnp.float32)
    y = xf * lax.rsqrt(jnp.mean(xf * xf, -1, keepdims=True) + LN_EPS) * g.astype(jnp.float32)
    return y.astype(x.dtype)

def _l2norm(u):
    uf = u.astype(jnp.float32)
    return (uf * lax.rsqrt(jnp.sum(uf * uf, -1, keepdims=True) + LN_EPS)).astype(u.dtype)

def _heads(u, h):
    B, L, _ = u.shape
    return u.reshape(B, L, h, -1).transpose(0, 2, 1, 3)

def _merge(u):
    B, h, L, d = u.shape
    return u.transpose(0, 2, 1, 3).reshape(B, L, h * d)

def _split_cols(p):
    offs = np.cumsum(IN_SIZES)[:-1].tolist()
    return jnp.split(p, offs, axis=-1)

def _modulate(x, shift, scale):
    return _layernorm(x) * (1 + scale) + shift

def _short_conv(u, w):
    C = u.shape[-1]
    pad = CONV_W // 2
    return lax.conv_general_dilated(u, w[:, None, :].astype(u.dtype), window_strides=(1,),
                                    padding=[(pad, pad)], dimension_numbers=('NWC', 'WIO', 'NWC'),
                                    feature_group_count=C)

def _axial_rope(rows, dim):
    row = jnp.repeat(jnp.arange(rows, dtype=jnp.float32), GRID_W)
    col = jnp.tile(jnp.arange(GRID_W, dtype=jnp.float32), rows)
    quarter = dim // 4
    inv = ROPE_THETA ** (-jnp.arange(quarter, dtype=jnp.float32) / quarter)
    ang = jnp.concatenate([row[:, None] * inv, col[:, None] * inv], -1)
    return jnp.cos(ang), jnp.sin(ang)

def _apply_rope(u, cos, sin):
    half = u.shape[-1] // 2
    u1, u2 = u[..., :half], u[..., half:]
    return jnp.concatenate([u1 * cos - u2 * sin, u1 * sin + u2 * cos], -1).astype(u.dtype)

def _gated_delta_scan(q, k, v, beta, g, s0, with_output):
    f32 = jnp.float32
    B, H, L, dk = k.shape
    dv = v.shape[-1]
    C = CHUNK
    N = L // C
    kc = k.reshape(B, H, N, C, dk).astype(f32)
    vc = v.reshape(B, H, N, C, dv).astype(f32)
    bc = beta.reshape(B, H, N, C).astype(f32)
    gcum = jnp.cumsum(g.reshape(B, H, N, C).astype(f32), axis=-1)
    causal = jnp.tril(jnp.ones((C, C), bool))
    strict = jnp.tril(jnp.ones((C, C), bool), -1)
    decay = jnp.exp(jnp.where(causal, gcum[..., :, None] - gcum[..., None, :], -jnp.inf))
    kk = jnp.einsum('bhncd,bhnmd->bhncm', kc, kc)
    lower = jnp.where(strict, kk * decay, 0.0) * bc[..., :, None]
    rhs = jnp.concatenate([vc * bc[..., None], kc * (bc * jnp.exp(gcum))[..., None]], -1)
    sol = lax.linalg.triangular_solve(lower + jnp.eye(C, dtype=f32), rhs, left_side=True,
                                      lower=True, unit_diagonal=True)
    u0, w = sol[..., :dv], sol[..., dv:]
    k_end = kc * jnp.exp(gcum[..., -1:] - gcum)[..., None]
    g_end = jnp.exp(gcum[..., -1])
    mv = lambda a: jnp.moveaxis(a, 2, 0)
    if with_output:
        qc = q.reshape(B, H, N, C, dk).astype(f32)
        intra = jnp.einsum('bhncd,bhnmd->bhncm', qc, kc) * decay
        q_dec = qc * jnp.exp(gcum)[..., None]

        def step(s, xs):
            u0_n, w_n, k_n, ge_n, qd_n, a_n = xs
            u = u0_n - jnp.einsum('bhcd,bhde->bhce', w_n, s)
            o = jnp.einsum('bhcd,bhde->bhce', qd_n, s) + jnp.einsum('bhcm,bhme->bhce', a_n, u)
            s = ge_n[..., None, None] * s + jnp.einsum('bhcd,bhce->bhde', k_n, u)
            return s, o

        s_fin, o = lax.scan(step, s0, (mv(u0), mv(w), mv(k_end), mv(g_end), mv(q_dec), mv(intra)))
        return jnp.moveaxis(o, 0, 2).reshape(B, H, L, dv).astype(v.dtype), s_fin

    def step_state(s, xs):
        u0_n, w_n, k_n, ge_n = xs
        u = u0_n - jnp.einsum('bhcd,bhde->bhce', w_n, s)
        return ge_n[..., None, None] * s + jnp.einsum('bhcd,bhce->bhde', k_n, u), None

    s_fin, _ = lax.scan(step_state, s0, (mv(u0), mv(w), mv(k_end), mv(g_end)))
    return None, s_fin

def _retention_scan(q, k, v, log_gamma, r0, with_output):
    f32 = jnp.float32
    B, H, L, dk = k.shape
    dv = v.shape[-1]
    C = CHUNK
    N = L // C
    lg = log_gamma.astype(f32)[:, None]
    pos = jnp.arange(C, dtype=f32)
    kc = k.reshape(B, H, N, C, dk).astype(f32)
    vc = v.reshape(B, H, N, C, dv).astype(f32)
    k_dec = kc * jnp.exp(lg * (C - 1 - pos))[None, :, None, :, None]
    chunk_decay = jnp.exp(lg[:, 0] * C)[None, :, None, None]
    mv = lambda a: jnp.moveaxis(a, 2, 0)
    if with_output:
        qc = q.reshape(B, H, N, C, dk).astype(f32)
        causal = jnp.tril(jnp.ones((C, C), bool))
        dmat = jnp.exp(jnp.where(causal, lg[:, :, None] * (pos[:, None] - pos[None, :]), -jnp.inf))
        intra = jnp.einsum('bhncd,bhnmd->bhncm', qc, kc) * dmat[None, :, None]
        q_dec = qc * jnp.exp(lg * (pos + 1))[None, :, None, :, None]

        def step(r, xs):
            kd_n, v_n, qd_n, a_n = xs
            o = jnp.einsum('bhcd,bhde->bhce', qd_n, r) + jnp.einsum('bhcm,bhme->bhce', a_n, v_n)
            return chunk_decay * r + jnp.einsum('bhcd,bhce->bhde', kd_n, v_n), o

        r_fin, o = lax.scan(step, r0, (mv(k_dec), mv(vc), mv(q_dec), mv(intra)))
        return jnp.moveaxis(o, 0, 2).reshape(B, H, L, dv).astype(v.dtype), r_fin

    def step_state(r, xs):
        kd_n, v_n = xs
        return chunk_decay * r + jnp.einsum('bhcd,bhce->bhde', kd_n, v_n), None

    r_fin, _ = lax.scan(step_state, r0, (mv(k_dec), mv(vc)))
    return None, r_fin

def _flip(t):
    return jnp.flip(t, axis=2)

def _gdn_mixer(parts_ctx, parts_lat, conv_w, a_log, dt_bias, norm_g, ctx_out):
    H = GDN_HEADS
    f32 = jnp.float32

    def prep(parts):
        q, k, v, z, b, a = parts
        qkv = jax.nn.silu(_short_conv(jnp.concatenate([q, k, v], -1), conv_w))
        q, k, v = jnp.split(qkv, [GDN_QK, 2 * GDN_QK], axis=-1)
        q = _l2norm(_heads(q, H)) * GDN_DK ** -0.5
        k = _l2norm(_heads(k, H))
        v = _heads(v, H)
        beta = jax.nn.sigmoid(b.astype(f32)).transpose(0, 2, 1)
        g = (-jnp.exp(a_log.astype(f32)) * jax.nn.softplus(a.astype(f32) + dt_bias.astype(f32))).transpose(0, 2, 1)
        return q, k, v, beta, g, z

    qc, kc, vc, bc, gc, zc = prep(parts_ctx)
    ql, kl, vl, bl, gl, zl = prep(parts_lat)
    s0 = jnp.zeros((kc.shape[0], H, GDN_DK, GDN_DV), f32)
    o_cf, s_f = _gated_delta_scan(qc, kc, vc, bc[:, :H], gc[:, :H], s0, ctx_out)
    o_lf, _ = _gated_delta_scan(ql, kl, vl, bl[:, :H], gl[:, :H], s_f, True)
    o_cb, s_b = _gated_delta_scan(_flip(qc), _flip(kc), _flip(vc), _flip(bc[:, H:]), _flip(gc[:, H:]), s0, ctx_out)
    o_lb, _ = _gated_delta_scan(_flip(ql), _flip(kl), _flip(vl), _flip(bl[:, H:]), _flip(gl[:, H:]), s_b, True)
    finish = lambda o, z: _merge(_rmsnorm(o, norm_g)) * jax.nn.silu(z)
    out_lat = finish(o_lf + _flip(o_lb), zl)
    out_ctx = finish(o_cf + _flip(o_cb), zc) if ctx_out else None
    return out_ctx, out_lat

def _retention_mixer(parts_ctx, parts_lat, log_gamma, norm_g, cos, sin, ctx_out):
    H = RET_HEADS

    def prep(parts, rope):
        q, k, v, gate = parts
        q = _heads(q, H)
        k = _heads(k, H) * RET_DK ** -0.5
        v = _heads(v, H)
        if rope:
            q = _apply_rope(q, cos, sin)
            k = _apply_rope(k, cos, sin)
        return q, k, v, gate

    qc, kc, vc, gtc = prep(parts_ctx, False)
    ql, kl, vl, gtl = prep(parts_lat, True)
    r0 = jnp.zeros((kc.shape[0], H, RET_DK, RET_DV), jnp.float32)
    o_cf, r_f = _retention_scan(qc, kc, vc, log_gamma[0], r0, ctx_out)
    o_lf, _ = _retention_scan(ql, kl, vl, log_gamma[0], r_f, True)
    o_cb, r_b = _retention_scan(_flip(qc), _flip(kc), _flip(vc), log_gamma[1], r0, ctx_out)
    o_lb, _ = _retention_scan(_flip(ql), _flip(kl), _flip(vl), log_gamma[1], r_b, True)
    finish = lambda o, gate: _merge(_layernorm(o)) * norm_g * jax.nn.silu(gate)
    out_lat = finish(o_lf + _flip(o_lb), gtl)
    out_ctx = finish(o_cf + _flip(o_cb), gtc) if ctx_out else None
    return out_ctx, out_lat

def _moe(h, w_router, router_bias, w_gate_up, w_down, w_shared_gate_up, w_shared_down):
    T = h.shape[0]
    s = jax.nn.sigmoid(h.astype(jnp.float32) @ w_router.astype(jnp.float32))
    sb = s + router_bias.astype(jnp.float32)
    per_group = N_EXPERTS // N_GROUPS
    gscore = lax.top_k(sb.reshape(T, N_GROUPS, per_group), 2)[0].sum(-1)
    _, gidx = lax.top_k(gscore, TOPK_GROUPS)
    gmask = jax.nn.one_hot(gidx, N_GROUPS, dtype=jnp.float32).sum(-2) > 0
    emask = jnp.repeat(gmask, per_group, axis=-1)
    _, eidx = lax.top_k(jnp.where(emask, sb, -jnp.inf), TOP_K)
    wsel = jnp.take_along_axis(s, eidx, axis=-1)
    wsel = wsel / wsel.sum(-1, keepdims=True) * ROUTED_SCALE
    gates = (jax.nn.one_hot(eidx, N_EXPERTS, dtype=jnp.float32) * wsel[..., None]).sum(1)
    gates = gates.T.astype(h.dtype)
    a_s, b_s = jnp.split(h @ w_shared_gate_up, 2, axis=-1)
    shared = (jax.nn.silu(a_s) * b_s) @ w_shared_down

    def expert_step(acc, xs):
        wgu, wd, ge = xs
        a, b = jnp.split(h @ wgu, 2, axis=-1)
        return acc + ge[:, None] * ((jax.nn.silu(a) * b) @ wd), None

    out, _ = lax.scan(expert_step, shared, (w_gate_up, w_down, gates))
    return out

def setup_inputs(seed: int = 0) -> dict:
    key = jax.random.key(seed)
    ks = jax.random.split(key, 24)
    f32 = jnp.float32
    nrm = lambda k, shape, scale: jax.random.normal(k, shape, f32) * scale
    D, E, F = D_MODEL, N_EXPERTS, EXPERT_FF
    dt = jnp.exp(jax.random.uniform(ks[9], (DEPTH, 2 * GDN_HEADS), f32, math.log(1e-3), math.log(1e-1)))
    base_gamma = jnp.log(1.0 - 2.0 ** (-5.0 - jnp.arange(RET_HEADS, dtype=f32)))
    return {
        'x': nrm(ks[0], (BATCH, SEQ, D), 1.0),
        'c': nrm(ks[1], (BATCH, D), 1.0),
        'ctx': nrm(ks[2], (BATCH, CTX_LEN, D), 1.0),
        'c_ctx': nrm(ks[3], (D,), 1.0),
        'w_mod': nrm(ks[4], (DEPTH, D, 6 * D), D ** -0.5),
        'b_mod': nrm(ks[5], (DEPTH, 6 * D), 0.02),
        'w_in': nrm(ks[6], (DEPTH, D, IN_WIDTH), D ** -0.5),
        'conv_w': nrm(ks[7], (DEPTH, CONV_W, 2 * GDN_QK + GDN_WIDTH), CONV_W ** -0.5),
        'gdn_a_log': jnp.log(jax.random.uniform(ks[8], (DEPTH, 2 * GDN_HEADS), f32, 1.0, 16.0)),
        'gdn_dt_bias': dt + jnp.log(-jnp.expm1(-dt)),
        'gdn_norm_g': 1.0 + nrm(ks[10], (DEPTH, GDN_DV), 0.02),
        'ret_log_gamma': base_gamma * jnp.exp(nrm(ks[11], (DEPTH, 2, RET_HEADS), 0.05)),
        'ret_norm_g': 1.0 + nrm(ks[12], (DEPTH, RET_WIDTH), 0.02),
        'w_out': nrm(ks[13], (DEPTH, MIX_WIDTH, D), DEEPNORM_BETA * MIX_WIDTH ** -0.5),
        'ln1_g': 1.0 + nrm(ks[14], (DEPTH, D), 0.02),
        'ln1_b': nrm(ks[15], (DEPTH, D), 0.02),
        'w_router': nrm(ks[16], (DEPTH, D, E), D ** -0.5),
        'router_bias': nrm(ks[17], (DEPTH, E), 0.01),
        'w_gate_up': nrm(ks[18], (DEPTH, E, D, 2 * F), D ** -0.5),
        'w_down': nrm(ks[19], (DEPTH, E, F, D), DEEPNORM_BETA * F ** -0.5),
        'w_shared_gate_up': nrm(ks[20], (DEPTH, D, 2 * SHARED_FF), D ** -0.5),
        'w_shared_down': nrm(ks[21], (DEPTH, SHARED_FF, D), DEEPNORM_BETA * SHARED_FF ** -0.5),
        'ln2_g': 1.0 + nrm(ks[22], (DEPTH, D), 0.02),
        'ln2_b': nrm(ks[23], (DEPTH, D), 0.02),
    }

def reference(x, c, ctx, c_ctx, w_mod, b_mod, w_in, conv_w, gdn_a_log, gdn_dt_bias, gdn_norm_g,
              ret_log_gamma, ret_norm_g, w_out, ln1_g, ln1_b, w_router, router_bias, w_gate_up, w_down,
              w_shared_gate_up, w_shared_down, ln2_g, ln2_b):
    B, L, D = x.shape
    Lc = ctx.shape[1]
    ROWS = L // GRID_W
    cos, sin = _axial_rope(ROWS, RET_DK)
    for layer in range(DEPTH):
        last = layer == DEPTH - 1
        mod_lat = (jax.nn.silu(c) @ w_mod[layer] + b_mod[layer])[:, None, :]
        mod_ctx = (jax.nn.silu(c_ctx[None]) @ w_mod[layer] + b_mod[layer])[:, None, :]
        sh1, sc1, g1, sh2, sc2, g2 = jnp.split(mod_lat, 6, axis=-1)
        csh1, csc1, cg1, csh2, csc2, cg2 = jnp.split(mod_ctx, 6, axis=-1)
        p_lat = _split_cols(_modulate(x, sh1, sc1) @ w_in[layer])
        p_ctx = _split_cols(_modulate(ctx, csh1, csc1) @ w_in[layer])
        a_ctx, a_lat = _gdn_mixer(p_ctx[:6], p_lat[:6], conv_w[layer], gdn_a_log[layer], gdn_dt_bias[layer],
                                  gdn_norm_g[layer], not last)
        r_ctx, r_lat = _retention_mixer(p_ctx[6:], p_lat[6:], ret_log_gamma[layer], ret_norm_g[layer],
                                        cos, sin, not last)
        y_lat = jnp.concatenate([a_lat, r_lat], -1) @ w_out[layer]
        x = _layernorm(DEEPNORM_ALPHA * x + g1 * y_lat, ln1_g[layer], ln1_b[layer])
        moe_w = (w_router[layer], router_bias[layer], w_gate_up[layer], w_down[layer],
                 w_shared_gate_up[layer], w_shared_down[layer])
        h_lat = _modulate(x, sh2, sc2).reshape(B * L, D)
        if last:
            f_lat = _moe(h_lat, *moe_w).reshape(B, L, D)
        else:
            y_ctx = jnp.concatenate([a_ctx, r_ctx], -1) @ w_out[layer]
            ctx = _layernorm(DEEPNORM_ALPHA * ctx + cg1 * y_ctx, ln1_g[layer], ln1_b[layer])
            h_ctx = _modulate(ctx, csh2, csc2).reshape(B * Lc, D)
            f_all = _moe(jnp.concatenate([h_ctx, h_lat], 0), *moe_w)
            f_lat = f_all[B * Lc:].reshape(B, L, D)
            ctx = _layernorm(DEEPNORM_ALPHA * ctx + cg2 * f_all[:B * Lc].reshape(B, Lc, D), ln2_g[layer], ln2_b[layer])
        x = _layernorm(DEEPNORM_ALPHA * x + g2 * f_lat, ln2_g[layer], ln2_b[layer])
    return x


_drawn_inputs = setup_inputs


def setup_inputs(seed=0):
    import zlib

    import numpy as np

    out = dict(_drawn_inputs(seed))
    spreads = {}
    factors = {'gdn_norm_g': 4.01, 'ret_norm_g': 3.532, 'ln2_g': 2.844, 'ln2_b': 2.91}
    for name, (base, spread) in spreads.items():
        noise = np.random.default_rng([zlib.crc32(name.encode()), seed]).standard_normal(out[name].shape)
        drawn = base * np.exp(spread * noise) if base else spread * noise
        out[name] = __import__('jax').numpy.asarray(drawn.astype(out[name].dtype))
    for name, factor in factors.items():
        out[name] = (out[name] * factor).astype(out[name].dtype)
    return out
```

```python
import math
from contextlib import ExitStack

import numpy as np

import concourse.bass as bass
from concourse import mybir

F32 = mybir.dt.float32
I32 = mybir.dt.int32
ALU = mybir.AluOpType
ACT = mybir.ActivationFunctionType

D, T, CTX, H, DK = 1024, 256, 256, 4, 128
NT = (T + CTX) // 128
KB = D // 128
C = 64
E, TOPK, GROUPS, TOPG, FF = 64, 8, 8, 4, 256
CAP = 64
ITEMS = 100
LEVELS = 6
EPS = 1e-6
ALPHA = 2.0 ** 0.25
BIG = 1048576.0
BETA_G = 8
Q0, K0, V0, Z0, BA0, RQ0, RK0, RV0, RG0 = 0, 512, 1024, 1536, 2048, 2064, 2576, 3088, 3600
CHUNKCOLS = 512

CONST = {}
_at = 0
for _n, _w in [("ident", 128), ("trif", 128), ("trib", 128), ("blk", 128), ("strict", 128), ("ones", 128),
               ("ymask", LEVELS * 2 * 64), ("u1mask", 2 * 64), ("neg", 2 * 64), ("i64", 64), ("iota64", 64),
               ("item", ITEMS), ("item64", ITEMS), ("cos", 256), ("sin", 256), ("part", 1)]:
    CONST[_n] = (_at, _w)
    _at += _w
NCONST = _at
NDIST = 2 * 1024 + 2 * 512


def constants():
    c = np.zeros((128, NCONST), np.float32)

    def put(name, a):
        o, w = CONST[name]
        c[:, o:o + w] = a

    p = np.arange(128)[:, None]
    f = np.arange(128)[None, :]
    same = (p // C) == (f // C)
    put("ident", p == f)
    put("trif", same & (p <= f))
    put("trib", same & (p >= f))
    put("blk", same)
    put("strict", p < f)
    put("ones", 1.0)
    i = p % C
    j = np.arange(C)[None, :]
    eye = (i == j).astype(np.float32)

    def lower(b):
        return ((i // (2 * b)) == (j // (2 * b))) & ((i // b) % 2 == 1) & ((j // b) % 2 == 0)

    def upper(b):
        return ((i // (2 * b)) == (j // (2 * b))) & ((i // b) % 2 == 0) & ((j // b) % 2 == 1)

    put("ymask", np.concatenate([eye - m(1 << l) for l in range(LEVELS) for m in (lower, upper)], 1))
    put("u1mask", np.concatenate([eye - upper(1), eye - lower(1)], 1))
    put("neg", np.concatenate([np.where(j > i, 0.0, -1e30), np.where(j < i, 0.0, -1e30)], 1))
    put("i64", eye)
    put("iota64", j)
    it = np.arange(ITEMS)[None, :]
    put("item", it)
    put("item64", it * float(CAP))
    t = np.arange(T)
    quarter = DK // 4
    inv = (np.float32(10000.0) ** (-np.arange(quarter, dtype=np.float32) / np.float32(quarter))).astype(np.float32)
    row, col = (t // 64).astype(np.float32), (t % 64).astype(np.float32)
    ang = np.concatenate([row[:, None] * inv, col[:, None] * inv], -1).astype(np.float32).T
    cos, sin = np.cos(ang), np.sin(ang)
    put("cos", np.concatenate([cos, cos], 0))
    put("sin", np.concatenate([sin, -sin], 0))
    put("part", p)
    d = np.zeros((128, NDIST), np.float32)
    q = np.arange(T)[None, :]
    for k in range(4):
        key = p + 128 * (k % 2)
        if k < 2:
            fwd, bwd = CTX + q - key, T - q + key
        else:
            fwd, bwd = np.maximum(q - key, 0), np.maximum(key - q, 0)
            d[:, 2048 + 256 * (k - 2):2048 + 256 * (k - 1)] = q >= key
            d[:, 2560 + 256 * (k - 2):2560 + 256 * (k - 1)] = q <= key
        d[:, 256 * k:256 * k + 256] = fwd
        d[:, 1024 + 256 * k:1024 + 256 * k + 256] = bwd
    return c, d


def bank_uses():
    u = ["small", "convw"] + [("mod1", i) for i in range(4)] + [("xT", k) for k in range(KB)]
    for g in range(12):
        u.append(("gdn", g))
        if g == 3:
            u.append("ba")
        if g >= 2:
            u.append(("toTok", g - 2))
        if g >= 4 and g - 4 not in range(4, 8):
            u.append(("toChan", g - 4))
        if g == 5:
            u.append("gcum")
        if g == 6:
            u += ["rows", "gend"]
    u += [("toTok", 10), ("toTok", 11)] + [("toChan", g) for g in (8, 9, 10, 11)]
    for h in range(H):
        u += [("kk", h), ("bc", 0, h), ("bc", 1, h)]
    for g in range(4):
        u.append(("T1", g))
    for l in range(1, LEVELS):
        u += [("X", l, g) for g in range(4)]
        for g in range(4):
            u += ([("T", l, g)] if l < LEVELS - 1 else []) + [("U", l, g)]
    u += [("eg", h) for h in range(H)]
    fill = filler()
    for s in range(8):
        u += [("nw", 0, s), ("nw", 1, s)] if s else []
        u.append(("u", s))
        u += fill[s]
        u += [("S", 0, s), ("S", 1, s)] if s < 7 else []
    u += [("o", 0), ("o", 1)]
    u += fill[8]
    u += [("mT", k) for k in range(4)]
    u += [("g1", 0), ("g1", 1)]
    u += [("y", a, b) for a in range(2) for b in range(2)]
    u += [("mod2", i) for i in range(4)] + [("hT", k) for k in range(4)] + ["lg"] + [("hk", k) for k in range(4)] + [("g2", 0), ("g2", 1)]
    u += ["rank", "cnt", "start", "selT", "item", "itrow"]
    u += [("sh", 0), ("sh", 1), ("shT", 0), ("shT", 1)]
    return u


def filler():
    f = [[] for _ in range(9)]
    rk = [("rk", h) for h in range(4)]
    rq = [("rq", h) for h in range(4)]
    rv = [("rv", t) for t in range(4)]
    z = [("z", t) for t in range(2)]
    gt = [("gt", t) for t in range(2)]
    f[0], f[1], f[2] = rk[:2], rk[2:], rq
    f[3], f[4] = rv[:2], rv[2:]
    f[5], f[6] = z, gt
    sc = [("sc", h, a) for h in range(H) for a in range(2)]
    f[8] = sc[:2] + [("ro", 0), ("ro", 1)] + sc[2:]
    return f


class Banks:

    def __init__(self, psum, filled, emptied):
        uses = bank_uses()
        self.at = {name: (n % 8, n // 8) for n, name in enumerate(uses)}
        assert len(self.at) == len(uses)
        self.psum, self.filled, self.emptied = psum, filled, emptied
        self.total = [len([0 for b, _ in self.at.values() if b == k]) for k in range(8)]

    def __getitem__(self, name):
        return self.psum[self.at[name][0]]

    def open(self, pe, name):
        b, n = self.at[name]
        if n:
            pe.wait_ge(self.emptied[b], n)

    def close(self, ins, name):
        ins.then_inc(self.filled[self.at[name][0]], 1)

    def wait_filled(self, eng, name):
        b, n = self.at[name]
        eng.wait_ge(self.filled[b], n + 1)

    def read(self, ins, name):
        ins.then_inc(self.emptied[self.at[name][0]], 1)

    def wait_read(self, eng, name):
        b, n = self.at[name]
        eng.wait_ge(self.emptied[b], n + 1)


SEMS = """consts_in small_in x_in dist_in rows_in ba_in router_in lnrows_in xres_in ln2_in norms_in rbias_in bmodr_in
root_in root_out sil xn modcols conv_raw conv_acc conv_silu squared gate_raw gate_exp gates_ready decay_arg gexp rows_ready
u1_ready dt_arg dt_exp at_ready qd_exp qd_ready step_in s_scaled raw_ready rope_done decay_exp decay_ready ro_done
z_ready g_ready mix_sq mix_ready x1n_ready lg_exp lg_bias sel_ready posx_ready counts_ready items_ready table_ready
sh_silu sh_gated shared_done final_norm out_ready out_in
vstep astep pstep gu_in0 gu_in1 dn_in0 dn_in1 gu_free dn_free
pick_ready gatherA gatherB hidA hidB gu_done silu_done gated flip_done flipped yA yB outA outB scattered""".split()


def chunks(a):
    def cols(w, c0, n=CHUNKCOLS):
        return w[:, c0:c0 + n].rearrange("(k p) n -> p k n", p=128)
    wm, wi, wo = a["w_mod"][0], a["w_in"][0], a["w_out"][0]
    out = [(("mod1", i), cols(wm, 512 * i)) for i in range(4)]
    out += [("gk", cols(wi, K0)), ("gv", cols(wi, V0)), ("gq", cols(wi, Q0)), ("rk", cols(wi, RK0)),
            ("rq", cols(wi, RQ0)), ("rv", cols(wi, RV0)), ("z", cols(wi, Z0)), ("gt", cols(wi, RG0))]
    out += [(("g1", i), cols(wm, 2048 + 512 * i)) for i in range(2)]
    out += [(("wo", i), cols(wo, 512 * i)) for i in range(2)]
    out += [(("mod2", i), cols(wm, 3072 + 512 * i)) for i in range(4)]
    out += [(("g2", i), cols(wm, 5120 + 512 * i)) for i in range(2)]
    out += [("shgu", cols(a["w_shared_gate_up"][0], 0))]
    out += [("shdn", a["w_shared_down"][0].rearrange("(k p) n -> p k n", p=128))]
    return out


RING = 3
LAST_USE = {"gk": ("gdn", 3), "gv": ("gdn", 7), "gq": ("gdn", 11), "rk": ("rk", 3), "rq": ("rq", 3), "rv": ("rv", 3),
            "z": ("z", 1), "gt": ("gt", 1), "shgu": ("sh", 1), ("wo", 0): ("y", 0, 1), ("wo", 1): ("y", 1, 1)}


def program(nc, a, out):
    with ExitStack() as ctx:
        arena = ctx.enter_context(nc.sbuf_tensor("arena", [128, 49152], F32))
        const = ctx.enter_context(nc.sbuf_tensor("constants", [128, NCONST], F32))
        psum = [ctx.enter_context(nc.psum_tensor(f"bank{i}", [128, 512], F32)) for i in range(8)]
        S = {n: ctx.enter_context(nc.semaphore(n)) for n in SEMS}
        ring_in = [ctx.enter_context(nc.semaphore(f"ring_in{i}")) for i in range(RING)]
        filled = [ctx.enter_context(nc.semaphore(f"filled{i}")) for i in range(8)]
        emptied = [ctx.enter_context(nc.semaphore(f"emptied{i}")) for i in range(8)]
        banks = Banks(psum, filled, emptied)

        def small(name, shape, dt=F32):
            return ctx.enter_context(nc.sbuf_tensor(name, shape, dt))

        rows64 = small("rows64", [64, 128])
        colsT = small("colsT", [128, 64])
        sil = small("sil", [128, 16])
        convw = small("convw", [128, 60])
        modc = small("modc", [128, 32])
        mod2 = small("mod2", [128, 16])
        st = small("st", [128, 64])
        mv = small("mv", [128, 32])
        GB = small("GB", [128, 64])
        gates = small("gates", [128, 8 * 32])
        ssq = small("ssq", [128, 48])
        ge = small("ge", [128, 64])
        small_consts = small("small_consts", [128, 32])
        eidx = small("eidx", [1, ITEMS + 4], I32)
        route = small("route", [128, 64])
        cst = {n: const[:, o:o + w] for n, (o, w) in CONST.items()}
        ident = cst["ident"]

        def A(off, n):
            return arena[:, off:off + n]

        ringbuf = [A(4096 * i, 4096).rearrange("p (k n) -> p k n", k=KB) for i in range(RING)]
        dist = A(12288, 3072)
        decayB = A(15360, 1024)
        ktok = A(16384, 2048).rearrange("p (t h d) -> p t h d", t=NT, h=H)
        vtok = A(18432, 2048).rearrange("p (t h d) -> p t h d", t=NT, h=H)
        kch = A(20480, 2048).rearrange("p (h t) -> p h t", h=H)
        decay = A(20480, 2048).rearrange("p (b n) -> p b n", b=2)
        kend = A(22528, 1024).rearrange("p (b h d) -> p b h d", b=2, h=H)
        nwT = A(23552, 1024).rearrange("p (b d h i) -> p b d h i", b=2, d=2, h=H)
        xmT = A(24576, 4096).rearrange("p (k t) -> p k t", k=KB)
        xall = A(28672, 4096).rearrange("p (t n) -> p t n", t=NT)
        state = A(28672, 4096).rearrange("p (s d h e) -> p s d h e", s=4, d=2, h=H)
        LT = A(32768, 2048).rearrange("p (d h t i) -> p d h t i", d=2, h=H, t=NT)
        vbeta = A(32768, 1024).rearrange("p (b h d) -> p b h d", b=2, h=H)
        kbeta = A(33792, 1024).rearrange("p (b h d) -> p b h d", b=2, h=H)
        Tm = A(34816, 2048).rearrange("p (d h t i) -> p d h t i", d=2, h=H, t=NT)
        usav = A(34816, 2048).rearrange("p (d t h e) -> p d t h e", d=2, t=2, h=H)
        Ym = A(36864, 2048).rearrange("p (d h t i) -> p d h t i", d=2, h=H, t=NT)
        qdec = A(36864, 2048).rearrange("p (d h t) -> p d h t", d=2, h=H)
        Um = A(38912, 2048).rearrange("p (d h t i) -> p d h t i", d=2, h=H, t=NT)
        AT = A(40960, 1024).rearrange("p (d h t i) -> p d h t i", d=2, h=H, t=2)
        convbuf = A(41984, 1040).rearrange("p (b s n) -> p b s n", b=2, s=2)
        convout = A(43024, 1024).rearrange("p (b n) -> p b n", b=2)
        rch = A(41984, 3072)
        rk = rch[:, 0:2048].rearrange("p (h t) -> p h t", h=H)
        rq = rch[:, 2048:3072].rearrange("p (h t) -> p h t", h=H)
        qch = A(45056, 1024).rearrange("p (h t) -> p h t", h=H)
        zs = A(45056, 1024).rearrange("p (t n) -> p t n", t=2)
        tmp = A(46080, 1024)
        raw = tmp.rearrange("p (b n) -> p b n", b=2)
        gs = tmp.rearrange("p (t n) -> p t n", t=2)
        rv = A(47104, 2048).rearrange("p (t n) -> p t n", t=NT)
        rowsT = A(23552, 128)[0:64, :]
        wba = A(47104, 128).rearrange("p (k n) -> p k n", k=KB)
        cwrows = A(36864, 1536)
        qtok = A(46080, 512).rearrange("p (b t d) -> p b t d", b=2, t=2)
        dtmp = A(46592, 512).rearrange("p (b t i) -> p b t i", b=2, t=NT)
        egb = A(46080, 1024).rearrange("p (b d n) -> p b d n", b=2, d=2)
        norms = A(38912, 640)
        junk = A(47360, 512)
        mix = A(24576, 2048).rearrange("p (t n) -> p t n", t=2)
        mixT = A(26624, 2048).rearrange("p (k t) -> p k t", k=KB)
        xres = A(28672, 2048).rearrange("p (t n) -> p t n", t=2)
        g1b = A(30720, 1024)
        lnr = A(34816, 2048)
        h_t = A(36864, 2048).rearrange("p (t n) -> p t n", t=2)
        x1 = A(38912, 2048).rearrange("p (t n) -> p t n", t=2)
        hT = A(41984, 2048).rearrange("p (k t) -> p k t", k=KB)
        htok = A(47104, 2048).rearrange("p (t n) -> p t n", t=2)
        g2b = A(46080, 1024)
        wr = A(32768, 512).rearrange("p (k n) -> p k n", k=KB)
        bmodr = A(44032, 2048)[0:1, :]
        rt = {n: A(33280 + 128 * i, 128).rearrange("p (t e) -> p t e", t=2)
              for i, n in enumerate(["s", "sb", "masked", "work", "sel", "gate", "posx", "max8"])}
        itemT = A(31232, 512)[0:64, :]
        onehot = A(31744, ITEMS)[0:64, :]
        rbias = A(31844, 64)
        g8 = A(31908, 64)
        tab = A(34304, 4 * ITEMS)
        gu_w = [A(8192 * i, 8192).rearrange("p (j k n) -> p j k n", j=2, k=KB) for i in range(2)]
        dn_w = [A(16384 + 4096 * i, 4096).rearrange("p (j k n) -> p j k n", j=2, k=2) for i in range(2)]
        pick = A(24576, 512).rearrange("p (b t s) -> p b t s", b=2, t=2)
        pickg = A(25088, 512).rearrange("p (b t s) -> p b t s", b=2, t=2)
        flip = A(25600, 1024).rearrange("p (b n) -> p b n", b=2)
        hid = A(26624, 2048).rearrange("p (b k s) -> p b k s", b=2, k=KB)
        ybuf = A(28672, 1024)
        sa = A(29696, 512).rearrange("p (t n) -> p t n", t=2)
        gbuf = A(30208, 512).rearrange("p (b n) -> p b n", b=2)
        shgT = A(30720, 512).rearrange("p (k t) -> p k t", k=2)
        tabv = tab.rearrange("p (w t i) -> p w t i", w=2, t=2)
        gcol = lambda w: gates[:, 32 * w:32 * w + 32]
        BETA, GRAW, EG, NBEG, KEND, GT, EGT, SCR = range(8)
        junk2 = A(22528, 512)

        def unit(m, g):
            return m[:, g // 2, 2 * (g % 2):2 * (g % 2) + 2].rearrange("p h t i -> p (h t) i")

        def hT_out(eng, k, modulate):
            use = ("hT", k)
            banks.wait_read(eng, ("mod2", 3))
            banks.wait_filled(eng, use)
            for i in range(2):
                m = 2 * k + i
                ins = modulate(hT[:, m, :], banks[use][:, 256 * i:256 * i + 256], mod2[:, 8 + m:9 + m], mod2[:, m:m + 1])
            banks.read(ins, use)

        CH = chunks(a)
        CI = {n: i for i, (n, _) in enumerate(CH)}
        block = ctx.enter_context(nc.Block())

        def rowcol(m, d, h):
            return m[:, 16 * d + h:16 * d + 16:4]

        def where(d, s):
            n = s if d == 0 else (3 - s if s < 4 else 11 - s)
            return n // 2, n % 2

        def trips_of(eng):
            n = eng.value_load(eidx[0:1, ITEMS:ITEMS + 1], min_val=1, max_val=96)
            return eng.snap((n + 3) // 4)

        @block.sync
        def _(sp):
            x2, ctx2 = a["x"][0], a["ctx"][0]
            sp.dma_start(rows64[0:8, :], a["c"].rearrange("a (k p) -> (a k) p", p=128)).then_inc(S["small_in"], 16)
            sp.dma_start(rows64[8:16, :], a["c_ctx"].rearrange("(k p) -> k p", p=128)).then_inc(S["small_in"], 16)
            sp.dma_start(rows64[16:64, :], a["b_mod"].rearrange("a (k p) -> (a k) p", p=128)).then_inc(S["small_in"], 16)
            sp.dma_start(const[:, :], a["const"]).then_inc(S["consts_in"], 16)

            def load_chunk(n):
                if n >= RING:
                    before = CH[n - RING][0]
                    banks.wait_filled(sp, LAST_USE.get(before, before))
                src = CH[n][1]
                o = 4096 * (n % RING)
                dst = ringbuf[n % RING] if src.shape[1] == KB else A(o, 2048).rearrange("p (k n) -> p k n", k=2)
                sp.dma_start(dst, src).then_inc(ring_in[n % RING], 16)

            load_chunk(0)
            for t in range(NT):
                src = ctx2 if t < 2 else x2
                sp.dma_start(xall[:, t, :], src[128 * (t % 2):128 * (t % 2) + 128, :]).then_inc(S["x_in"], 16)
            load_chunk(1)
            load_chunk(2)
            sp.dma_start(cwrows[0:5, :], a["conv_w"][0]).then_inc(S["rows_in"], 16)
            sp.dma_start(small_consts[:, 0:8], a["gdn_a_log"].to_broadcast([128, 8])).then_inc(S["rows_in"], 16)
            sp.dma_start(small_consts[:, 8:16], a["gdn_dt_bias"].to_broadcast([128, 8])).then_inc(S["rows_in"], 16)
            sp.dma_start(small_consts[:, 16:24], a["ret_log_gamma"][0].rearrange("d h -> (d h)").unsqueeze(0).to_broadcast([128, 8])).then_inc(S["rows_in"], 16)
            sp.dma_start(wba, a["w_in"][0][:, BA0:BA0 + 16].rearrange("(k p) n -> p k n", p=128)).then_inc(S["ba_in"], 16)
            for n in range(RING, len(CH)):
                name = CH[n][0]
                if name == "rq":
                    sp.dma_start(dist, a["dist"]).then_inc(S["dist_in"], 16)
                if name == ("g1", 0):
                    banks.wait_filled(sp, ("u", 7))
                    sp.dma_start(norms[:, 0:128], a["gdn_norm_g"].to_broadcast([128, 128])).then_inc(S["norms_in"], 16)
                    sp.dma_start(norms[:, 128:640], a["ret_norm_g"].to_broadcast([128, 512])).then_inc(S["norms_in"], 16)
                    banks.wait_filled(sp, ("o", 1))
                    for t in range(2):
                        sp.dma_start(xres[:, t, :], x2[128 * t:128 * t + 128, :]).then_inc(S["xres_in"], 16)
                    sp.dma_start(lnr[:, 0:1024], a["ln1_g"].to_broadcast([128, D])).then_inc(S["lnrows_in"], 16)
                    sp.dma_start(lnr[:, 1024:2048], a["ln1_b"].to_broadcast([128, D])).then_inc(S["lnrows_in"], 16)
                    sp.dma_start(wr, a["w_router"][0].rearrange("(k p) n -> p k n", p=128)).then_inc(S["router_in"], 16)
                    sp.wait_ge(S["mix_ready"], 4)
                    sp.dma_start(bmodr[:, 0:1024], a["b_mod"][:, 2048:3072]).then_inc(S["bmodr_in"], 16)
                    sp.dma_start(bmodr[:, 1024:2048], a["b_mod"][:, 5120:6144]).then_inc(S["bmodr_in"], 16)
                    sp.dma_start(rbias, a["router_bias"].to_broadcast([128, E])).then_inc(S["rbias_in"], 16)
                load_chunk(n)
            sp.wait_ge(S["x1n_ready"], 2)
            sp.dma_start(lnr[:, 0:1024], a["ln2_g"].to_broadcast([128, D])).then_inc(S["ln2_in"], 16)
            sp.dma_start(lnr[:, 1024:2048], a["ln2_b"].to_broadcast([128, D])).then_inc(S["ln2_in"], 16)
            sp.wait_ge(S["table_ready"], 1)
            trips = trips_of(sp)
            with sp.Fori(0, trips) as it:
                for u in range(2):
                    es = [sp.value_load(eidx[0:1, bass.ds(it * 4 + (2 * u + j), 1)], min_val=0, max_val=E - 1) for j in range(2)]
                    sp.wait_ge(S["gu_free"], it * 2 + (u + 1))
                    for j in range(2):
                        src = a["w_gate_up"][0, bass.ds(es[j], 1)].rearrange("a (k p) n -> p (a k) n", p=128)
                        sp.dma_start(gu_w[u][:, j], src).then_inc(S[f"gu_in{u}"], 16)
                    sp.wait_ge(S["dn_free"], it * 2 + (u + 1))
                    for j in range(2):
                        src = a["w_down"][0, bass.ds(es[j], 1)].rearrange("a (k p) n -> p (a k) n", p=128)
                        sp.dma_start(dn_w[u][:, j], src).then_inc(S[f"dn_in{u}"], 16)
            for t in range(2):
                sp.wait_ge(S["out_ready"], 1 + t)
                sp.dma_start(out[0, 128 * t:128 * t + 128, :], h_t[:, t, :]).then_inc(S["out_in"], 16)
            sp.wait_ge(S["out_in"], 32)

        @block.tensor
        def _(pe):
            mm, tr = nc.tensor.matmul, nc.tensor.transpose

            def chunk(name):
                n = CI[name]
                pe.wait_ge(ring_in[n % RING], 16 * (n // RING + 1))
                return ringbuf[n % RING]

            pe.wait_ge(S["consts_in"], 16)
            pe.wait_ge(S["small_in"], 48)
            b = banks["small"]
            banks.close(tr(b[:, 0:64], rows64[:, :], ident[0:64, 0:64]), "small")
            pe.wait_ge(S["rows_in"], 64)
            b = banks["convw"]
            for i in range(12):
                ins = tr(b[:, 5 * i:5 * i + 5], cwrows[0:5, 128 * i:128 * i + 128], ident[0:5, 0:5])
            banks.close(ins, "convw")

            def mod_cols(use, vecs):
                w = chunk(use)
                banks.open(pe, use)
                b = banks[use]
                for m in range(4):
                    for k in range(KB):
                        rhs = sil[:, k:k + 9:8] if vecs == 2 else sil[:, k:k + 1]
                        ins = mm(b[:, vecs * m:vecs * m + vecs], w[:, k, 128 * m:128 * m + 128], rhs,
                                 start=(k == 0), stop=(k == KB - 1))
                banks.close(ins, use)

            pe.wait_ge(S["sil"], 1)
            for i in range(4):
                mod_cols(("mod1", i), 2)
            for k in range(KB):
                banks.open(pe, ("xT", k))
                b = banks[("xT", k)]
                for t in range(NT):
                    if k == 0:
                        pe.wait_ge(S["xn"], t + 1)
                    ins = tr(b[:, 128 * t:128 * t + 128], xall[:, t, 128 * k:128 * k + 128], ident)
                banks.close(ins, ("xT", k))

            def channel(use, name, h, cols):
                w = chunk(name)
                banks.open(pe, use)
                b = banks[use]
                n = cols.stop - cols.start
                for k in range(KB):
                    ins = mm(b[:, 0:n], w[:, k, 128 * h:128 * h + 128], xmT[:, k, cols], start=(k == 0), stop=(k == KB - 1))
                banks.close(ins, use)

            def tokens(use, name, t):
                w = chunk(name)
                banks.open(pe, use)
                b = banks[use]
                for k in range(KB):
                    ins = mm(b[:, :], xmT[:, k, 128 * t:128 * t + 128], w[:, k, :], start=(k == 0), stop=(k == KB - 1))
                banks.close(ins, use)

            def to_tok(g):
                use = ("toTok", g)
                banks.open(pe, use)
                pe.wait_ge(S["conv_silu"], g + 1)
                b = banks[use]
                for t in range(4 if g < 8 else 2):
                    ins = tr(b[:, 128 * t:128 * t + 128], convout[:, g % 2, 128 * t:128 * t + 128], ident)
                banks.close(ins, use)

            def to_chan(g):
                use = ("toChan", g)
                banks.open(pe, use)
                banks.wait_read(pe, ("toTok", g))
                b = banks[use]
                for t in range(4 if g < 8 else 2):
                    src = ktok[:, t, g, :] if g < 8 else qtok[:, g % 2, t, :]
                    ins = tr(b[:, 128 * t:128 * t + 128], src, ident)
                banks.close(ins, use)

            for k in range(KB):
                banks.wait_read(pe, ("xT", k))
            pe.wait_ge(S["ba_in"], 16)
            for g in range(12):
                channel(("gdn", g), ("gk", "gv", "gq")[g // 4], g % 4, slice(0, 512) if g < 8 else slice(256, 512))
                if g == 3:
                    banks.open(pe, "ba")
                    b = banks["ba"]
                    for t in range(NT):
                        for k in range(KB):
                            ins = mm(b[:, 16 * t:16 * t + 16], xmT[:, k, 128 * t:128 * t + 128], wba[:, k, :],
                                     start=(k == 0), stop=(k == KB - 1))
                    banks.close(ins, "ba")
                if g >= 2:
                    to_tok(g - 2)
                if g >= 4 and g - 4 not in range(4, 8):
                    to_chan(g - 4)
                if g == 5:
                    pe.wait_ge(S["gates_ready"], 1)
                    banks.open(pe, "gcum")
                    b = banks["gcum"]
                    mm(b[:, 0:16], cst["trif"], gcol(GRAW)[:, 0:16])
                    mm(b[:, 16:32], cst["trib"], gcol(GRAW)[:, 16:32])
                    banks.close(mm(b[:, 32:64], cst["blk"], gcol(GRAW)), "gcum")
                if g == 6:
                    banks.wait_read(pe, "gcum")
                    banks.open(pe, "rows")
                    b = banks["rows"]
                    pe.wait_ge(S["gexp"], 1)
                    banks.close(tr(b[0:64, 0:128], GB[:, :], ident), "rows")
                    banks.open(pe, "gend")
                    b = banks["gend"]
                    for c in range(2):
                        ins = mm(b[:, 32 * c:32 * c + 32], ident[:, 64 * c:64 * c + 1].to_broadcast([128, 128]), gcol(EGT))
                    banks.close(ins, "gend")
            to_tok(10)
            to_tok(11)
            for g in (8, 9, 10, 11):
                to_chan(g)

            def spread(out_ap, row, rhs, m):
                return mm(out_ap, ident[0:64, row:row + 1].to_broadcast([64, m]), rhs)

            banks.wait_read(pe, "rows")
            for h in range(H):
                use = ("kk", h)
                banks.open(pe, use)
                banks.wait_read(pe, ("toChan", h))
                banks.wait_read(pe, ("toChan", 8 + h))
                b = banks[use]
                for t in range(NT):
                    for c in range(2):
                        s = slice(128 * t + 64 * c, 128 * t + 64 * c + 64)
                        mm(b[64 * c:64 * c + 64, 64 * t:64 * t + 64], kch[:, h, s], kch[:, h, s])
                for t in range(2):
                    for c in range(2):
                        o = 128 * t + 64 * c
                        ins = mm(b[64 * c:64 * c + 64, 256 + 64 * t:320 + 64 * t], kch[:, h, 256 + o:320 + o], qch[:, h, o:o + 64])
                banks.close(ins, use)
                for d in range(2):
                    use = ("bc", d, h)
                    banks.open(pe, use)
                    b = banks[use]
                    for w in range(2):
                        for t in range(NT):
                            for c in range(2):
                                ins = spread(b[64 * c:64 * c + 64, 256 * w + 64 * t:256 * w + 64 * t + 64],
                                             32 * w + 16 * d + 4 * t + h, rowsT[:, 64 * c:64 * c + 64], 64)
                    banks.close(ins, use)

            def packed(use, lhs, rhs):
                banks.open(pe, use)
                b = banks[use]
                for n in range(8):
                    for c in range(2):
                        p = slice(64 * c, 64 * c + 64)
                        r = cst["i64"][p, :] if rhs is None else rhs[p, n, :]
                        ins = mm(b[p, 64 * n:64 * n + 64], lhs[p, n, :], r)
                banks.close(ins, use)

            for g in range(4):
                pe.wait_ge(S["u1_ready"], g + 1)
                packed(("T1", g), unit(Um, g), None)
            for l in range(1, LEVELS):
                for g in range(4):
                    banks.wait_read(pe, ("T1", g) if l == 1 else ("T", l - 1, g))
                    packed(("X", l, g), unit(LT, g), unit(Tm, g))
                for g in range(4):
                    banks.wait_read(pe, ("X", l, g))
                    if l > 1:
                        banks.wait_read(pe, ("U", l - 1, g))
                    if l < LEVELS - 1:
                        packed(("T", l, g), unit(Um, g), unit(Ym, g))
                    packed(("U", l, g), unit(Ym, g), unit(Um, g))

            for h in range(H):
                use = ("eg", h)
                banks.open(pe, use)
                b = banks[use]
                for d in range(2):
                    for t in range(2):
                        ins = spread(b[:, 256 * d + 128 * t:256 * d + 128 * t + 128], 16 * d + 4 * (2 + t) + h, rowsT, 128)
                banks.close(ins, use)

            def fill(use):
                kind, n = use
                if kind == "rk":
                    channel(use, "rk", n, slice(0, 512))
                elif kind == "rq":
                    channel(use, "rq", n, slice(256, 512))
                elif kind == "rv":
                    tokens(use, "rv", n)
                else:
                    tokens(use, kind, 2 + n)

            for g in range(4):
                banks.wait_read(pe, ("U", LEVELS - 1, g))
            for s in range(8):
                pe.wait_ge(S["step_in"], s + 1)
                at = [where(d, s) for d in range(2)]
                part = [slice(64 * c, 64 * c + 64) for _, c in at]
                if s:
                    for d in range(2):
                        use = ("nw", d, s)
                        banks.open(pe, use)
                        b = banks[use]
                        for h in range(H):
                            ins = mm(b[:, 64 * h:64 * h + 64], kbeta[part[d], s % 2, h, :], Um[part[d], d, h, at[d][0], :])
                        banks.close(ins, use)
                use = ("u", s)
                banks.open(pe, use)
                b = banks[use]
                if s:
                    for d in range(2):
                        banks.wait_read(pe, ("nw", d, s))
                        banks.wait_read(pe, ("S", d, s - 1))
                for h in range(H):
                    for d in range(2):
                        o = b[part[d], 128 * h:128 * h + 128]
                        ins = mm(o, Um[part[d], d, h, at[d][0], :], vbeta[part[d], s % 2, h, :], start=True, stop=(s == 0))
                        if s:
                            ins = mm(o, nwT[:, s % 2, d, h, :], state[:, s % 4, d, h, :], start=False, stop=True)
                banks.close(ins, use)
                for f in filler()[s]:
                    fill(f)
                if s < 7:
                    banks.wait_read(pe, ("u", s))
                    for d in range(2):
                        use = ("S", d, s)
                        banks.open(pe, use)
                        b = banks[use]
                        for h in range(H):
                            ins = mm(b[:, 128 * h:128 * h + 128], kend[part[d], s % 2, h, :], usav[part[d], d, at[d][0] % 2, h, :])
                        banks.close(ins, use)
            banks.wait_read(pe, ("u", 7))
            pe.wait_ge(S["qd_ready"], 8)
            pe.wait_ge(S["at_ready"], 8)
            for t in range(2):
                use = ("o", t)
                banks.open(pe, use)
                b = banks[use]
                for h in range(H):
                    for c in range(2):
                        p = slice(64 * c, 64 * c + 64)
                        o = b[p, 128 * h:128 * h + 128]
                        m = 2 * t + c
                        cols = slice(64 * m, 64 * m + 64)
                        mm(o, qdec[:, 0, h, cols], state[:, m, 0, h, :], start=True, stop=False)
                        mm(o, qdec[:, 1, h, cols], state[:, 3 - m, 1, h, :], start=False, stop=False)
                        mm(o, AT[p, 0, h, t, :], usav[p, 0, t, h, :], start=False, stop=False)
                        ins = mm(o, AT[p, 1, h, t, :], usav[p, 1, t, h, :], start=False, stop=True)
                banks.close(ins, use)

            def ret_out(h):
                for q in range(2):
                    banks.wait_read(pe, ("sc", h, q))
                for t in range(2):
                    b = banks[("ro", t)]
                    for kt in range(NT):
                        ins = mm(b[:, 128 * h:128 * h + 128], decay[:, h % 2, 256 * kt + 128 * t:256 * kt + 128 * t + 128],
                                 rv[:, kt, 128 * h:128 * h + 128], start=(kt == 0), stop=(kt == NT - 1))
                    if h == H - 1:
                        banks.close(ins, ("ro", t))
                if h < H - 1:
                    ins.then_inc(S["ro_done"], 1)

            for t in range(2):
                banks.open(pe, ("ro", t))
            for n in range(NT):
                banks.wait_read(pe, ("rv", n))
            pe.wait_ge(S["rope_done"], 8)
            for h in range(H):
                for q in range(2):
                    use = ("sc", h, q)
                    banks.open(pe, use)
                    b = banks[use]
                    for k in range(2):
                        kt = 2 * q + k
                        ins = mm(b[:, 256 * k:256 * k + 256], rk[:, h, 128 * kt:128 * kt + 128], rq[:, h, :])
                    banks.close(ins, use)
                if h:
                    ret_out(h - 1)
            ret_out(H - 1)

            for k in range(4):
                use = ("mT", k)
                banks.open(pe, use)
                pe.wait_ge(S["mix_ready"], 2 if k < 2 else 4)
                b = banks[use]
                for i in range(2):
                    for t in range(2):
                        ins = tr(b[:, 256 * i + 128 * t:256 * i + 128 * t + 128], mix[:, t, 128 * (2 * k + i):128 * (2 * k + i) + 128], ident)
                banks.close(ins, use)

            def wide(use, brow):
                w = chunk(use)
                banks.open(pe, use)
                b = banks[use]
                for k in range(KB):
                    mm(b[:, :], sil[:, k:k + 1].to_broadcast([128, 128]), w[:, k, :], start=(k == 0), stop=False)
                banks.close(mm(b[:, :], cst["ones"][0:1, :], brow, start=False, stop=True), use)

            pe.wait_ge(S["bmodr_in"], 32)
            for i in range(2):
                wide(("g1", i), bmodr[0:1, 512 * i:512 * i + 512])
            for k in range(4):
                banks.wait_read(pe, ("mT", k))
            for half in range(2):
                w = chunk(("wo", half))
                for t in range(2):
                    use = ("y", half, t)
                    banks.open(pe, use)
                    b = banks[use]
                    for k in range(KB):
                        ins = mm(b[:, :], mixT[:, k, 128 * t:128 * t + 128], w[:, k, :], start=(k == 0), stop=(k == KB - 1))
                    banks.close(ins, use)
            for i in range(4):
                mod_cols(("mod2", i), 1)
            for k in range(4):
                use = ("hT", k)
                banks.open(pe, use)
                b = banks[use]
                for i in range(2):
                    for t in range(2):
                        pe.wait_ge(S["x1n_ready"], t + 1)
                        ins = tr(b[:, 256 * i + 128 * t:256 * i + 128 * t + 128], h_t[:, t, 128 * (2 * k + i):128 * (2 * k + i) + 128], ident)
                banks.close(ins, use)
            banks.open(pe, "lg")
            b = banks["lg"]
            for k in range(4):
                banks.wait_read(pe, ("hT", k))
            pe.wait_ge(S["router_in"], 16)
            for t in range(2):
                for k in range(KB):
                    ins = mm(b[:, 64 * t:64 * t + 64], hT[:, k, 128 * t:128 * t + 128], wr[:, k, :], start=(k == 0), stop=(k == KB - 1))
            banks.close(ins, "lg")
            for n in range(4):
                use = ("hk", n)
                t, half = n // 2, n % 2
                banks.open(pe, use)
                b = banks[use]
                for i in range(4):
                    ins = tr(b[:, 128 * i:128 * i + 128], hT[:, 4 * half + i, 128 * t:128 * t + 128], ident)
                banks.close(ins, use)
            for i in range(2):
                wide(("g2", i), bmodr[0:1, 1024 + 512 * i:1536 + 512 * i])

            pe.wait_ge(S["sel_ready"], 1)
            banks.open(pe, "rank")
            b = banks["rank"]
            sel = rt["sel"]
            mm(b[:, 0:64], cst["strict"], sel[:, 0, :])
            mm(b[:, 64:128], cst["ones"], sel[:, 0, :], start=True, stop=False)
            banks.close(mm(b[:, 64:128], cst["strict"], sel[:, 1, :], start=False, stop=True), "rank")
            banks.open(pe, "cnt")
            b = banks["cnt"]
            mm(b[0:64, 0:1], sel[:, 0, :], cst["ones"][:, 0:1], start=True, stop=False)
            banks.close(mm(b[0:64, 0:1], sel[:, 1, :], cst["ones"][:, 0:1], start=False, stop=True), "cnt")
            w = chunk("shgu")

            def shared_up(t):
                use = ("sh", t)
                banks.open(pe, use)
                b = banks[use]
                for k in range(KB):
                    ins = mm(b[:, :], hT[:, k, 128 * t:128 * t + 128], w[:, k, :], start=(k == 0), stop=(k == KB - 1))
                banks.close(ins, use)

            shared_up(0)
            banks.open(pe, "start")
            b = banks["start"]
            pe.wait_ge(S["counts_ready"], 1)
            banks.close(mm(b[0:64, 0:1], cst["strict"][0:64, 0:64], route[0:64, 8:9]), "start")
            banks.open(pe, "selT")
            b = banks["selT"]
            pe.wait_ge(S["posx_ready"], 1)
            for n, m in enumerate(("posx", "gate")):
                for t in range(2):
                    ins = tr(b[0:64, 256 * n + 128 * t:256 * n + 128 * t + 128], rt[m][:, t, :], ident)
            banks.close(ins, "selT")
            shared_up(1)
            banks.open(pe, "item")
            b = banks["item"]
            pe.wait_ge(S["items_ready"], 1)
            for n in range(4):
                ins = mm(b[:, n * ITEMS:(n + 1) * ITEMS], itemT[:, 128 * n:128 * n + 128], onehot)
            banks.close(ins, "item")
            banks.open(pe, "itrow")
            b = banks["itrow"]
            mm(b[0:1, 0:ITEMS], cst["part"][0:64, :], onehot)
            banks.close(mm(b[0:1, ITEMS:ITEMS + 1], route[0:64, 8:9], cst["ones"][0:64, 0:1]), "itrow")
            for t in range(2):
                use = ("shT", t)
                banks.open(pe, use)
                pe.wait_ge(S["sh_gated"], t + 1)
                b = banks[use]
                for k in range(2):
                    ins = tr(b[:, 128 * k:128 * k + 128], sa[:, t, 128 * k:128 * k + 128], ident)
                banks.close(ins, use)
            chunk("shdn")
            wsd = A(4096 * (CI["shdn"] % RING), 2048).rearrange("p (k n) -> p k n", k=2)
            for k in range(8):
                pe.wait_ge(emptied[k], banks.total[k])

            def acc(t, half):
                return psum[2 * t + half]

            for t in range(2):
                for half in range(2):
                    for k in range(2):
                        mm(acc(t, half)[:, :], shgT[:, k, 128 * t:128 * t + 128], wsd[:, k, 512 * half:512 * half + 512],
                           start=(k == 0), stop=False)

            gA, gB, gU, gF = psum[4], psum[5], psum[6], psum[7]

            def gather(half, buf, free, by):
                b = (gA, gB)[half]
                for k in range(4):
                    for t in range(2):
                        ins = mm(b[:, 128 * k:128 * k + 128], htok[:, t, 128 * (4 * half + k):128 * (4 * half + k) + 128],
                                 pick[:, buf, t, :], start=(t == 0), stop=(t == 1))
                        if free is not None and k == 0 and t == 0:
                            ins.then_inc(free, by)
                ins.then_inc(S[("gatherA", "gatherB")[half]], 1)

            def scatter(buf, last):
                for t in range(2):
                    for half in range(2):
                        ins = mm(acc(t, half)[:, :], flip[:, buf, 256 + 128 * t:256 + 128 * t + 128],
                                 ybuf[:, 512 * half:512 * half + 512], start=False, stop=last)
                        if t == 0 and half == 0 and not last:
                            ins.then_inc(S["gu_free"], 1)
                ins.then_inc(S["scattered"], 1)

            pe.wait_ge(S["table_ready"], 1)
            trips = trips_of(pe)
            pe.wait_ge(S["pick_ready"], 1)
            gather(0, 0, S["gu_free"], 2)
            gather(1, 0, S["dn_free"], 2)
            with pe.Fori(0, trips) as it:
                for u in range(2):
                    pe.wait_ge(S[f"gu_in{u}"], it * 32 + 32)
                    pe.wait_ge(S["hidA"], it * 2 + (u + 1))
                    pe.wait_ge(S["outA"], it * 2 + (u + 1))
                    for k in range(KB):
                        if k == 4:
                            pe.wait_ge(S["hidB"], it * 2 + (u + 1))
                        for j in range(2):
                            ins = mm(gU[64 * j:64 * j + 64, :], hid[:, u, k, 64 * j:64 * j + 64], gu_w[u][:, j, k, :],
                                     start=(k == 0), stop=(k == KB - 1))
                    ins.then_inc(S["gu_done"], 1)
                    pe.wait_ge(S["outB"], it * 2 + (u + 1))
                    scatter(1 - u, False)
                    pe.wait_ge(S["gated"], it * 2 + (u + 2))
                    for n in range(2):
                        tr(gF[:, 128 * n:128 * n + 128], gbuf[:, u, 128 * n:128 * n + 128], ident)
                    for n in range(2):
                        ins = tr(gF[:, 256 + 128 * n:256 + 128 * n + 128], pickg[:, u, n, :], ident)
                    ins.then_inc(S["flip_done"], 1)
                    pe.wait_ge(S["pick_ready"], it * 2 + (u + 2))
                    gather(0, 1 - u, None, 0)
                    pe.wait_ge(S["flipped"], it * 2 + (u + 1))
                    pe.wait_ge(S[f"dn_in{u}"], it * 32 + 32)
                    for half in range(2):
                        b = (gU, gF)[half]
                        for k in range(2):
                            for j in range(2):
                                ins = mm(b[64 * j:64 * j + 64, :], flip[:, u, 128 * k + 64 * j:128 * k + 64 * j + 64],
                                         dn_w[u][:, j, k, 512 * half:512 * half + 512], start=(k == 0), stop=(k == 1))
                        ins.then_inc(S[("yA", "yB")[half]], 1)
                    gather(1, 1 - u, S["dn_free"], 1)
            pe.wait_ge(S["outA"], trips * 2 + 1)
            pe.wait_ge(S["outB"], trips * 2 + 1)
            scatter(1, True)

        @block.scalar
        def _(act):
            n_done = [0]

            def act_fn(out_ap, in_ap, f, **kw):
                return nc.scalar.activation(out_ap, in_ap, f, **kw)

            def step(ins):
                n_done[0] += 1
                ins.then_inc(S["astep"], 1)
                act.wait_ge(S["astep"], n_done[0])

            def sqrt(dst, src, scale=1.0, add=EPS):
                act_fn(dst, src, ACT.Sqrt, scale=scale, bias=add).then_inc(S["root_out"], 1)

            roots_in = [0]

            def sqrt_var(ap):
                roots_in[0] += 1
                act.wait_ge(S["root_in"], roots_in[0])
                sqrt(ap, ap)

            banks.wait_read(act, "small")
            act_fn(sil[:, :], colsT[:, 0:16], ACT.Silu).then_inc(S["sil"], 1)
            for t in range(NT):
                sqrt_var(mv[:, 2:3])
            act.wait_ge(S["modcols"], 1)
            for k in range(1, KB, 2):
                use = ("xT", k)
                banks.wait_filled(act, use)
                b = banks[use]
                for v, cols in ((1, slice(0, 256)), (0, slice(256, 512))):
                    ins = act_fn(xmT[:, k, cols], b[:, cols], ACT.Identity, bias=modc[:, 2 * k + v:2 * k + v + 1],
                                 scale=modc[:, 16 + 2 * k + v:16 + 2 * k + v + 1])
                banks.read(ins, use)

            def square(g):
                use = ("toTok", g)
                banks.wait_filled(act, use)
                b = banks[use]
                for t in range(4 if g < 8 else 2):
                    ins = act_fn(junk[:, 128 * t:128 * t + 128], b[:, 128 * t:128 * t + 128], ACT.Square, accum_out=ssq[:, 4 * g + t:4 * g + t + 1])
                step(ins)
                r = ssq[:, 4 * g:4 * g + (4 if g < 8 else 2)]
                sqrt(r, r, *((1.0, EPS) if g < 8 else (float(DK), DK * EPS)))

            def copy_out(use, dst, src):
                banks.wait_filled(act, use)
                banks.read(act_fn(dst, src, ACT.Copy), use)

            def tok_part(g):
                if 4 <= g < 8:
                    copy_out(("toTok", g), vtok[:, :, g - 4, :], banks[("toTok", g)][:, :].rearrange("p (t d) -> p t d", t=4))
                else:
                    square(g)

            def chan_part(g):
                if g < 4:
                    copy_out(("toChan", g), kch[:, g, :], banks[("toChan", g)][:, :])
                else:
                    copy_out(("toChan", g), qch[:, g - 8, :], banks[("toChan", g)][:, 0:256])

            act.wait_ge(S["vstep"], 1)
            for g in range(12):
                use = ("gdn", g)
                banks.wait_filled(act, use)
                b = banks[use]
                if g >= 2:
                    act.wait_ge(S["conv_acc"], g - 1)
                if g < 8:
                    ins = act_fn(convbuf[:, g % 2, :, 2:258], b[:, :].rearrange("p (s n) -> p s n", s=2), ACT.Copy)
                else:
                    ins = act_fn(convbuf[:, g % 2, 1, 2:258], b[:, 0:256], ACT.Copy)
                banks.read(ins, use)
                act.wait_ge(S["conv_acc"], g + 1)
                n = 512 if g < 8 else 256
                act_fn(convout[:, g % 2, 0:n], convout[:, g % 2, 0:n], ACT.Silu).then_inc(S["conv_silu"], 1)
                if g >= 2:
                    tok_part(g - 2)
                if g >= 4 and g - 4 not in range(4, 8):
                    chan_part(g - 4)
                if g == 3:
                    act.wait_ge(S["gate_raw"], 1)
                    act_fn(gcol(BETA), gcol(BETA), ACT.Exp, scale=-1.0)
                    act_fn(small_consts[:, 24:32], small_consts[:, 0:8], ACT.Exp)
                    step(act_fn(gcol(SCR), gcol(SCR), ACT.Exp, scale=-1.0))
                    act_fn(gcol(SCR), gcol(SCR), ACT.Ln, bias=1.0).then_inc(S["gate_exp"], 1)
                if g == 5:
                    act.wait_ge(S["decay_arg"], 1)
                    act_fn(gcol(EG), GB[:, 0:32], ACT.Exp)
                    act_fn(gcol(KEND), gcol(SCR), ACT.Exp)
                    act_fn(gcol(EGT), gcol(GT), ACT.Exp).then_inc(S["gexp"], 1)
            tok_part(10)
            tok_part(11)
            for g in (8, 9, 10, 11):
                chan_part(g)
            for n in range(8):
                act.wait_ge(S["dt_arg"], n + 1)
                act_fn(dtmp[:, n % 2], dtmp[:, n % 2], ACT.Exp).then_inc(S["dt_exp"], 1)
            for l in range(LEVELS - 1):
                for g in range(4):
                    use = ("T1", g) if l == 0 else ("T", l, g)
                    copy_out(use, unit(Tm, g), banks[use][:, :].rearrange("p (n i) -> p n i", n=8))
            for h in range(H):
                use = ("eg", h)
                if h >= 2:
                    act.wait_ge(S["qd_ready"], 2 * (h - 1))
                else:
                    act.wait_ge(S["at_ready"], 8)
                banks.wait_filled(act, use)
                banks.read(act_fn(egb[:, h % 2], banks[use][:, :].rearrange("p (d n) -> p d n", d=2), ACT.Exp), use)
            n_raw = 0

            def decays(h):
                if h == 0:
                    act.wait_ge(S["dist_in"], 16)
                if h >= 2:
                    act.wait_ge(S["ro_done"], h - 1)
                if h:
                    act.wait_ge(S["decay_ready"], h)
                act_fn(decay[:, h % 2, :], dist[:, 0:1024], ACT.Exp, scale=small_consts[:, 16 + h:17 + h])
                act_fn(decayB, dist[:, 1024:2048], ACT.Exp, scale=small_consts[:, 20 + h:21 + h]).then_inc(S["decay_exp"], 1)

            for s in range(8):
                if s:
                    for d in range(2):
                        use = ("nw", d, s)
                        copy_out(use, nwT[:, s % 2, d], banks[use][:, 0:256].rearrange("p (h i) -> p h i", h=H))
                for use in filler()[s]:
                    kind, n = use
                    banks.wait_filled(act, use)
                    b = banks[use]
                    if kind in ("rk", "rq"):
                        if n_raw == 0:
                            act.wait_ge(S["qd_ready"], 8)
                        if n_raw >= 2:
                            act.wait_ge(S["rope_done"], n_raw - 1)
                        if kind == "rk":
                            act_fn(rk[:, n, 0:256], b[:, 0:256], ACT.Copy)
                            ins = act_fn(raw[:, n_raw % 2, 0:256], b[:, 256:512], ACT.Copy)
                        else:
                            ins = act_fn(raw[:, n_raw % 2, 0:256], b[:, 0:256], ACT.Copy)
                        banks.read(ins, use)
                        n_raw += 1
                    elif kind == "rv":
                        banks.read(act_fn(rv[:, n, :], b[:, :], ACT.Copy), use)
                    elif kind == "z":
                        banks.read(act_fn(zs[:, n, :], b[:, :], ACT.Silu), use)
                    else:
                        act.wait_ge(S["rope_done"], 8)
                        banks.read(act_fn(gs[:, n, :], b[:, :], ACT.Silu), use)
                if s == 4:
                    decays(0)
                if s == 5:
                    decays(1)
            for t in range(2):
                use = ("o", t)
                banks.wait_filled(act, use)
                b = banks[use]
                for h in range(H):
                    ins = act_fn(junk2[:, 128 * h:128 * h + 128], b[:, 128 * h:128 * h + 128], ACT.Square, accum_out=ssq[:, 4 * t + h:4 * t + h + 1])
                step(ins)
                sqrt(ssq[:, 4 * t:4 * t + 4], ssq[:, 4 * t:4 * t + 4], 1.0 / DK, EPS)
            decays(2)
            decays(3)
            for t in range(2):
                sqrt_var(mv[:, 8:12])
            for k in range(4):
                if k % 2:
                    copy_out(("mT", k), mixT[:, 2 * k:2 * k + 2, :], banks[("mT", k)][:, :].rearrange("p (k t) -> p k t", k=2))
            for i in range(2):
                copy_out(("g1", i), g1b[:, 512 * i:512 * i + 512], banks[("g1", i)][:, :])
            for t in range(4):
                sqrt_var(mv[:, 2:3])
            for k in range(4):
                if k % 2:
                    hT_out(act, k, lambda o, i, sc, bi: act_fn(o, i, ACT.Identity, scale=sc, bias=bi))
            banks.wait_filled(act, "lg")
            act_fn(rt["s"], banks["lg"][:, 0:128].rearrange("p (t e) -> p t e", t=2), ACT.Exp, scale=-1.0).then_inc(emptied[banks.at["lg"][0]], 1)
            for n in range(4):
                t, half = n // 2, n % 2
                copy_out(("hk", n), htok[:, t, 512 * half:512 * half + 512], banks[("hk", n)][:, :])
            for i in range(2):
                copy_out(("g2", i), g2b[:, 512 * i:512 * i + 512], banks[("g2", i)][:, :])
            for t in range(2):
                banks.wait_filled(act, ("sh", t))
                act_fn(sa[:, t, :], banks[("sh", t)][:, 0:256], ACT.Silu).then_inc(S["sh_silu"], 1)
            for t in range(2):
                use = ("shT", t)
                copy_out(use, shgT[:, :, 128 * t:128 * t + 128], banks[use][:, 0:256].rearrange("p (k t) -> p k t", k=2))

            act.wait_ge(S["table_ready"], 1)
            trips = trips_of(act)
            act.wait_ge(S["gatherA"], 1)
            act_fn(hid[:, 0, 0:4, :], psum[4][:, :].rearrange("p (k s) -> p k s", k=4), ACT.Copy).then_inc(S["hidA"], 1)
            with act.Fori(0, trips) as it:
                for u in range(2):
                    act.wait_ge(S["gu_done"], it * 2 + (u + 1))
                    act.wait_ge(S["gated"], it * 2 + (u + 1))
                    act_fn(sa[:, 0, :], psum[6][:, 0:256], ACT.Silu).then_inc(S["silu_done"], 1)
                    act.wait_ge(S["gatherA"], it * 2 + (u + 2))
                    act_fn(hid[:, 1 - u, 0:4, :], psum[4][:, :].rearrange("p (k s) -> p k s", k=4), ACT.Copy).then_inc(S["hidA"], 1)
                    act.wait_ge(S["yA"], it * 2 + (u + 1))
                    act.wait_ge(S["scattered"], it * 2 + (u + 1))
                    act_fn(ybuf[:, 0:512], psum[6][:, :], ACT.Copy).then_inc(S["outA"], 1)
            for t in range(2):
                sqrt_var(mv[:, 2:3])

        @block.vector
        def _(dve):
            V = nc.vector
            n_done = [0]

            def step(ins):
                n_done[0] += 1
                ins.then_inc(S["vstep"], 1)
                dve.wait_ge(S["vstep"], n_done[0])

            n_roots = [0]

            def rooted(ap):
                n_roots[0] += 1
                dve.wait_ge(S["root_out"], n_roots[0])
                step(V.reciprocal(ap, ap))

            def layernorm(dst, src, col):
                s0 = st[:, 0:12].rearrange("p (a n) -> p a n", a=2)
                for i in range(2):
                    ins = V.bn_stats(s0[:, i, :], src[:, 512 * i:512 * i + 512])
                step(ins)
                step(V.bn_aggr(mv[:, 0:2], s0))
                V.tensor_copy(mv[:, 2:3], mv[:, 1:2]).then_inc(S["root_in"], 1)
                rooted(mv[:, 2:3])
                return V.tensor_scalar(dst, src, mv[:, 0:1], mv[:, 2:3], ALU.subtract, ALU.mult)

            def bct(ap, n, m):
                return ap.unsqueeze(2).to_broadcast([ap.shape[0], n, m])

            step(V.memset(A(41984, 1040), 0.0))
            banks.wait_filled(dve, "small")
            banks.read(V.tensor_copy(colsT[:, :], banks["small"][:, 0:64]), "small")
            for t in range(NT):
                dve.wait_ge(S["x_in"], 64)
                layernorm(xall[:, t, :], xall[:, t, :], t).then_inc(S["xn"], 1)
            banks.wait_filled(dve, "convw")
            banks.read(V.tensor_copy(convw[:, :], banks["convw"][:, 0:60]), "convw")
            banks.wait_read(dve, "small")
            for i in range(4):
                use = ("mod1", i)
                banks.wait_filled(dve, use)
                banks.read(V.scalar_tensor_tensor(
                    out=modc[:, 8 * i:8 * i + 8].rearrange("p (m v) -> p m v", v=2),
                    in0=banks[use][:, 0:8].rearrange("p (m v) -> p m v", v=2), scalar=1.0 if i >= 2 else 0.0,
                    in1=bct(colsT[:, 16 + 4 * i:20 + 4 * i], 4, 2), op0=ALU.add, op1=ALU.add), use)
            banks.wait_read(dve, ("mod1", 3))
            V.memset(st[:, 60:61], 0.0).then_inc(S["modcols"], 1)
            for k in range(0, KB, 2):
                use = ("xT", k)
                banks.wait_filled(dve, use)
                b = banks[use]
                for v, cols in ((1, slice(0, 256)), (0, slice(256, 512))):
                    ins = V.tensor_scalar(xmT[:, k, cols], b[:, cols], modc[:, 16 + 2 * k + v:17 + 2 * k + v],
                                          modc[:, 2 * k + v:2 * k + v + 1], ALU.mult, ALU.add)
                banks.read(ins, use)

            def conv(g):
                dve_in = convbuf[:, g % 2, :, :] if g < 8 else convbuf[:, g % 2, 1:2, :]
                banks.wait_read(dve, ("gdn", g))
                if g >= 2:
                    banks.wait_filled(dve, ("toTok", g - 2))
                n = 2 if g < 8 else 1
                o = convout[:, g % 2, 0:256 * n].rearrange("p (s n) -> p s n", s=n)
                tile = {0: 4, 1: 8, 2: 0}[g // 4] + g % 4
                for j in range(5):
                    src, w = dve_in[:, :, j:j + 256], convw[:, 5 * tile + j:5 * tile + j + 1]
                    if j == 0:
                        ins = V.tensor_scalar(o, src, w, None, ALU.mult)
                    else:
                        ins = V.scalar_tensor_tensor(out=o, in0=src, scalar=w, in1=o, op0=ALU.mult, op1=ALU.add)
                    if j < 4:
                        step(ins)
                ins.then_inc(S["conv_acc"], 1)

            def tok_part(g):
                if 4 <= g < 8:
                    return
                use = ("toTok", g)
                n = 4 if g < 8 else 2
                r = ssq[:, 4 * g:4 * g + n]
                rooted(r)
                if g < 8:
                    dst = ktok[:, :, g, :]
                else:
                    if g >= 10:
                        banks.wait_filled(dve, ("toChan", g - 2))
                    dst = qtok[:, g % 2, :, :]
                banks.read(V.tensor_tensor(dst, banks[use][:, 0:128 * n].rearrange("p (t d) -> p t d", t=n), bct(r, n, 128), ALU.mult), use)

            for g in range(12):
                conv(g)
                if g >= 2:
                    tok_part(g - 2)
                if g == 3:
                    banks.wait_filled(dve, "ba")
                    b = banks["ba"][:, 0:64].rearrange("p (t w d h) -> p w t d h", t=4, w=2, d=2)

                    def dth(m, d):
                        return m.rearrange("p (d t h) -> p d t h", d=2, t=4)[:, d]
                    for d in range(2):
                        V.tensor_copy(dth(gcol(BETA), d), b[:, 0, :, d, :])
                        ins = V.tensor_tensor(dth(gcol(GRAW), d), b[:, 1, :, d, :],
                                              small_consts[:, 8 + 4 * d:12 + 4 * d].unsqueeze(1).to_broadcast([128, 4, 4]), ALU.add)
                    banks.read(ins, "ba")
                    banks.wait_read(dve, "ba")
                    V.scalar_tensor_tensor(out=gcol(SCR), in0=gcol(GRAW), scalar=-1.0, in1=gcol(GRAW), op0=ALU.mult, op1=ALU.max).then_inc(S["gate_raw"], 1)
                if g == 4:
                    dve.wait_ge(S["gate_exp"], 1)
                    V.tensor_scalar(gcol(BETA), gcol(BETA), 1.0, None, ALU.add)
                    step(V.scalar_tensor_tensor(out=gcol(GRAW), in0=gcol(GRAW), scalar=0.0, in1=gcol(SCR), op0=ALU.max, op1=ALU.add))
                    step(V.reciprocal(GB[:, 32:64], gcol(BETA)))
                    V.tensor_copy(gcol(BETA), GB[:, 32:64])
                    for d in range(2):
                        m = gcol(GRAW).rearrange("p (d t h) -> p d t h", d=2, t=4)[:, d]
                        ins = V.scalar_tensor_tensor(out=m, in0=m, scalar=-1.0,
                                                     in1=small_consts[:, 24 + 4 * d:28 + 4 * d].unsqueeze(1).to_broadcast([128, 4, 4]),
                                                     op0=ALU.mult, op1=ALU.mult)
                    ins.then_inc(S["gates_ready"], 1)
                if g == 5:
                    banks.wait_filled(dve, "gcum")
                    V.tensor_copy(GB[:, 0:32], banks["gcum"][:, 0:32])
                    banks.read(V.tensor_copy(gcol(GT), banks["gcum"][:, 32:64]), "gcum")
                    banks.wait_read(dve, "gcum")
                    V.tensor_tensor(gcol(SCR), gcol(GT), GB[:, 0:32], ALU.subtract).then_inc(S["decay_arg"], 1)
                if g == 6:
                    dve.wait_ge(S["gexp"], 1)
                    V.scalar_tensor_tensor(out=gcol(NBEG), in0=gcol(BETA), scalar=-1.0, in1=gcol(EG), op0=ALU.mult, op1=ALU.mult)
                    banks.wait_filled(dve, "rows")
                    banks.read(V.tensor_copy(rowsT, banks["rows"][0:64, 0:128]), "rows")
                    banks.wait_filled(dve, "gend")
                    banks.read(V.tensor_copy(ge[:, :], banks["gend"][:, 0:64]), "gend")
            tok_part(10)
            tok_part(11)

            banks.wait_filled(dve, ("toChan", 11))

            def dt_argument(n):
                h, d = n // 2, n % 2
                use = ("bc", d, h)
                banks.wait_filled(dve, use)
                m = dtmp[:, n % 2]
                step(V.tensor_tensor(m, banks[use][:, 0:256].rearrange("p (t i) -> p t i", t=4), bct(rowcol(GB, d, h), 4, 64), ALU.subtract))
                V.tensor_tensor(m, m, cst["neg"][:, 64 * d:64 * d + 64].unsqueeze(1).to_broadcast([128, 4, 64]), ALU.add).then_inc(S["dt_arg"], 1)

            def i64(n):
                return cst["i64"].unsqueeze(1).to_broadcast([128, n, 64])

            def dt_finish(n):
                h, d = n // 2, n % 2
                use = ("bc", d, h)
                dve.wait_ge(S["dt_exp"], n + 1)
                m = dtmp[:, n % 2]
                L, At = LT[:, d, h], AT[:, d, h]
                kk = banks[("kk", h)]
                step(V.tensor_tensor(At, m[:, 2:4, :], i64(2), ALU.add))
                ins = V.tensor_tensor(L, m, banks[use][:, 256:512].rearrange("p (t i) -> p t i", t=4), ALU.mult)
                banks.read(ins, use)
                ins = V.tensor_tensor(At, At, kk[:, 256:384].rearrange("p (t i) -> p t i", t=2), ALU.mult)
                ins.then_inc(S["at_ready"], 1)
                banks.wait_read(dve, use)
                ins = V.tensor_tensor(L, L, kk[:, 0:256].rearrange("p (t i) -> p t i", t=4), ALU.mult)
                if d:
                    banks.read(ins, ("kk", h))
                    banks.wait_read(dve, ("kk", h))
                else:
                    step(ins)
                step(V.tensor_tensor(L, L, i64(4), ALU.add))

            for n in range(9):
                if n < 8:
                    if n % 2 == 0:
                        banks.wait_filled(dve, ("kk", n // 2))
                    dt_argument(n)
                if n:
                    dt_finish(n - 1)
            for g in range(4):
                d = g // 2
                V.tensor_tensor(unit(Um, g), unit(LT, g), cst["u1mask"][:, 64 * d:64 * d + 64].unsqueeze(1).to_broadcast([128, 8, 64]),
                                ALU.mult).then_inc(S["u1_ready"], 1)
            for l in range(1, LEVELS):
                for g in range(4):
                    use = ("X", l, g)
                    o = 64 * (2 * l + g // 2)
                    banks.wait_filled(dve, use)
                    banks.read(V.tensor_tensor(unit(Ym, g), banks[use][:, :].rearrange("p (n i) -> p n i", n=8),
                                               cst["ymask"][:, o:o + 64].unsqueeze(1).to_broadcast([128, 8, 64]), ALU.mult), use)
                for g in range(4):
                    use = ("U", l, g)
                    banks.wait_filled(dve, use)
                    banks.read(V.tensor_copy(unit(Um, g), banks[use][:, :].rearrange("p (n i) -> p n i", n=8)), use)
            for h in range(H):
                banks.wait_read(dve, ("eg", h))
                for d in range(2):
                    V.tensor_tensor(qdec[:, d, h, :], egb[:, h % 2, d, :], qch[:, h, :], ALU.mult).then_inc(S["qd_ready"], 1)

            n_rope = 0
            for s in range(8):
                use = ("u", s)
                banks.wait_filled(dve, use)
                for d in range(2):
                    t, c = where(d, s)
                    p = slice(64 * c, 64 * c + 64)
                    ins = V.tensor_copy(usav[p, d, t % 2], banks[use][p, :].rearrange("p (h e) -> p h e", h=H))
                banks.read(ins, use)
                for f in filler()[s]:
                    if f[0] in ("rk", "rq"):
                        banks.wait_read(dve, f)
                        r, dst = raw[:, n_rope % 2, :], (rk[:, f[1], 256:512] if f[0] == "rk" else rq[:, f[1], :])
                        V.tensor_tensor(r[0:64, 256:512], r[64:128, 0:256], cst["sin"][64:128, :], ALU.mult)
                        V.tensor_tensor(r[64:128, 256:512], r[0:64, 0:256], cst["sin"][0:64, :], ALU.mult)
                        step(V.tensor_tensor(dst, r[:, 0:256], cst["cos"], ALU.mult))
                        V.tensor_tensor(dst, dst, r[:, 256:512], ALU.add).then_inc(S["rope_done"], 1)
                        n_rope += 1
                if s < 7:
                    for d in range(2):
                        use = ("S", d, s)
                        banks.wait_filled(dve, use)
                        b = banks[use][:, :].rearrange("p (h e) -> p h e", h=H)
                        nxt = state[:, (s + 1) % 4, d]
                        if s == 0:
                            banks.read(V.tensor_copy(nxt, b), use)
                        else:
                            dve.wait_ge(S["s_scaled"], 2 * (s - 1) + d + 1)
                            banks.read(V.tensor_tensor(nxt, nxt, b, ALU.add), use)
            dve.wait_ge(S["norms_in"], 32)
            for n in range(2):
                banks.wait_read(dve, ("z", n))
                banks.wait_read(dve, ("gt", n))
            for t in range(2):
                use = ("o", t)
                r = ssq[:, 4 * t:4 * t + 4]
                rooted(r)
                m = mix[:, t, 0:512]
                m4 = m.rearrange("p (h e) -> p h e", h=H)
                banks.read(V.tensor_tensor(m4, banks[use][:, :].rearrange("p (h e) -> p h e", h=H), bct(r, 4, 128), ALU.mult), use)
                banks.wait_read(dve, use)
                step(V.tensor_tensor(m, m, zs[:, t, :], ALU.mult))
                V.tensor_tensor(m4, m4, norms[:, 0:128].unsqueeze(1).to_broadcast([128, 4, 128]), ALU.mult).then_inc(S["mix_ready"], 1)
            for h in range(H):
                dve.wait_ge(S["decay_ready"], h + 1)
                for q in range(2):
                    use = ("sc", h, q)
                    banks.wait_filled(dve, use)
                    m = decay[:, h % 2, 512 * q:512 * q + 512]
                    banks.read(V.scalar_tensor_tensor(out=m, in0=banks[use][:, :], scalar=DK ** -0.5, in1=m, op0=ALU.mult, op1=ALU.mult), use)
            for t in range(2):
                use = ("ro", t)
                banks.wait_filled(dve, use)
                b = banks[use]
                for h in range(H):
                    ins = V.bn_stats(st[:, 6 * h:6 * h + 6], b[:, 128 * h:128 * h + 128])
                step(ins)
                for h in range(H):
                    ins = V.bn_aggr(mv[:, 2 * h:2 * h + 2], st[:, 6 * h:6 * h + 6])
                step(ins)
                V.tensor_copy(mv[:, 8:12], mv[:, 1:8:2]).then_inc(S["root_in"], 1)
                rooted(mv[:, 8:12])
                for h in range(H):
                    ins = V.tensor_scalar(mix[:, t, 512 + 128 * h:640 + 128 * h], b[:, 128 * h:128 * h + 128],
                                          mv[:, 2 * h:2 * h + 1], mv[:, 8 + h:9 + h], ALU.subtract, ALU.mult)
                banks.read(ins, use)
                banks.wait_read(dve, use)
                m = mix[:, t, 512:1024]
                step(V.tensor_tensor(m, m, norms[:, 128:640], ALU.mult))
                V.tensor_tensor(m, m, gs[:, t, :], ALU.mult).then_inc(S["mix_ready"], 1)
            for k in (0, 2):
                use = ("mT", k)
                banks.wait_filled(dve, use)
                banks.read(V.tensor_copy(mixT[:, 2 * k:2 * k + 2, :], banks[use][:, :].rearrange("p (k t) -> p k t", k=2)), use)
            for i in range(2):
                banks.wait_read(dve, ("g1", i))
            for half in range(2):
                for t in range(2):
                    use = ("y", half, t)
                    banks.wait_filled(dve, use)
                    cols = slice(512 * half, 512 * half + 512)
                    banks.read(V.tensor_tensor(h_t[:, t, cols], banks[use][:, :], g1b[:, cols], ALU.mult), use)
            banks.wait_read(dve, ("y", 1, 1))
            dve.wait_ge(S["xres_in"], 32)
            dve.wait_ge(S["lnrows_in"], 32)

            def residual_norm(t, res):
                m = h_t[:, t, :]
                step(V.scalar_tensor_tensor(out=m, in0=res, scalar=ALPHA, in1=m, op0=ALU.mult, op1=ALU.add))
                step(layernorm(m, m, t))
                step(V.tensor_tensor(m, m, lnr[:, 0:1024], ALU.mult))
                return m, lnr[:, 1024:2048]

            for t in range(2):
                m, bias = residual_norm(t, xres[:, t, :])
                step(V.tensor_tensor(x1[:, t, :], m, bias, ALU.add))
                layernorm(h_t[:, t, :], x1[:, t, :], t).then_inc(S["x1n_ready"], 1)
            for i in range(4):
                use = ("mod2", i)
                banks.wait_filled(dve, use)
                banks.read(V.scalar_tensor_tensor(out=mod2[:, 4 * i:4 * i + 4], in0=banks[use][:, 0:4], scalar=1.0 if i >= 2 else 0.0,
                                                  in1=colsT[:, 16 + 24 + 4 * i:16 + 28 + 4 * i], op0=ALU.add, op1=ALU.add), use)
            banks.wait_read(dve, ("mod2", 3))
            for k in (0, 2):
                hT_out(dve, k, lambda o, i, sc, bi: V.tensor_scalar(o, i, sc, bi, ALU.mult, ALU.add))

            s_, sb, masked, work, sel, gate, posx, max8 = (rt[n] for n in ("s", "sb", "masked", "work", "sel", "gate", "posx", "max8"))
            banks.wait_read(dve, "lg")
            dve.wait_ge(S["rbias_in"], 16)
            step(V.tensor_scalar(s_, s_, 1.0, None, ALU.add))
            step(V.reciprocal(s_, s_))
            step(V.tensor_tensor(sb, s_, rbias.unsqueeze(1).to_broadcast([128, 2, 64]), ALU.add))
            for t in range(2):
                for g in range(GROUPS):
                    ins = V.max(max8[:, t, 8 * g:8 * g + 8], sb[:, t, 8 * g:8 * g + 8])
            step(ins)
            gsc, gm8, gwork, gpen = (g8[:, 16 * i:16 * i + 16].rearrange("p (t g) -> p t g", t=2) for i in range(4))
            step(V.tensor_tensor(gsc, max8[:, :, 0:64:8], max8[:, :, 1:64:8], ALU.add))
            for t in range(2):
                ins = V.max(gm8[:, t, :], gsc[:, t, :])
            step(ins)
            step(V.memset(gm8[:, :, TOPG:8], 1e30))
            for t in range(2):
                ins = V.match_replace(gwork[:, t, :], gm8[:, t, :], gsc[:, t, :], -1e30)
            step(ins)
            step(V.tensor_scalar(gwork, gwork, -1e29, None, ALU.is_lt))
            step(V.tensor_scalar(gpen, gwork, -1.0, 1e30, ALU.add, ALU.mult))

            def by_expert(m, t):
                return m[:, t, :].rearrange("p (g e) -> p g e", g=GROUPS)

            for t in range(2):
                ins = V.tensor_tensor(by_expert(masked, t), by_expert(sb, t), gwork[:, t, :].unsqueeze(2).to_broadcast([128, 8, 8]), ALU.mult)
            step(ins)
            for t in range(2):
                ins = V.tensor_tensor(by_expert(masked, t), by_expert(masked, t), gpen[:, t, :].unsqueeze(2).to_broadcast([128, 8, 8]), ALU.add)
            step(ins)
            for t in range(2):
                ins = V.max(gm8[:, t, :], masked[:, t, :])
            step(ins)
            for t in range(2):
                ins = V.match_replace(work[:, t, :], gm8[:, t, :], masked[:, t, :], -3e38)
            step(ins)
            step(V.tensor_scalar(sel, work, -2e38, None, ALU.is_lt))
            V.memset(st[:, 60:61], 0.0).then_inc(S["sel_ready"], 1)
            step(V.tensor_tensor(gate, s_, sel, ALU.mult))
            step(V.tensor_reduce(st[:, 40:42], gate, mybir.AxisListType.X, ALU.add))
            step(V.reciprocal(st[:, 42:44], st[:, 40:42]))
            V.scalar_tensor_tensor(out=gate, in0=gate, scalar=2.5, in1=bct(st[:, 42:44], 2, 64), op0=ALU.mult, op1=ALU.mult)
            banks.wait_filled(dve, "cnt")
            banks.read(V.tensor_copy(route[0:64, 0:1], banks["cnt"][0:64, 0:1]), "cnt")
            banks.wait_read(dve, "cnt")
            for r in range(T // CAP):
                ins = V.tensor_scalar(route[0:64, 1 + r:2 + r], route[0:64, 0:1], float(CAP * r), None, ALU.is_gt)
            step(ins)
            V.tensor_reduce(route[0:64, 8:9], route[0:64, 1:5], mybir.AxisListType.X, ALU.add).then_inc(S["counts_ready"], 1)
            dve.wait_ge(S["counts_ready"], 1)
            banks.wait_filled(dve, "rank")
            banks.read(V.scalar_tensor_tensor(out=posx, in0=banks["rank"][:, 0:128].rearrange("p (t e) -> p t e", t=2), scalar=BIG,
                                              in1=sel, op0=ALU.add, op1=ALU.mult), "rank")
            banks.wait_read(dve, "rank")
            V.tensor_scalar(posx, posx, -BIG, None, ALU.add).then_inc(S["posx_ready"], 1)
            banks.wait_filled(dve, "start")
            banks.read(V.tensor_copy(route[0:64, 9:10], banks["start"][0:64, 0:1]), "start")
            banks.wait_read(dve, "start")
            V.tensor_tensor(route[0:64, 10:11], route[0:64, 9:10], route[0:64, 8:9], ALU.add)
            V.tensor_scalar(route[0:64, 11:12], route[0:64, 9:10], float(CAP), None, ALU.mult)
            step(V.tensor_scalar(route[0:64, 12:12 + 0 + 1], route[0:64, 9:10], 0.0, None, ALU.add))
            step(V.tensor_scalar(onehot, cst["item"][0:64, :], route[0:64, 9:10], None, ALU.is_ge))
            step(V.scalar_tensor_tensor(out=onehot, in0=cst["item"][0:64, :], scalar=route[0:64, 10:11], in1=onehot, op0=ALU.is_lt, op1=ALU.mult))
            banks.wait_filled(dve, "selT")
            b = banks["selT"]
            V.tensor_scalar(itemT[:, 0:256], b[0:64, 0:256], route[0:64, 11:12], None, ALU.add)
            banks.read(V.tensor_copy(itemT[:, 256:512], b[0:64, 256:512]), "selT")
            banks.wait_read(dve, "selT")
            V.memset(st[:, 61:62], 0.0).then_inc(S["items_ready"], 1)
            banks.wait_filled(dve, "item")
            b = banks["item"][:, 0:4 * ITEMS].rearrange("p (w t i) -> p w t i", w=2, t=2)
            V.tensor_tensor(tabv[:, 0], b[:, 0], cst["item64"].unsqueeze(1).to_broadcast([128, 2, ITEMS]), ALU.subtract)
            banks.read(V.tensor_copy(tabv[:, 1], b[:, 1]), "item")
            banks.wait_filled(dve, "itrow")
            banks.read(V.tensor_copy(eidx[0:1, 0:ITEMS + 1], banks["itrow"][0:1, 0:ITEMS + 1]), "itrow")
            banks.wait_read(dve, "item")
            banks.wait_read(dve, "itrow")
            V.memset(st[:, 62:63], 0.0).then_inc(S["table_ready"], 1)
            for t in range(2):
                use = ("sh", t)
                dve.wait_ge(S["sh_silu"], t + 1)
                V.tensor_tensor(sa[:, t, :], sa[:, t, :], banks[use][:, 256:512], ALU.mult).then_inc(emptied[banks.at[use][0]], 1)
                banks.wait_read(dve, use)
                V.memset(st[:, 60 + t:61 + t], 0.0).then_inc(S["sh_gated"], 1)

            def choose(buf, col):
                rank = tabv[:, 0, :, col].unsqueeze(3).to_broadcast([128, 2, 2, 64])
                wgt = tabv[:, 1, :, col].unsqueeze(3).to_broadcast([128, 2, 2, 64])
                io = cst["iota64"].unsqueeze(1).unsqueeze(1).to_broadcast([128, 2, 2, 64])
                o = pick[:, buf].rearrange("p t (j s) -> p t j s", j=2)
                og = pickg[:, buf].rearrange("p t (j s) -> p t j s", j=2)
                ins = V.tensor_tensor(o, io, rank, ALU.is_equal)
                return ins, lambda: V.tensor_tensor(og, o, wgt, ALU.mult)

            V.memset(flip[:, 1, :], 0.0).then_inc(S["gated"], 1)
            V.memset(ybuf[:, 0:512], 0.0).then_inc(S["outA"], 1)
            V.memset(ybuf[:, 512:1024], 0.0).then_inc(S["outB"], 1)
            ins, weigh = choose(0, slice(0, 2))
            step(ins)
            weigh().then_inc(S["pick_ready"], 1)
            trips = trips_of(dve)
            dve.wait_ge(S["gatherB"], 1)
            V.tensor_copy(hid[:, 0, 4:8, :], psum[5][:, :].rearrange("p (k s) -> p k s", k=4)).then_inc(S["hidB"], 1)
            chosen = n_done[0]
            with dve.Fori(0, trips) as it:
                for u in range(2):
                    ins, weigh = choose(1 - u, bass.ds(it * 4 + (2 * u + 2), 2))
                    ins.then_inc(S["vstep"], 1)
                    dve.wait_ge(S["vstep"], it * 2 + (u + 1 + chosen))
                    weigh().then_inc(S["pick_ready"], 1)
                    dve.wait_ge(S["silu_done"], it * 2 + (u + 1))
                    V.tensor_tensor(gbuf[:, u, :], sa[:, 0, :], psum[6][:, 256:512], ALU.mult).then_inc(S["gated"], 1)
                    dve.wait_ge(S["flip_done"], it * 2 + (u + 1))
                    V.tensor_copy(flip[:, u, :], psum[7][:, :]).then_inc(S["flipped"], 1)
                    dve.wait_ge(S["yB"], it * 2 + (u + 1))
                    dve.wait_ge(S["scattered"], it * 2 + (u + 1))
                    V.tensor_copy(ybuf[:, 512:1024], psum[7][:, :]).then_inc(S["outB"], 1)
                    dve.wait_ge(S["gatherB"], it * 2 + (u + 2))
                    V.tensor_copy(hid[:, 1 - u, 4:8, :], psum[5][:, :].rearrange("p (k s) -> p k s", k=4)).then_inc(S["hidB"], 1)

            n_done[0] = 0
            dve.wait_ge(S["scattered"], trips * 2 + 1)
            dve.wait_ge(S["ln2_in"], 32)
            for i in range(2):
                banks.wait_read(dve, ("g2", i))

            def last_step(ins):
                n_done[0] += 1
                ins.then_inc(S["final_norm"], 1)
                dve.wait_ge(S["final_norm"], n_done[0])
            step = last_step
            for t in range(2):
                for half in range(2):
                    cols = slice(512 * half, 512 * half + 512)
                    step(V.tensor_tensor(h_t[:, t, cols], psum[2 * t + half][:, :], g2b[:, cols], ALU.mult))
                m, bias = residual_norm(t, x1[:, t, :])
                V.tensor_tensor(m, m, bias, ALU.add).then_inc(S["out_ready"], 1)

        @block.gpsimd
        def _(pool):
            G = nc.gpsimd
            n_done = [0]

            def step(ins):
                n_done[0] += 1
                ins.then_inc(S["pstep"], 1)
                pool.wait_ge(S["pstep"], n_done[0])

            def inputs(s):
                if s == 0:
                    banks.wait_filled(pool, ("X", LEVELS - 1, 3))
                    banks.wait_read(pool, ("toTok", 7))
                if s >= 2:
                    banks.wait_filled(pool, ("S", 1, s - 2))
                for n, (src, w, dst) in enumerate(((vtok, BETA, vbeta), (ktok, NBEG, kbeta), (ktok, KEND, kend))):
                    for d in range(2):
                        t, c = where(d, s)
                        p = slice(64 * c, 64 * c + 64)
                        o = 16 * d + 4 * t
                        ins = G.tensor_tensor(dst[p, s % 2], src[p, t], gcol(w)[p, o:o + 4].unsqueeze(2).to_broadcast([64, 4, 128]), ALU.mult)
                        if (n, d) != (2, 1):
                            step(ins)
                ins.then_inc(S["step_in"], 1)
                pool.wait_ge(S["step_in"], s + 1)

            inputs(0)
            inputs(1)
            for s in range(1, 8):
                if s < 7:
                    for d in range(2):
                        banks.wait_read(pool, ("S", d, s - 1))
                        t, c = where(d, s)
                        o = 32 * c + 16 * d + 4 * t
                        G.tensor_tensor(state[:, (s + 1) % 4, d], state[:, s % 4, d], ge[:, o:o + 4].unsqueeze(2).to_broadcast([128, 4, 128]),
                                        ALU.mult).then_inc(S["s_scaled"], 1)
                    pool.wait_ge(S["s_scaled"], 2 * s)
                    inputs(s + 1)
            for h in range(H):
                pool.wait_ge(S["decay_exp"], h + 1)
                m = decay[:, h % 2, :]
                G.tensor_tensor(m[:, 512:1024], m[:, 512:1024], dist[:, 2048:2560], ALU.mult)
                step(G.tensor_tensor(decayB[:, 512:1024], decayB[:, 512:1024], dist[:, 2560:3072], ALU.mult))
                G.tensor_tensor(m, m, decayB, ALU.add).then_inc(S["decay_ready"], 1)


NAMES = ["x", "c", "ctx", "c_ctx", "w_mod", "b_mod", "w_in", "conv_w", "gdn_a_log", "gdn_dt_bias", "gdn_norm_g",
         "ret_log_gamma", "ret_norm_g", "w_out", "ln1_g", "ln1_b", "w_router", "router_bias", "w_gate_up", "w_down",
         "w_shared_gate_up", "w_shared_down", "ln2_g", "ln2_b"]


def build(nc, shapes):
    a = {n: nc.dram_tensor(n, s, F32, kind="ExternalInput").ap() for n, s in shapes.items()}
    out = nc.dram_tensor("out", (1, T, D), F32, kind="ExternalOutput").ap()
    program(nc, a, out)


def kernel(**inputs):
    import concourse.bacc as bacc
    from concourse.bass_utils import run_bass_kernel_spmd

    arrays = {n: np.ascontiguousarray(inputs[n]) for n in NAMES}
    arrays["const"], arrays["dist"] = constants()
    nc = bacc.Bacc("TRN2", target_bir_lowering=False, num_devices=1)
    build(nc, {n: v.shape for n, v in arrays.items()})
    r = run_bass_kernel_spmd(nc, [arrays], core_ids=[0])
    return r.results[0]["out"]
```

```python
import math
from contextlib import ExitStack

import numpy as np

import concourse.bass as bass
from concourse import mybir

F32 = mybir.dt.float32
I32 = mybir.dt.int32
ALU = mybir.AluOpType
ACT = mybir.ActivationFunctionType

D, T, CTX, H, DK = 1024, 256, 256, 4, 128
NT = (T + CTX) // 128
KB = D // 128
C = 64
E, TOPK, GROUPS, TOPG, FF = 64, 8, 8, 4, 256
CAP = 64
ITEMS = 100
LEVELS = 6
EPS = 1e-6
ALPHA = 2.0 ** 0.25
BIG = 1048576.0
BETA_G = 8
Q0, K0, V0, Z0, BA0, RQ0, RK0, RV0, RG0 = 0, 512, 1024, 1536, 2048, 2064, 2576, 3088, 3600
CHUNKCOLS = 512

CONST = {}
_at = 0
for _n, _w in [("ident", 128), ("two", 2), ("trif", 128), ("trib", 128), ("blk", 128), ("strict", 128), ("ones", 128),
               ("ymask", LEVELS * 2 * 64), ("u1mask", 2 * 64), ("neg", 2 * 64), ("i64", 64), ("iota64", 64),
               ("item", ITEMS), ("item64", ITEMS), ("cos", 256), ("sin", 256), ("part", 1)]:
    CONST[_n] = (_at, _w)
    _at += _w
NCONST = _at
NDIST = 2 * 1024


def constants():
    c = np.zeros((128, NCONST), np.float32)

    def put(name, a):
        o, w = CONST[name]
        c[:, o:o + w] = a

    p = np.arange(128)[:, None]
    f = np.arange(128)[None, :]
    same = (p // C) == (f // C)
    put("ident", p == f)
    put("two", np.concatenate([p % 32 == 0, p % 32 == 1], 1))
    put("trif", same & (p <= f))
    put("trib", same & (p >= f))
    put("blk", same)
    put("strict", p < f)
    put("ones", 1.0)
    i = p % C
    j = np.arange(C)[None, :]
    eye = (i == j).astype(np.float32)

    def lower(b):
        return ((i // (2 * b)) == (j // (2 * b))) & ((i // b) % 2 == 1) & ((j // b) % 2 == 0)

    def upper(b):
        return ((i // (2 * b)) == (j // (2 * b))) & ((i // b) % 2 == 0) & ((j // b) % 2 == 1)

    put("ymask", np.concatenate([eye - m(1 << l) for l in range(LEVELS) for m in (lower, upper)], 1))
    put("u1mask", np.concatenate([eye - upper(1), eye - lower(1)], 1))
    put("neg", np.concatenate([np.where(j > i, 0.0, -1e30), np.where(j < i, 0.0, -1e30)], 1))
    put("i64", eye)
    put("iota64", j)
    it = np.arange(ITEMS)[None, :]
    put("item", it)
    put("item64", it * float(CAP))
    t = np.arange(T)
    quarter = DK // 4
    inv = (np.float32(10000.0) ** (-np.arange(quarter, dtype=np.float32) / np.float32(quarter))).astype(np.float32)
    row, col = (t // 64).astype(np.float32), (t % 64).astype(np.float32)
    ang = np.concatenate([row[:, None] * inv, col[:, None] * inv], -1).astype(np.float32).T
    cos, sin = np.cos(ang), np.sin(ang)
    put("cos", np.concatenate([cos, cos], 0))
    put("sin", np.concatenate([sin, -sin], 0))
    put("part", p)
    d = np.zeros((128, NDIST), np.float32)
    q = np.arange(T)[None, :]
    for k in range(4):
        key = p + 128 * (k % 2)
        if k < 2:
            fwd, bwd = CTX + q - key, T - q + key
        else:
            fwd, bwd = np.maximum(q - key, 0), np.maximum(key - q, 0)
        d[:, 256 * k:256 * k + 256] = fwd
        d[:, 1024 + 256 * k:1024 + 256 * k + 256] = bwd
    return c, d


def bank_uses():
    u = ["small"]
    for i in range(4):
        u += [("mod", i)] + ([("modT", i - 1)] if i else [])
    u += [("modT", 3), "convw"] + [("xT", k) for k in range(KB)]
    for g in range(12):
        u.append(("gdn", g))
        if g == 3:
            u.append("ba")
        if g >= 2:
            u.append(("toTok", g - 2))
        if g >= 4 and g - 4 not in range(4, 8):
            u.append(("toChan", g - 4))
        if 2 <= g <= 9:
            u.append(("mod", g + 2))
            if g > 2:
                u.append(("modT", g + 1))
        if g == 5:
            u.append("gcum")
        if g == 6:
            u += ["rows", "gend"]
        if g == 10:
            u.append(("modT", 11))
    u += [("toTok", 10), ("toTok", 11)] + [("toChan", g) for g in (8, 9, 10, 11)]
    for h in range(H):
        u += [("kk", h), ("bc", 0, h), ("bc", 1, h)]
    for g in range(4):
        u.append(("T1", g))
    for l in range(1, LEVELS):
        u += [("X", l, g) for g in range(4)]
        for g in range(4):
            u += ([("T", l, g)] if l < LEVELS - 1 else []) + [("U", l, g)]
    u += [("eg", h) for h in range(H)]
    fill = filler()
    for s in range(8):
        u += [("nw", 0, s), ("nw", 1, s)] if s else []
        u.append(("u", s))
        u += fill[s]
        u += [("S", 0, s), ("S", 1, s)] if s < 7 else []
    u += [("o", 0), ("o", 1)]
    u += fill[8]
    u += [("g1", 0), ("g1", 1), ("mT", 0), ("mT", 1)]
    u += [("y", half, t) for half in range(2) for t in range(2)]
    u += [("mT", 2), ("mT", 3)]
    u += [("hT", k) for k in range(4)] + ["lg"] + [("hk", k) for k in range(4)]
    u += ["rank", "cnt", ("g2", 0), ("g2", 1), "start", "itrow", "selT", ("sh", 0), "item", ("sh", 1), ("shT", 0), ("shT", 1)]
    return u


def filler():
    f = [[] for _ in range(9)]
    rk = [("rk", h) for h in range(4)]
    rq = [("rq", h) for h in range(4)]
    rv = [("rv", t) for t in range(4)]
    z = [("z", t) for t in range(2)]
    gt = [("gt", t) for t in range(2)]
    f[0], f[1], f[2] = rk[:2], rk[2:], rq
    f[3], f[4] = rv[:2], rv[2:]
    f[5], f[6] = z, gt
    sc = [("sc", h, a) for h in range(H) for a in range(2)]
    f[8] = sc[:2] + [("ro", 0), ("ro", 1)] + sc[2:]
    return f


class Banks:

    def __init__(self, psum, filled, emptied):
        self.at, nth, held, b = {}, [0] * 8, set(), 7
        for name in bank_uses():
            if name == ("mT", 2):
                held.clear()
            b = (b + 1) % 8
            while b in held:
                b = (b + 1) % 8
            self.at[name] = (b, nth[b])
            nth[b] += 1
            if name[0] == "ro":
                held.add(b)
        self.psum, self.filled, self.emptied = psum, filled, emptied
        self.total = nth

    def __getitem__(self, name):
        return self.psum[self.at[name][0]]

    def open(self, pe, name):
        b, n = self.at[name]
        if n:
            pe.wait_ge(self.emptied[b], n)

    def close(self, ins, name):
        ins.then_inc(self.filled[self.at[name][0]], 1)

    def wait_filled(self, eng, name):
        b, n = self.at[name]
        eng.wait_ge(self.filled[b], n + 1)

    def read(self, ins, name):
        ins.then_inc(self.emptied[self.at[name][0]], 1)

    def wait_read(self, eng, name):
        b, n = self.at[name]
        eng.wait_ge(self.emptied[b], n + 1)


SEMS = """ident_in consts_in small_in x_in dist_in rows_in ba_in router_in lnrows_in xres_in ln2_in norms_in rbias_in
root_in root_out sil xn modcols conv_raw conv_acc conv_silu squared gate_raw gate_exp gates_ready decay_arg gexp rows_ready
u1_ready zeroed dt_arg dt_exp at_ready qd_exp qd_ready step_in s_scaled raw_ready rope_done ret_arg decay_exp decay_ready
z_ready g_ready mix_sq mix_ready x1n_ready lg_exp lg_bias sel_ready posx_ready counts_ready items_ready onehot_ready eidx_ready table_ready shgu_in shdn_in gains_ready ln_ready
sh_silu sh_gated shared_done final_norm out_ready out_in
vstep astep pstep gu_in0 gu_in1 dn_in0 dn_in1 gu_free dn_free
pick_ready gatherA gatherB hidA hidB gu_done silu_done gated flip_done flipped yA yB outA outB scattered""".split()


def chunks(a):
    def cols(w, c0, n=CHUNKCOLS):
        return w[:, c0:c0 + n].rearrange("(k p) n -> p k n", p=128)
    wm, wi, wo = a["w_mod"][0], a["w_in"][0], a["w_out"][0]
    def mod(i):
        return ("mod", i), cols(wm, 512 * i)
    w_in = {"gk": K0, "gv": V0, "gq": Q0, "rk": RK0, "rq": RQ0, "rv": RV0, "z": Z0, "gt": RG0}
    w_in = {n: (n, cols(wi, c0)) for n, c0 in w_in.items()}
    out = [mod(i) for i in range(4)] + [w_in["gk"], w_in["gv"], mod(4), mod(5), w_in["gq"], mod(6), mod(7), w_in["rk"],
                                        mod(8), mod(9), w_in["rq"], mod(10), mod(11), w_in["rv"], w_in["z"], w_in["gt"]]
    out += [(("wo", i), cols(wo, 512 * i)) for i in range(2)]
    return out


def slots(names):
    slot, order, nth = {}, [2, 0, 1], {}
    for n in names:
        if n[0] == "mod":
            slot[n] = {2: 0, 3: 1}.get(n[1], 3 + n[1] % 2)
        else:
            slot[n] = order[0]
            order = order[1:] + order[:1]
    seen = [0] * SLOTS
    for n in names:
        nth[n] = seen[slot[n]]
        seen[slot[n]] += 1
    return slot, nth


SLOTS = 5
LAST_USE = {"gk": ("gdn", 3), "gv": ("gdn", 7), "gq": ("gdn", 11), "rk": ("rk", 3), "rq": ("rq", 3), "rv": ("rv", 3),
            "z": ("z", 1), "gt": ("gt", 1), ("wo", 0): ("y", 0, 1), ("wo", 1): ("y", 1, 1)}


def program(nc, a, out):
    with ExitStack() as ctx:
        arena = ctx.enter_context(nc.sbuf_tensor("arena", [128, 49152], F32))
        const = ctx.enter_context(nc.sbuf_tensor("constants", [128, NCONST], F32))
        psum = [ctx.enter_context(nc.psum_tensor(f"bank{i}", [128, 512], F32)) for i in range(8)]
        S = {n: ctx.enter_context(nc.semaphore(n)) for n in SEMS}
        ring_in = [ctx.enter_context(nc.semaphore(f"ring_in{i}")) for i in range(SLOTS)]
        filled = [ctx.enter_context(nc.semaphore(f"filled{i}")) for i in range(8)]
        emptied = [ctx.enter_context(nc.semaphore(f"emptied{i}")) for i in range(8)]
        banks = Banks(psum, filled, emptied)

        def small(name, shape, dt=F32):
            return ctx.enter_context(nc.sbuf_tensor(name, shape, dt))

        rows64 = small("rows64", [64, 128])
        colsT = small("colsT", [128, 64])
        convw = small("convw", [128, 60])
        modc = small("modc", [128, 96])
        st = small("st", [128, 64])
        mv = small("mv", [128, 32])
        GB = small("GB", [128, 64])
        GBt = small("GBt", [128, 64])
        gates = small("gates", [128, 8 * 32])
        ssq = small("ssq", [128, 48])
        ge = small("ge", [128, 64])
        small_consts = small("small_consts", [128, 32])
        eidx = small("eidx", [1, ITEMS + 4], I32)
        route = small("route", [128, 64])
        cst = {n: const[:, o:o + w] for n, (o, w) in CONST.items()}
        ident = cst["ident"]

        def A(off, n):
            return arena[:, off:off + n]

        slot_at = [0, 4096, 8192, 32768, 36864]
        ringbuf = [A(o, 4096).rearrange("p (k n) -> p k n", k=KB) for o in slot_at]
        dist = A(12288, 2048)
        decayB = A(15360, 1024).rearrange("p (b n) -> p b n", b=2)
        ktok = A(16384, 2048).rearrange("p (t h d) -> p t h d", t=NT, h=H)
        vtok = A(18432, 2048).rearrange("p (t h d) -> p t h d", t=NT, h=H)
        kch = A(20480, 2048).rearrange("p (h t) -> p h t", h=H)
        decay = [A(o, 1024) for o in (20480, 21504, 14336, 33792)]
        kend = A(22528, 1024).rearrange("p (b h d) -> p b h d", b=2, h=H)
        nwT = A(23552, 1024).rearrange("p (b d h i) -> p b d h i", b=2, d=2, h=H)
        xmT = A(24576, 4096).rearrange("p (k t) -> p k t", k=KB)
        xall = A(28672, 4096).rearrange("p (t n) -> p t n", t=NT)
        state = A(28672, 4096).rearrange("p (s d h e) -> p s d h e", s=4, d=2, h=H)
        LT = A(32768, 2048).rearrange("p (d h t i) -> p d h t i", d=2, h=H, t=NT)
        Tbd = [A(12288 + 1024 * g, 1024) for g in range(4)]
        Ubd = [A(28672 + 1024 * g, 1024) for g in range(4)]
        Ybd = [A(o, 1024) for o in (41984, 43008, 44032, 47104)]
        vbeta = A(32768, 1024).rearrange("p (b h d) -> p b h d", b=2, h=H)
        kbeta = A(33792, 1024).rearrange("p (b h d) -> p b h d", b=2, h=H)
        Tm = A(34816, 2048).rearrange("p (d h t i) -> p d h t i", d=2, h=H, t=NT)
        usav = A(34816, 2048).rearrange("p (d t h e) -> p d t h e", d=2, t=2, h=H)
        Ym = A(36864, 2048).rearrange("p (d h t i) -> p d h t i", d=2, h=H, t=NT)
        qdec = A(36864, 2048).rearrange("p (d h t) -> p d h t", d=2, h=H)
        Um = A(38912, 2048).rearrange("p (d h t i) -> p d h t i", d=2, h=H, t=NT)
        AT = A(40960, 1024).rearrange("p (d h t i) -> p d h t i", d=2, h=H, t=2)
        convbuf = A(41984, 1040).rearrange("p (b s n) -> p b s n", b=2, s=2)
        convout = A(43024, 1024).rearrange("p (b n) -> p b n", b=2)
        rch = A(41984, 3072)
        rk = rch[:, 0:2048].rearrange("p (h t) -> p h t", h=H)
        rq = rch[:, 2048:3072].rearrange("p (h t) -> p h t", h=H)
        qch = A(45056, 1024).rearrange("p (h t) -> p h t", h=H)
        zs = A(45056, 1024).rearrange("p (t n) -> p t n", t=2)
        tmp = A(46080, 1024)
        raw = tmp.rearrange("p (b n) -> p b n", b=2)
        gs = tmp.rearrange("p (t n) -> p t n", t=2)
        rv = A(47104, 2048).rearrange("p (t n) -> p t n", t=NT)
        rowsT = A(23936, 512)[0:16, :]
        wba = A(47104, 128).rearrange("p (k n) -> p k n", k=KB)
        cwrows = A(16384, 1536)
        modrow = A(22528, 1024).rearrange("p (b n) -> p b n", b=2)
        sil = A(23680, 256).rearrange("p (k m) -> p k m", k=KB)
        qtok = A(46080, 512).rearrange("p (b t d) -> p b t d", b=2, t=2)
        dtmp = A(46592, 512).rearrange("p (b t i) -> p b t i", b=2, t=NT)
        egb = A(46080, 1024).rearrange("p (b d n) -> p b d n", b=2, d=2)
        norms = A(38912, 640)
        junk = A(47360, 512)
        mix = A(24576, 2048).rearrange("p (t n) -> p t n", t=2)
        mixT = A(26624, 2048).rearrange("p (k t) -> p k t", k=KB)
        xres = A(28672, 2048).rearrange("p (t n) -> p t n", t=2)
        g1b = A(30720, 1024)
        lnr = A(34816, 2048)
        h_t = A(36864, 2048).rearrange("p (t n) -> p t n", t=2)
        x1 = A(38912, 2048).rearrange("p (t n) -> p t n", t=2)
        hT = A(41984, 2048).rearrange("p (k t) -> p k t", k=KB)
        htok = A(47104, 2048).rearrange("p (t n) -> p t n", t=2)
        g2b = A(46080, 1024)
        wr = A(32768, 512).rearrange("p (k n) -> p k n", k=KB)
        rt = {n: A(33280 + 128 * i, 128).rearrange("p (t e) -> p t e", t=2)
              for i, n in enumerate(["s", "sb", "masked", "work", "sel", "gate", "posx", "max8"])}
        itemT = A(31232, 512)[0:64, :]
        onehot = A(31744, ITEMS)[0:64, :]
        rbias = A(31844, 64)
        g8 = A(31908, 64)
        tab = A(34304, 4 * ITEMS)
        wsgu = A(20480, 4096).rearrange("p (k n) -> p k n", k=KB)
        wsd = A(44032, 2048).rearrange("p (k n) -> p k n", k=2)
        gu_w = [A(8192 * i, 8192).rearrange("p (j k n) -> p j k n", j=2, k=KB) for i in range(2)]
        dn_w = [A(16384 + 4096 * i, 4096).rearrange("p (j k n) -> p j k n", j=2, k=2) for i in range(2)]
        pick = A(24576, 512).rearrange("p (b t s) -> p b t s", b=2, t=2)
        pickg = A(25088, 512).rearrange("p (b t s) -> p b t s", b=2, t=2)
        flip = A(25600, 1024).rearrange("p (b n) -> p b n", b=2)
        hid = A(26624, 2048).rearrange("p (b k s) -> p b k s", b=2, k=KB)
        ybuf = A(28672, 1024)
        sa = A(29696, 512).rearrange("p (t n) -> p t n", t=2)
        gbuf = A(30208, 512).rearrange("p (b n) -> p b n", b=2)
        shgT = A(30720, 512).rearrange("p (k t) -> p k t", k=2)
        tabv = tab.rearrange("p (w t i) -> p w t i", w=2, t=2)
        gcol = lambda w: gates[:, 32 * w:32 * w + 32]
        BETA, GRAW, EG, NBEG, KEND, GT, EGT, SCR = range(8)
        junk2 = A(22528, 512)

        def unit(m, g):
            return m[:, g // 2, 2 * (g % 2):2 * (g % 2) + 2].rearrange("p h t i -> p (h t) i")

        def corners(bd):
            m = bd.rearrange("p (n i) -> p n i", n=8)
            return [(slice(64 * c, 64 * c + 64), m[64 * c:64 * c + 64, :, 64 * c:64 * c + 64]) for c in range(2)]

        def hT_out(eng, k, modulate):
            use = ("hT", k)
            banks.wait_read(eng, ("modT", 11))
            banks.wait_filled(eng, use)
            for i in range(2):
                m = 2 * k + i
                ins = modulate(hT[:, m, :], banks[use][:, 256 * i:256 * i + 256], modc[:, 64 + 2 * m:65 + 2 * m], modc[:, 48 + 2 * m:49 + 2 * m])
            banks.read(ins, use)

        CH = chunks(a)
        slot, nth = slots([n for n, _ in CH])
        block = ctx.enter_context(nc.Block())

        def rowcol(m, d, h):
            return m[:, 16 * d + h:16 * d + 16:4]

        def where(d, s):
            n = s if d == 0 else (3 - s if s < 4 else 11 - s)
            return n // 2, n % 2

        def trips_of(eng):
            n = eng.value_load(eidx[0:1, ITEMS:ITEMS + 1], min_val=1, max_val=96)
            return eng.snap((n + 3) // 4)

        @block.sync
        def _(sp):
            x2, ctx2 = a["x"][0], a["ctx"][0]
            sp.dma_start(rows64[0:8, :], a["c"].rearrange("a (k p) -> (a k) p", p=128)).then_inc(S["small_in"], 16)
            sp.dma_start(rows64[8:16, :], a["c_ctx"].rearrange("(k p) -> k p", p=128)).then_inc(S["small_in"], 16)
            sp.dma_start(rows64[16:64, :], a["b_mod"].rearrange("a (k p) -> (a k) p", p=128)).then_inc(S["small_in"], 16)
            early = CONST["two"][0] + CONST["two"][1]
            sp.dma_start(const[:, 0:early], a["const"][:, 0:early]).then_inc(S["ident_in"], 16)
            last = {}

            def load_chunk(n):
                name, src = CH[n]
                s = slot[name]
                if s in last:
                    banks.wait_filled(sp, LAST_USE.get(last[s], last[s]))
                last[s] = name
                sp.dma_start(ringbuf[s], src).then_inc(ring_in[s], 16)

            for t in range(NT):
                src = ctx2 if t < 2 else x2
                sp.dma_start(xall[:, t, :], src[128 * (t % 2):128 * (t % 2) + 128, :]).then_inc(S["x_in"], 16)
            for n in range(4):
                load_chunk(n)
            sp.dma_start(cwrows[0:5, :], a["conv_w"][0]).then_inc(S["rows_in"], 16)
            sp.dma_start(small_consts[:, 0:8], a["gdn_a_log"].to_broadcast([128, 8])).then_inc(S["rows_in"], 16)
            sp.dma_start(small_consts[:, 8:16], a["gdn_dt_bias"].to_broadcast([128, 8])).then_inc(S["rows_in"], 16)
            sp.dma_start(small_consts[:, 16:24], a["ret_log_gamma"][0].rearrange("d h -> (d h)").unsqueeze(0).to_broadcast([128, 8])).then_inc(S["rows_in"], 16)
            sp.dma_start(wba, a["w_in"][0][:, BA0:BA0 + 16].rearrange("(k p) n -> p k n", p=128)).then_inc(S["ba_in"], 16)
            load_chunk(4)
            sp.dma_start(const[:, early:], a["const"][:, early:]).then_inc(S["consts_in"], 16)
            for n in range(5, len(CH)):
                name = CH[n][0]
                if name == "z":
                    banks.wait_filled(sp, ("X", LEVELS - 1, 3))
                    sp.dma_start(dist, a["dist"]).then_inc(S["dist_in"], 16)
                load_chunk(n)
            banks.wait_filled(sp, ("u", 7))
            sp.dma_start(norms[:, 0:128], a["gdn_norm_g"].to_broadcast([128, 128])).then_inc(S["norms_in"], 16)
            sp.dma_start(norms[:, 128:640], a["ret_norm_g"].to_broadcast([128, 512])).then_inc(S["norms_in"], 16)
            banks.wait_filled(sp, ("o", 1))
            for t in range(2):
                sp.dma_start(xres[:, t, :], x2[128 * t:128 * t + 128, :]).then_inc(S["xres_in"], 16)
            sp.dma_start(lnr[:, 0:1024], a["ln1_g"].to_broadcast([128, D])).then_inc(S["lnrows_in"], 16)
            sp.dma_start(lnr[:, 1024:2048], a["ln1_b"].to_broadcast([128, D])).then_inc(S["lnrows_in"], 16)
            sp.dma_start(wr, a["w_router"][0].rearrange("(k p) n -> p k n", p=128)).then_inc(S["router_in"], 16)
            sp.dma_start(rbias, a["router_bias"].to_broadcast([128, E])).then_inc(S["rbias_in"], 16)
            banks.wait_filled(sp, ("ro", 1))
            sp.dma_start(wsgu, a["w_shared_gate_up"][0].rearrange("(k p) n -> p k n", p=128)).then_inc(S["shgu_in"], 16)
            sp.wait_ge(S["mix_ready"], 4)
            sp.dma_start(wsd, a["w_shared_down"][0].rearrange("(k p) n -> p k n", p=128)).then_inc(S["shdn_in"], 16)
            sp.wait_ge(S["x1n_ready"], 2)
            sp.dma_start(lnr[:, 0:1024], a["ln2_g"].to_broadcast([128, D])).then_inc(S["ln2_in"], 16)
            sp.dma_start(lnr[:, 1024:2048], a["ln2_b"].to_broadcast([128, D])).then_inc(S["ln2_in"], 16)
            sp.wait_ge(S["eidx_ready"], 1)
            trips = trips_of(sp)
            with sp.Fori(0, trips) as it:
                for u in range(2):
                    es = [sp.value_load(eidx[0:1, bass.ds(it * 4 + (2 * u + j), 1)], min_val=0, max_val=E - 1) for j in range(2)]
                    sp.wait_ge(S["gu_free"], it * 2 + (u + 1))
                    for j in range(2):
                        src = a["w_gate_up"][0, bass.ds(es[j], 1)].rearrange("a (k p) n -> p (a k) n", p=128)
                        sp.dma_start(gu_w[u][:, j], src).then_inc(S[f"gu_in{u}"], 16)
                    sp.wait_ge(S["dn_free"], it * 2 + (u + 1))
                    for j in range(2):
                        src = a["w_down"][0, bass.ds(es[j], 1)].rearrange("a (k p) n -> p (a k) n", p=128)
                        sp.dma_start(dn_w[u][:, j], src).then_inc(S[f"dn_in{u}"], 16)
            for t in range(2):
                sp.wait_ge(S["out_ready"], 1 + t)
                sp.dma_start(out[0, 128 * t:128 * t + 128, :], h_t[:, t, :]).then_inc(S["out_in"], 16)
            sp.wait_ge(S["out_in"], 32)

        @block.tensor
        def _(pe):
            mm, tr = nc.tensor.matmul, nc.tensor.transpose

            def chunk(name):
                pe.wait_ge(ring_in[slot[name]], 16 * (nth[name] + 1))
                return ringbuf[slot[name]]

            pe.wait_ge(S["ident_in"], 16)
            pe.wait_ge(S["small_in"], 48)
            b = banks["small"]
            banks.close(tr(b[:, 0:64], rows64[:, :], ident[0:64, 0:64]), "small")

            def mod_rows(i):
                use = ("mod", i)
                w = chunk(use)
                banks.open(pe, use)
                b = banks[use]
                for r in range(2):
                    for j in range(4):
                        k = 4 * r + j
                        ins = mm(b[32 * j:32 * j + 32, :], sil[:, k, :], w[:, k, :], start=(r == 0), stop=(r == 1))
                banks.close(ins, use)

            def mod_cols(i):
                use = ("modT", i)
                banks.open(pe, use)
                banks.wait_read(pe, ("mod", i))
                b = banks[use]
                for m in range(4):
                    ins = mm(b[:, 2 * m:2 * m + 2], modrow[:, i % 2, 128 * m:128 * m + 128], cst["two"])
                banks.close(ins, use)

            pe.wait_ge(S["sil"], 1)
            for i in range(4):
                mod_rows(i)
                if i:
                    mod_cols(i - 1)
            mod_cols(3)
            pe.wait_ge(S["rows_in"], 64)
            b = banks["convw"]
            for i in range(12):
                ins = tr(b[:, 5 * i:5 * i + 5], cwrows[0:5, 128 * i:128 * i + 128], ident[0:5, 0:5])
            banks.close(ins, "convw")
            for k in range(KB):
                banks.open(pe, ("xT", k))
                b = banks[("xT", k)]
                for t in range(NT):
                    if k == 0:
                        pe.wait_ge(S["xn"], t + 1)
                    ins = tr(b[:, 128 * t:128 * t + 128], xall[:, t, 128 * k:128 * k + 128], ident)
                banks.close(ins, ("xT", k))

            def channel(use, name, h, cols):
                w = chunk(name)
                banks.open(pe, use)
                b = banks[use]
                n = cols.stop - cols.start
                for k in range(KB):
                    ins = mm(b[:, 0:n], w[:, k, 128 * h:128 * h + 128], xmT[:, k, cols], start=(k == 0), stop=(k == KB - 1))
                banks.close(ins, use)

            def tokens(use, name, t):
                w = chunk(name)
                banks.open(pe, use)
                b = banks[use]
                for k in range(KB):
                    ins = mm(b[:, :], xmT[:, k, 128 * t:128 * t + 128], w[:, k, :], start=(k == 0), stop=(k == KB - 1))
                banks.close(ins, use)

            def to_tok(g):
                use = ("toTok", g)
                banks.open(pe, use)
                pe.wait_ge(S["conv_silu"], g + 1)
                b = banks[use]
                for t in range(4 if g < 8 else 2):
                    ins = tr(b[:, 128 * t:128 * t + 128], convout[:, g % 2, 128 * t:128 * t + 128], ident)
                banks.close(ins, use)

            def to_chan(g):
                use = ("toChan", g)
                banks.open(pe, use)
                banks.wait_read(pe, ("toTok", g))
                b = banks[use]
                for t in range(4 if g < 8 else 2):
                    src = ktok[:, t, g, :] if g < 8 else qtok[:, g % 2, t, :]
                    ins = tr(b[:, 128 * t:128 * t + 128], src, ident)
                banks.close(ins, use)

            for k in range(KB):
                banks.wait_read(pe, ("xT", k))
            pe.wait_ge(S["ba_in"], 16)
            for g in range(12):
                channel(("gdn", g), ("gk", "gv", "gq")[g // 4], g % 4, slice(0, 512) if g < 8 else slice(256, 512))
                if g == 3:
                    banks.open(pe, "ba")
                    b = banks["ba"]
                    for t in range(NT):
                        for k in range(KB):
                            ins = mm(b[:, 16 * t:16 * t + 16], xmT[:, k, 128 * t:128 * t + 128], wba[:, k, :],
                                     start=(k == 0), stop=(k == KB - 1))
                    banks.close(ins, "ba")
                if g >= 2:
                    to_tok(g - 2)
                if g >= 4 and g - 4 not in range(4, 8):
                    to_chan(g - 4)
                if 2 <= g <= 9:
                    mod_rows(g + 2)
                    if g > 2:
                        mod_cols(g + 1)
                if g == 5:
                    pe.wait_ge(S["consts_in"], 16)
                    pe.wait_ge(S["gates_ready"], 1)
                    banks.open(pe, "gcum")
                    b = banks["gcum"]
                    mm(b[:, 0:16], cst["trif"], gcol(GRAW)[:, 0:16])
                    mm(b[:, 16:32], cst["trib"], gcol(GRAW)[:, 16:32])
                    banks.close(mm(b[:, 32:64], cst["blk"], gcol(GRAW)), "gcum")
                if g == 6:
                    banks.wait_read(pe, "gcum")
                    banks.open(pe, "rows")
                    b = banks["rows"]
                    pe.wait_ge(S["gexp"], 1)
                    for t in range(NT):
                        ins = tr(b[0:16, 128 * t:128 * t + 128], GBt[:, 16 * t:16 * t + 16], ident)
                    banks.close(ins, "rows")
                    banks.open(pe, "gend")
                    b = banks["gend"]
                    for c in range(2):
                        ins = mm(b[:, 32 * c:32 * c + 32], ident[:, 64 * c:64 * c + 1].to_broadcast([128, 128]), gcol(EGT))
                    banks.close(ins, "gend")
                if g == 10:
                    mod_cols(11)
            to_tok(10)
            to_tok(11)
            for g in (8, 9, 10, 11):
                to_chan(g)

            def spread(out_ap, w, d, h, cols, m):
                row = 8 * w + 4 * d + h
                return mm(out_ap, ident[0:16, row:row + 1].to_broadcast([16, m]), cols)

            banks.wait_read(pe, "rows")
            for h in range(H):
                use = ("kk", h)
                banks.open(pe, use)
                banks.wait_read(pe, ("toChan", h))
                banks.wait_read(pe, ("toChan", 8 + h))
                b = banks[use]
                for t in range(NT):
                    for c in range(2):
                        s = slice(128 * t + 64 * c, 128 * t + 64 * c + 64)
                        mm(b[64 * c:64 * c + 64, 64 * t:64 * t + 64], kch[:, h, s], kch[:, h, s])
                for t in range(2):
                    for c in range(2):
                        o = 128 * t + 64 * c
                        ins = mm(b[64 * c:64 * c + 64, 256 + 64 * t:320 + 64 * t], kch[:, h, 256 + o:320 + o], qch[:, h, o:o + 64])
                banks.close(ins, use)
                for d in range(2):
                    use = ("bc", d, h)
                    banks.open(pe, use)
                    b = banks[use]
                    for w in range(2):
                        for c in range(2):
                            ins = spread(b[64 * c:64 * c + 64, 256 * w:256 * w + 256], w, d, h,
                                         rowsT.rearrange("p (t c i) -> p t c i", t=NT, c=2)[:, :, c, :], 64)
                    banks.close(ins, use)

            def cross(use, stacked, bd):
                banks.open(pe, use)
                b = banks[use]
                for n in range(8):
                    x = 64 * (n % 2)
                    ins = mm(b[x:x + 64, 128 * (n // 2):128 * (n // 2) + 128], stacked[:, n, :], bd[:, 128 * n:128 * n + 128])
                banks.close(ins, use)

            def straight(use, lhs, rhs):
                banks.open(pe, use)
                b = banks[use]
                for n in range(8):
                    for x in range(2):
                        p = slice(64 * x, 64 * x + 64)
                        ins = mm(b[p, 64 * n:64 * n + 64], lhs[p, n, :], rhs[p, n, :])
                banks.close(ins, use)

            for g in range(4):
                use = ("T1", g)
                pe.wait_ge(S["u1_ready"], g + 1)
                banks.open(pe, use)
                b = banks[use]
                for n in range(4):
                    ins = tr(b[:, 128 * n:128 * n + 128], unit(Um, g)[:, 2 * n:2 * n + 2, :].rearrange("p n i -> p (n i)"), ident)
                banks.close(ins, use)
            for l in range(1, LEVELS):
                for g in range(4):
                    banks.wait_read(pe, ("T1", g) if l == 1 else ("T", l - 1, g))
                    cross(("X", l, g), unit(LT, g), Tbd[g])
                for g in range(4):
                    banks.wait_read(pe, ("X", l, g))
                    if l > 1:
                        banks.wait_read(pe, ("U", l - 1, g))
                    if l < LEVELS - 1:
                        cross(("T", l, g), unit(Um, g), Ybd[g])
                        straight(("U", l, g), unit(Ym, g), unit(Um, g))
                    else:
                        cross(("U", l, g), unit(Ym, g), Ubd[g])

            for h in range(H):
                use = ("eg", h)
                banks.open(pe, use)
                b = banks[use]
                for d in range(2):
                    ins = spread(b[:, 256 * d:256 * d + 256], 0, d, h, rowsT[:, 256:512], 128)
                banks.close(ins, use)

            def fill(use):
                kind, n = use
                if kind == "rk":
                    channel(use, "rk", n, slice(0, 512))
                elif kind == "rq":
                    channel(use, "rq", n, slice(256, 512))
                elif kind == "rv":
                    tokens(use, "rv", n)
                else:
                    tokens(use, kind, 2 + n)

            for g in range(4):
                banks.wait_read(pe, ("U", LEVELS - 1, g))
            for s in range(8):
                pe.wait_ge(S["step_in"], s + 1)
                at = [where(d, s) for d in range(2)]
                part = [slice(64 * c, 64 * c + 64) for _, c in at]
                if s:
                    for d in range(2):
                        use = ("nw", d, s)
                        banks.open(pe, use)
                        b = banks[use]
                        for h in range(H):
                            ins = mm(b[:, 64 * h:64 * h + 64], kbeta[part[d], s % 2, h, :], Um[part[d], d, h, at[d][0], :])
                        banks.close(ins, use)
                use = ("u", s)
                banks.open(pe, use)
                b = banks[use]
                if s:
                    for d in range(2):
                        banks.wait_read(pe, ("nw", d, s))
                        banks.wait_read(pe, ("S", d, s - 1))
                for h in range(H):
                    for d in range(2):
                        o = b[part[d], 128 * h:128 * h + 128]
                        ins = mm(o, Um[part[d], d, h, at[d][0], :], vbeta[part[d], s % 2, h, :], start=True, stop=(s == 0))
                        if s:
                            ins = mm(o, nwT[:, s % 2, d, h, :], state[:, s % 4, d, h, :], start=False, stop=True)
                banks.close(ins, use)
                for f in filler()[s]:
                    fill(f)
                if s < 7:
                    banks.wait_read(pe, ("u", s))
                    for d in range(2):
                        use = ("S", d, s)
                        banks.open(pe, use)
                        b = banks[use]
                        for h in range(H):
                            ins = mm(b[:, 128 * h:128 * h + 128], kend[part[d], s % 2, h, :], usav[part[d], d, at[d][0] % 2, h, :])
                        banks.close(ins, use)
            banks.wait_read(pe, ("u", 7))
            pe.wait_ge(S["qd_ready"], 8)
            pe.wait_ge(S["at_ready"], 8)
            for t in range(2):
                use = ("o", t)
                banks.open(pe, use)
                b = banks[use]
                for h in range(H):
                    for c in range(2):
                        p = slice(64 * c, 64 * c + 64)
                        o = b[p, 128 * h:128 * h + 128]
                        m = 2 * t + c
                        cols = slice(64 * m, 64 * m + 64)
                        mm(o, qdec[:, 0, h, cols], state[:, m, 0, h, :], start=True, stop=False)
                        mm(o, qdec[:, 1, h, cols], state[:, 3 - m, 1, h, :], start=False, stop=False)
                        mm(o, AT[p, 0, h, t, :], usav[p, 0, t, h, :], start=False, stop=False)
                        ins = mm(o, AT[p, 1, h, t, :], usav[p, 1, t, h, :], start=False, stop=True)
                banks.close(ins, use)

            def ret_out(h):
                for q in range(2):
                    banks.wait_read(pe, ("sc", h, q))
                for t in range(2):
                    b = banks[("ro", t)]
                    for kt in range(NT):
                        ins = mm(b[:, 128 * h:128 * h + 128], decay[h][:, 256 * kt + 128 * t:256 * kt + 128 * t + 128],
                                 rv[:, kt, 128 * h:128 * h + 128], start=(kt == 0), stop=(kt == NT - 1))
                    if h == H - 1:
                        banks.close(ins, ("ro", t))

            for t in range(2):
                banks.open(pe, ("ro", t))
            for n in range(NT):
                banks.wait_read(pe, ("rv", n))
            pe.wait_ge(S["rope_done"], 8)
            for h in range(H):
                for q in range(2):
                    use = ("sc", h, q)
                    banks.open(pe, use)
                    b = banks[use]
                    for k in range(2):
                        kt = 2 * q + k
                        ins = mm(b[:, 256 * k:256 * k + 256], rk[:, h, 128 * kt:128 * kt + 128], rq[:, h, :])
                    banks.close(ins, use)
                if h:
                    ret_out(h - 1)
            ret_out(H - 1)

            def to_mixT(k):
                use = ("mT", k)
                banks.open(pe, use)
                pe.wait_ge(S["mix_ready"], 2 if k < 2 else 4)
                b = banks[use]
                for i in range(2):
                    for t in range(2):
                        ins = tr(b[:, 256 * i + 128 * t:256 * i + 128 * t + 128], mix[:, t, 128 * (2 * k + i):128 * (2 * k + i) + 128], ident)
                banks.close(ins, use)

            def wide(use, block):
                banks.open(pe, use)
                b = banks[use]
                for m in range(4):
                    c = 2 * (block + m)
                    ins = mm(b[:, 128 * m:128 * m + 128], modc[:, c:c + 1].to_broadcast([128, 128]), ident)
                banks.close(ins, use)

            for i in range(2):
                wide(("g1", i), 16 + 4 * i)
            for part in range(2):
                for k in range(2 * part, 2 * part + 2):
                    to_mixT(k)
                for k in range(2 * part, 2 * part + 2):
                    banks.wait_read(pe, ("mT", k))
                for half in range(2):
                    w = chunk(("wo", half))
                    for t in range(2):
                        use = ("y", half, t)
                        if part == 0:
                            banks.open(pe, use)
                        b = banks[use]
                        for k in range(4 * part, 4 * part + 4):
                            ins = mm(b[:, :], mixT[:, k, 128 * t:128 * t + 128], w[:, k, :], start=(k == 0), stop=(k == KB - 1))
                        if part == 1:
                            banks.close(ins, use)
            for k in range(4):
                use = ("hT", k)
                banks.open(pe, use)
                b = banks[use]
                for i in range(2):
                    for t in range(2):
                        pe.wait_ge(S["x1n_ready"], t + 1)
                        ins = tr(b[:, 256 * i + 128 * t:256 * i + 128 * t + 128], h_t[:, t, 128 * (2 * k + i):128 * (2 * k + i) + 128], ident)
                banks.close(ins, use)
            banks.open(pe, "lg")
            b = banks["lg"]
            for k in range(4):
                banks.wait_read(pe, ("hT", k))
            pe.wait_ge(S["router_in"], 16)
            for t in range(2):
                for k in range(KB):
                    ins = mm(b[:, 64 * t:64 * t + 64], hT[:, k, 128 * t:128 * t + 128], wr[:, k, :], start=(k == 0), stop=(k == KB - 1))
            banks.close(ins, "lg")
            for n in range(4):
                use = ("hk", n)
                t, half = n // 2, n % 2
                banks.open(pe, use)
                b = banks[use]
                for i in range(4):
                    ins = tr(b[:, 128 * i:128 * i + 128], hT[:, 4 * half + i, 128 * t:128 * t + 128], ident)
                banks.close(ins, use)
            pe.wait_ge(S["sel_ready"], 1)
            banks.open(pe, "rank")
            b = banks["rank"]
            sel = rt["sel"]
            mm(b[:, 0:64], cst["strict"], sel[:, 0, :]).then_inc(S["gu_free"], 2)
            mm(b[:, 64:128], cst["ones"], sel[:, 0, :], start=True, stop=False)
            banks.close(mm(b[:, 64:128], cst["strict"], sel[:, 1, :], start=False, stop=True), "rank")
            banks.open(pe, "cnt")
            b = banks["cnt"]
            mm(b[0:64, 0:1], sel[:, 0, :], cst["ones"][:, 0:1], start=True, stop=False).then_inc(S["dn_free"], 1)
            banks.close(mm(b[0:64, 0:1], sel[:, 1, :], cst["ones"][:, 0:1], start=False, stop=True), "cnt")
            for i in range(2):
                wide(("g2", i), 40 + 4 * i)
            banks.open(pe, "start")
            b = banks["start"]
            pe.wait_ge(S["counts_ready"], 1)
            banks.close(mm(b[0:64, 0:1], cst["strict"][0:64, 0:64], route[0:64, 8:9]), "start")
            banks.open(pe, "itrow")
            b = banks["itrow"]
            pe.wait_ge(S["onehot_ready"], 1)
            mm(b[0:1, 0:ITEMS], cst["part"][0:64, :], onehot)
            banks.close(mm(b[0:1, ITEMS:ITEMS + 1], route[0:64, 8:9], cst["ones"][0:64, 0:1]), "itrow")
            banks.open(pe, "selT")
            b = banks["selT"]
            pe.wait_ge(S["posx_ready"], 1)
            for n, m in enumerate(("posx", "gate")):
                for t in range(2):
                    ins = tr(b[0:64, 256 * n + 128 * t:256 * n + 128 * t + 128], rt[m][:, t, :], ident)
            banks.close(ins, "selT")

            def shared_up(t):
                use = ("sh", t)
                banks.open(pe, use)
                b = banks[use]
                for k in range(KB):
                    ins = mm(b[:, :], hT[:, k, 128 * t:128 * t + 128], wsgu[:, k, :], start=(k == 0), stop=(k == KB - 1))
                banks.close(ins, use)

            pe.wait_ge(S["shgu_in"], 16)
            shared_up(0)
            banks.open(pe, "item")
            b = banks["item"]
            pe.wait_ge(S["items_ready"], 1)
            for n in range(4):
                ins = mm(b[:, n * ITEMS:(n + 1) * ITEMS], itemT[:, 128 * n:128 * n + 128], onehot)
            banks.close(ins, "item")
            shared_up(1)
            for t in range(2):
                use = ("shT", t)
                banks.open(pe, use)
                pe.wait_ge(S["sh_gated"], t + 1)
                b = banks[use]
                for k in range(2):
                    ins = tr(b[:, 128 * k:128 * k + 128], sa[:, t, 128 * k:128 * k + 128], ident)
                    if t == 0 and k == 0:
                        ins.then_inc(S["dn_free"], 1)
                banks.close(ins, use)
            pe.wait_ge(S["shdn_in"], 16)
            for k in range(8):
                pe.wait_ge(emptied[k], banks.total[k])

            def acc(t, half):
                return psum[2 * t + half]

            for t in range(2):
                for half in range(2):
                    for k in range(2):
                        mm(acc(t, half)[:, :], shgT[:, k, 128 * t:128 * t + 128], wsd[:, k, 512 * half:512 * half + 512],
                           start=(k == 0), stop=False)

            gA, gB, gU, gF = psum[4], psum[5], psum[6], psum[7]

            def gather(half, buf, free, by):
                b = (gA, gB)[half]
                for k in range(4):
                    for t in range(2):
                        ins = mm(b[:, 128 * k:128 * k + 128], htok[:, t, 128 * (4 * half + k):128 * (4 * half + k) + 128],
                                 pick[:, buf, t, :], start=(t == 0), stop=(t == 1))
                        if free is not None and k == 0 and t == 0:
                            ins.then_inc(free, by)
                ins.then_inc(S[("gatherA", "gatherB")[half]], 1)

            def scatter(buf, last):
                for t in range(2):
                    for half in range(2):
                        ins = mm(acc(t, half)[:, :], flip[:, buf, 256 + 128 * t:256 + 128 * t + 128],
                                 ybuf[:, 512 * half:512 * half + 512], start=False, stop=last)
                        if t == 0 and half == 0 and not last:
                            ins.then_inc(S["gu_free"], 1)
                ins.then_inc(S["scattered"], 1)

            pe.wait_ge(S["table_ready"], 1)
            trips = trips_of(pe)
            pe.wait_ge(S["pick_ready"], 1)
            gather(0, 0, None, 0)
            gather(1, 0, None, 0)
            with pe.Fori(0, trips) as it:
                for u in range(2):
                    pe.wait_ge(S[f"gu_in{u}"], it * 32 + 32)
                    pe.wait_ge(S["hidA"], it * 2 + (u + 1))
                    pe.wait_ge(S["outA"], it * 2 + (u + 1))
                    for k in range(KB):
                        if k == 4:
                            pe.wait_ge(S["hidB"], it * 2 + (u + 1))
                        for j in range(2):
                            ins = mm(gU[64 * j:64 * j + 64, :], hid[:, u, k, 64 * j:64 * j + 64], gu_w[u][:, j, k, :],
                                     start=(k == 0), stop=(k == KB - 1))
                    ins.then_inc(S["gu_done"], 1)
                    pe.wait_ge(S["outB"], it * 2 + (u + 1))
                    scatter(1 - u, False)
                    pe.wait_ge(S["gated"], it * 2 + (u + 2))
                    for n in range(2):
                        tr(gF[:, 128 * n:128 * n + 128], gbuf[:, u, 128 * n:128 * n + 128], ident)
                    for n in range(2):
                        ins = tr(gF[:, 256 + 128 * n:256 + 128 * n + 128], pickg[:, u, n, :], ident)
                    ins.then_inc(S["flip_done"], 1)
                    pe.wait_ge(S["pick_ready"], it * 2 + (u + 2))
                    gather(0, 1 - u, None, 0)
                    pe.wait_ge(S["flipped"], it * 2 + (u + 1))
                    pe.wait_ge(S[f"dn_in{u}"], it * 32 + 32)
                    for half in range(2):
                        b = (gU, gF)[half]
                        for k in range(2):
                            for j in range(2):
                                ins = mm(b[64 * j:64 * j + 64, :], flip[:, u, 128 * k + 64 * j:128 * k + 64 * j + 64],
                                         dn_w[u][:, j, k, 512 * half:512 * half + 512], start=(k == 0), stop=(k == 1))
                        ins.then_inc(S[("yA", "yB")[half]], 1)
                    gather(1, 1 - u, S["dn_free"], 1)
            pe.wait_ge(S["outA"], trips * 2 + 1)
            pe.wait_ge(S["outB"], trips * 2 + 1)
            scatter(1, True)

        @block.scalar
        def _(act):
            n_done = [0]

            def act_fn(out_ap, in_ap, f, **kw):
                return nc.scalar.activation(out_ap, in_ap, f, **kw)

            def step(ins):
                n_done[0] += 1
                ins.then_inc(S["astep"], 1)
                act.wait_ge(S["astep"], n_done[0])

            def sqrt(dst, src, scale=1.0, add=EPS):
                act_fn(dst, src, ACT.Sqrt, scale=scale, bias=add).then_inc(S["root_out"], 1)

            roots_in = [0]

            def sqrt_var(ap):
                roots_in[0] += 1
                act.wait_ge(S["root_in"], roots_in[0])
                sqrt(ap, ap)

            def var(t):
                return mv[:, 18 + t:19 + t]

            banks.wait_read(act, "small")
            act_fn(sil[:, :, 0:2], colsT[:, 0:16].rearrange("p (v k) -> p k v", v=2), ACT.Silu).then_inc(S["sil"], 1)
            for t in range(NT):
                sqrt_var(mv[:, 2:3])

            def mod_rows_out(i):
                use = ("mod", i)
                banks.wait_filled(act, use)
                if i >= 2:
                    banks.wait_filled(act, ("modT", i - 2))
                banks.read(act_fn(modrow[:, i % 2, :], banks[use][:, :], ACT.Copy), use)

            for i in range(4):
                mod_rows_out(i)
            act.wait_ge(S["modcols"], 1)
            for k in range(1, KB, 2):
                use = ("xT", k)
                banks.wait_filled(act, use)
                b = banks[use]
                for v, cols in ((1, slice(0, 256)), (0, slice(256, 512))):
                    ins = act_fn(xmT[:, k, cols], b[:, cols], ACT.Identity, bias=modc[:, 2 * k + v:2 * k + v + 1],
                                 scale=modc[:, 16 + 2 * k + v:16 + 2 * k + v + 1])
                banks.read(ins, use)

            def square(g):
                use = ("toTok", g)
                banks.wait_filled(act, use)
                b = banks[use]
                for t in range(4 if g < 8 else 2):
                    ins = act_fn(junk[:, 128 * t:128 * t + 128], b[:, 128 * t:128 * t + 128], ACT.Square, accum_out=ssq[:, 4 * g + t:4 * g + t + 1])
                step(ins)
                r = ssq[:, 4 * g:4 * g + (4 if g < 8 else 2)]
                sqrt(r, r, *((1.0, EPS) if g < 8 else (float(DK), DK * EPS)))

            def copy_out(use, dst, src):
                banks.wait_filled(act, use)
                banks.read(act_fn(dst, src, ACT.Copy), use)

            def tok_part(g):
                if 4 <= g < 8:
                    copy_out(("toTok", g), vtok[:, :, g - 4, :], banks[("toTok", g)][:, :].rearrange("p (t d) -> p t d", t=4))
                else:
                    square(g)

            def chan_part(g):
                if g < 4:
                    copy_out(("toChan", g), kch[:, g, :], banks[("toChan", g)][:, :])
                else:
                    copy_out(("toChan", g), qch[:, g - 8, :], banks[("toChan", g)][:, 0:256])

            act.wait_ge(S["vstep"], 1)
            for g in range(12):
                use = ("gdn", g)
                banks.wait_filled(act, use)
                b = banks[use]
                if g >= 2:
                    act.wait_ge(S["conv_acc"], g - 1)
                if g < 8:
                    ins = act_fn(convbuf[:, g % 2, :, 2:258], b[:, :].rearrange("p (s n) -> p s n", s=2), ACT.Copy)
                else:
                    ins = act_fn(convbuf[:, g % 2, 1, 2:258], b[:, 0:256], ACT.Copy)
                banks.read(ins, use)
                act.wait_ge(S["conv_acc"], g + 1)
                n = 512 if g < 8 else 256
                act_fn(convout[:, g % 2, 0:n], convout[:, g % 2, 0:n], ACT.Silu).then_inc(S["conv_silu"], 1)
                if g >= 2:
                    tok_part(g - 2)
                if g >= 4 and g - 4 not in range(4, 8):
                    chan_part(g - 4)
                if 2 <= g <= 9:
                    mod_rows_out(g + 2)
                if g == 3:
                    act.wait_ge(S["gate_raw"], 1)
                    act_fn(gcol(BETA), gcol(BETA), ACT.Exp, scale=-1.0)
                    act_fn(small_consts[:, 24:32], small_consts[:, 0:8], ACT.Exp)
                    step(act_fn(gcol(SCR), gcol(SCR), ACT.Exp, scale=-1.0))
                    act_fn(gcol(SCR), gcol(SCR), ACT.Ln, bias=1.0).then_inc(S["gate_exp"], 1)
                if g == 5:
                    act.wait_ge(S["decay_arg"], 1)
                    act_fn(gcol(EG), GB[:, 0:32], ACT.Exp)
                    act_fn(gcol(KEND), gcol(SCR), ACT.Exp)
                    act_fn(gcol(EGT), gcol(GT), ACT.Exp).then_inc(S["gexp"], 1)
            tok_part(10)
            tok_part(11)
            for g in (8, 9, 10, 11):
                chan_part(g)
            for n in range(8):
                act.wait_ge(S["dt_arg"], n + 1)
                act_fn(dtmp[:, n % 2], dtmp[:, n % 2], ACT.Exp).then_inc(S["dt_exp"], 1)

            def places(use):
                return banks[use][:, :].rearrange("p (n i) -> p n i", n=8)

            def block_diagonal(bd, use):
                banks.wait_filled(act, use)
                for p, corner in corners(bd):
                    ins = act_fn(corner, places(use)[p], ACT.Copy)
                banks.read(ins, use)

            act.wait_ge(S["zeroed"], 2)
            for g in range(4):
                block_diagonal(Tbd[g], ("T1", g))
            for l in range(1, LEVELS):
                for g in range(4):
                    if l < LEVELS - 1:
                        block_diagonal(Tbd[g], ("T", l, g))
                    if l == LEVELS - 2:
                        block_diagonal(Ubd[g], ("U", l, g))
                    else:
                        copy_out(("U", l, g), unit(Um, g), places(("U", l, g)))
            for h in range(H):
                use = ("eg", h)
                if h >= 2:
                    act.wait_ge(S["qd_ready"], 2 * (h - 1))
                else:
                    act.wait_ge(S["at_ready"], 8)
                banks.wait_filled(act, use)
                banks.read(act_fn(egb[:, h % 2], banks[use][:, :].rearrange("p (d n) -> p d n", d=2), ACT.Exp), use)
            n_raw = 0

            def decays(h):
                if h == 0:
                    act.wait_ge(S["dist_in"], 16)
                if h >= 2:
                    act.wait_ge(S["decay_ready"], h - 1)
                act.wait_ge(S["ret_arg"], h + 1)
                act_fn(decay[h][:, 0:512], dist[:, 0:512], ACT.Exp, scale=small_consts[:, 16 + h:17 + h])
                act_fn(decayB[:, h % 2], dist[:, 1024:1536], ACT.Exp, scale=small_consts[:, 20 + h:21 + h])
                act_fn(decay[h][:, 512:1024], decay[h][:, 512:1024], ACT.Exp).then_inc(S["decay_exp"], 1)

            for s in range(8):
                if s:
                    for d in range(2):
                        use = ("nw", d, s)
                        copy_out(use, nwT[:, s % 2, d], banks[use][:, 0:256].rearrange("p (h i) -> p h i", h=H))
                for use in filler()[s]:
                    kind, n = use
                    banks.wait_filled(act, use)
                    b = banks[use]
                    if kind in ("rk", "rq"):
                        if n_raw == 0:
                            act.wait_ge(S["qd_ready"], 8)
                        if n_raw >= 2:
                            act.wait_ge(S["rope_done"], n_raw - 1)
                        if kind == "rk":
                            act_fn(rk[:, n, 0:256], b[:, 0:256], ACT.Copy)
                            ins = act_fn(raw[:, n_raw % 2, 0:256], b[:, 256:512], ACT.Copy)
                        else:
                            ins = act_fn(raw[:, n_raw % 2, 0:256], b[:, 0:256], ACT.Copy)
                        banks.read(ins, use)
                        n_raw += 1
                    elif kind == "rv":
                        banks.read(act_fn(rv[:, n, :], b[:, :], ACT.Copy), use)
                    elif kind == "z":
                        banks.read(act_fn(zs[:, n, :], b[:, :], ACT.Silu), use)
                    else:
                        act.wait_ge(S["rope_done"], 8)
                        banks.read(act_fn(gs[:, n, :], b[:, :], ACT.Silu), use)
                if s >= 4:
                    decays(s - 4)
            for t in range(2):
                use = ("o", t)
                banks.wait_filled(act, use)
                b = banks[use]
                for h in range(H):
                    ins = act_fn(junk2[:, 128 * h:128 * h + 128], b[:, 128 * h:128 * h + 128], ACT.Square, accum_out=ssq[:, 4 * t + h:4 * t + h + 1])
                step(ins)
                sqrt(ssq[:, 4 * t:4 * t + 4], ssq[:, 4 * t:4 * t + 4], 1.0 / DK, EPS)
            for i in range(2):
                copy_out(("g1", i), g1b[:, 512 * i:512 * i + 512], banks[("g1", i)][:, :])

            def mixT_out(k):
                copy_out(("mT", k), mixT[:, 2 * k:2 * k + 2, :], banks[("mT", k)][:, :].rearrange("p (k t) -> p k t", k=2))

            sqrt_var(mv[:, 8:12])
            mixT_out(0)
            mixT_out(1)
            sqrt_var(mv[:, 8:12])
            mixT_out(3)
            for t in range(2):
                for i in range(2):
                    sqrt_var(var(t))
            for t in range(2):
                act.wait_ge(S["ln_ready"], t + 1)
                act_fn(h_t[:, t, :], x1[:, t, :], ACT.Identity, scale=var(t), bias=mv[:, 16 + t:17 + t]).then_inc(S["x1n_ready"], 1)
            for k in range(4):
                if k % 2:
                    hT_out(act, k, lambda o, i, sc, bi: act_fn(o, i, ACT.Identity, scale=sc, bias=bi))
            banks.wait_filled(act, "lg")
            act_fn(rt["s"], banks["lg"][:, 0:128].rearrange("p (t e) -> p t e", t=2), ACT.Exp, scale=-1.0).then_inc(emptied[banks.at["lg"][0]], 1)
            for n in range(4):
                t, half = n // 2, n % 2
                copy_out(("hk", n), htok[:, t, 512 * half:512 * half + 512], banks[("hk", n)][:, :])
            for i in range(2):
                copy_out(("g2", i), g2b[:, 512 * i:512 * i + 512], banks[("g2", i)][:, :])
            for t in range(2):
                banks.wait_filled(act, ("sh", t))
                act_fn(sa[:, t, :], banks[("sh", t)][:, 0:256], ACT.Silu).then_inc(S["sh_silu"], 1)
            for t in range(2):
                use = ("shT", t)
                copy_out(use, shgT[:, :, 128 * t:128 * t + 128], banks[use][:, 0:256].rearrange("p (k t) -> p k t", k=2))

            act.wait_ge(S["table_ready"], 1)
            trips = trips_of(act)
            act.wait_ge(S["gatherA"], 1)
            act_fn(hid[:, 0, 0:4, :], psum[4][:, :].rearrange("p (k s) -> p k s", k=4), ACT.Copy).then_inc(S["hidA"], 1)
            with act.Fori(0, trips) as it:
                for u in range(2):
                    act.wait_ge(S["gu_done"], it * 2 + (u + 1))
                    act.wait_ge(S["gated"], it * 2 + (u + 1))
                    act_fn(sa[:, 0, :], psum[6][:, 0:256], ACT.Silu).then_inc(S["silu_done"], 1)
                    act.wait_ge(S["gatherA"], it * 2 + (u + 2))
                    act_fn(hid[:, 1 - u, 0:4, :], psum[4][:, :].rearrange("p (k s) -> p k s", k=4), ACT.Copy).then_inc(S["hidA"], 1)
                    act.wait_ge(S["yA"], it * 2 + (u + 1))
                    act.wait_ge(S["scattered"], it * 2 + (u + 1))
                    act_fn(ybuf[:, 0:512], psum[6][:, :], ACT.Copy).then_inc(S["outA"], 1)
            for t in range(2):
                sqrt_var(var(t))

        @block.vector
        def _(dve):
            V = nc.vector
            n_done = [0]

            def step(ins):
                n_done[0] += 1
                ins.then_inc(S["vstep"], 1)
                dve.wait_ge(S["vstep"], n_done[0])

            n_roots = [0]

            def rooted(ap):
                n_roots[0] += 1
                dve.wait_ge(S["root_out"], n_roots[0])
                step(V.reciprocal(ap, ap))

            def layernorm(dst, src, col):
                s0 = st[:, 0:12].rearrange("p (a n) -> p a n", a=2)
                for i in range(2):
                    ins = V.bn_stats(s0[:, i, :], src[:, 512 * i:512 * i + 512])
                step(ins)
                step(V.bn_aggr(mv[:, 0:2], s0))
                V.tensor_copy(mv[:, 2:3], mv[:, 1:2]).then_inc(S["root_in"], 1)
                rooted(mv[:, 2:3])
                return V.tensor_scalar(dst, src, mv[:, 0:1], mv[:, 2:3], ALU.subtract, ALU.mult)

            def bct(ap, n, m):
                return ap.unsqueeze(2).to_broadcast([ap.shape[0], n, m])

            V.memset(sil, 0.0)
            step(V.memset(A(41984, 1040), 0.0))
            banks.wait_filled(dve, "small")
            banks.read(V.tensor_copy(colsT[:, :], banks["small"][:, 0:64]), "small")
            for t in range(NT):
                dve.wait_ge(S["x_in"], 64)
                layernorm(xall[:, t, :], xall[:, t, :], t).then_inc(S["xn"], 1)
            banks.wait_filled(dve, "convw")
            banks.read(V.tensor_copy(convw[:, :], banks["convw"][:, 0:60]), "convw")
            banks.wait_read(dve, "small")

            def mod_bias(i):
                use = ("modT", i)
                banks.wait_filled(dve, use)
                banks.read(V.scalar_tensor_tensor(
                    out=modc[:, 8 * i:8 * i + 8].rearrange("p (m v) -> p m v", v=2),
                    in0=banks[use][:, 0:8].rearrange("p (m v) -> p m v", v=2), scalar=1.0 if i in (2, 3, 8, 9) else 0.0,
                    in1=bct(colsT[:, 16 + 4 * i:20 + 4 * i], 4, 2), op0=ALU.add, op1=ALU.add), use)

            for i in range(4):
                mod_bias(i)
            banks.wait_read(dve, ("modT", 3))
            V.memset(st[:, 60:61], 0.0).then_inc(S["modcols"], 1)
            for k in range(0, KB, 2):
                use = ("xT", k)
                banks.wait_filled(dve, use)
                b = banks[use]
                for v, cols in ((1, slice(0, 256)), (0, slice(256, 512))):
                    ins = V.tensor_scalar(xmT[:, k, cols], b[:, cols], modc[:, 16 + 2 * k + v:17 + 2 * k + v],
                                          modc[:, 2 * k + v:2 * k + v + 1], ALU.mult, ALU.add)
                banks.read(ins, use)

            def conv(g):
                dve_in = convbuf[:, g % 2, :, :] if g < 8 else convbuf[:, g % 2, 1:2, :]
                banks.wait_read(dve, ("gdn", g))
                if g >= 2:
                    banks.wait_filled(dve, ("toTok", g - 2))
                n = 2 if g < 8 else 1
                o = convout[:, g % 2, 0:256 * n].rearrange("p (s n) -> p s n", s=n)
                tile = {0: 4, 1: 8, 2: 0}[g // 4] + g % 4
                for j in range(5):
                    src, w = dve_in[:, :, j:j + 256], convw[:, 5 * tile + j:5 * tile + j + 1]
                    if j == 0:
                        ins = V.tensor_scalar(o, src, w, None, ALU.mult)
                    else:
                        ins = V.scalar_tensor_tensor(out=o, in0=src, scalar=w, in1=o, op0=ALU.mult, op1=ALU.add)
                    if j < 4:
                        step(ins)
                ins.then_inc(S["conv_acc"], 1)

            def tok_part(g):
                if 4 <= g < 8:
                    return
                use = ("toTok", g)
                n = 4 if g < 8 else 2
                r = ssq[:, 4 * g:4 * g + n]
                rooted(r)
                if g < 8:
                    dst = ktok[:, :, g, :]
                else:
                    if g >= 10:
                        banks.wait_filled(dve, ("toChan", g - 2))
                    dst = qtok[:, g % 2, :, :]
                banks.read(V.tensor_tensor(dst, banks[use][:, 0:128 * n].rearrange("p (t d) -> p t d", t=n), bct(r, n, 128), ALU.mult), use)

            for g in range(12):
                conv(g)
                if g >= 2:
                    tok_part(g - 2)
                if 3 <= g <= 10:
                    mod_bias(g + 1)
                if g == 3:
                    banks.wait_filled(dve, "ba")
                    b = banks["ba"][:, 0:64].rearrange("p (t w d h) -> p w t d h", t=4, w=2, d=2)

                    def dth(m, d):
                        return m.rearrange("p (d t h) -> p d t h", d=2, t=4)[:, d]
                    for d in range(2):
                        V.tensor_copy(dth(gcol(BETA), d), b[:, 0, :, d, :])
                        ins = V.tensor_tensor(dth(gcol(GRAW), d), b[:, 1, :, d, :],
                                              small_consts[:, 8 + 4 * d:12 + 4 * d].unsqueeze(1).to_broadcast([128, 4, 4]), ALU.add)
                    banks.read(ins, "ba")
                    banks.wait_read(dve, "ba")
                    V.scalar_tensor_tensor(out=gcol(SCR), in0=gcol(GRAW), scalar=-1.0, in1=gcol(GRAW), op0=ALU.mult, op1=ALU.max).then_inc(S["gate_raw"], 1)
                if g == 4:
                    dve.wait_ge(S["gate_exp"], 1)
                    V.tensor_scalar(gcol(BETA), gcol(BETA), 1.0, None, ALU.add)
                    step(V.scalar_tensor_tensor(out=gcol(GRAW), in0=gcol(GRAW), scalar=0.0, in1=gcol(SCR), op0=ALU.max, op1=ALU.add))
                    step(V.reciprocal(GB[:, 32:64], gcol(BETA)))
                    V.tensor_copy(gcol(BETA), GB[:, 32:64])
                    for d in range(2):
                        m = gcol(GRAW).rearrange("p (d t h) -> p d t h", d=2, t=4)[:, d]
                        ins = V.scalar_tensor_tensor(out=m, in0=m, scalar=-1.0,
                                                     in1=small_consts[:, 24 + 4 * d:28 + 4 * d].unsqueeze(1).to_broadcast([128, 4, 4]),
                                                     op0=ALU.mult, op1=ALU.mult)
                    ins.then_inc(S["gates_ready"], 1)
                if g == 5:
                    banks.wait_filled(dve, "gcum")
                    V.tensor_copy(GB[:, 0:32], banks["gcum"][:, 0:32])
                    banks.read(V.tensor_copy(gcol(GT), banks["gcum"][:, 32:64]), "gcum")
                    banks.wait_read(dve, "gcum")
                    V.tensor_copy(GBt[:, :].rearrange("p (t x h) -> p x t h", x=4, h=H), GB[:, :].rearrange("p (x t h) -> p x t h", x=4, h=H))
                    V.tensor_tensor(gcol(SCR), gcol(GT), GB[:, 0:32], ALU.subtract).then_inc(S["decay_arg"], 1)
                if g == 6:
                    dve.wait_ge(S["gexp"], 1)
                    V.scalar_tensor_tensor(out=gcol(NBEG), in0=gcol(BETA), scalar=-1.0, in1=gcol(EG), op0=ALU.mult, op1=ALU.mult)
                    banks.wait_filled(dve, "rows")
                    banks.read(V.tensor_copy(rowsT, banks["rows"][0:16, :]), "rows")
                    banks.wait_filled(dve, "gend")
                    banks.read(V.tensor_copy(ge[:, :], banks["gend"][:, 0:64]), "gend")
            tok_part(10)
            tok_part(11)


            def dt_argument(n):
                h, d = n // 2, n % 2
                use = ("bc", d, h)
                banks.wait_filled(dve, use)
                m = dtmp[:, n % 2]
                step(V.tensor_tensor(m, banks[use][:, 0:256].rearrange("p (t i) -> p t i", t=4), bct(rowcol(GB, d, h), 4, 64), ALU.subtract))
                V.tensor_tensor(m, m, cst["neg"][:, 64 * d:64 * d + 64].unsqueeze(1).to_broadcast([128, 4, 64]), ALU.add).then_inc(S["dt_arg"], 1)

            def i64(n):
                return cst["i64"].unsqueeze(1).to_broadcast([128, n, 64])

            def dt_finish(n):
                h, d = n // 2, n % 2
                use = ("bc", d, h)
                dve.wait_ge(S["dt_exp"], n + 1)
                m = dtmp[:, n % 2]
                L, At = LT[:, d, h], AT[:, d, h]
                kk = banks[("kk", h)]
                step(V.tensor_tensor(At, m[:, 2:4, :], i64(2), ALU.add))
                ins = V.tensor_tensor(L, m, banks[use][:, 256:512].rearrange("p (t i) -> p t i", t=4), ALU.mult)
                banks.read(ins, use)
                ins = V.tensor_tensor(At, At, kk[:, 256:384].rearrange("p (t i) -> p t i", t=2), ALU.mult)
                ins.then_inc(S["at_ready"], 1)
                banks.wait_read(dve, use)
                ins = V.tensor_tensor(L, L, kk[:, 0:256].rearrange("p (t i) -> p t i", t=4), ALU.mult)
                if d:
                    banks.read(ins, ("kk", h))
                    banks.wait_read(dve, ("kk", h))
                else:
                    step(ins)
                step(V.tensor_tensor(L, L, i64(4), ALU.add))

            for n in range(9):
                if n < 8:
                    if n % 2 == 0:
                        banks.wait_filled(dve, ("kk", n // 2))
                    dt_argument(n)
                if n:
                    dt_finish(n - 1)
            for g in range(4):
                o = 64 * (g // 2)
                for x in range(2):
                    for c in range(2):
                        p = slice(64 * c, 64 * c + 64)
                        ins = V.tensor_tensor(unit(Um, g)[64 * x:64 * x + 64, c::2, :], unit(LT, g)[p, x::2, :],
                                              cst["u1mask"][p, o:o + 64].unsqueeze(1).to_broadcast([64, 4, 64]), ALU.mult)
                ins.then_inc(S["u1_ready"], 1)
            dve.wait_ge(S["zeroed"], 3)
            for l in range(1, LEVELS):
                for g in range(4):
                    use = ("X", l, g)
                    banks.wait_filled(dve, use)
                    b = banks[use][:, :].rearrange("p (n i) -> p n i", n=8)
                    o = 64 * (2 * l + g // 2)
                    mask = cst["ymask"][:, o:o + 64].unsqueeze(1).to_broadcast([128, 8, 64])
                    if l < LEVELS - 1:
                        for p, corner in corners(Ybd[g]):
                            V.tensor_tensor(corner, b[p], mask[p], ALU.mult)
                    banks.read(V.tensor_tensor(unit(Ym, g), b, mask, ALU.mult), use)
            for h in range(H):
                banks.wait_read(dve, ("eg", h))
                for d in range(2):
                    V.tensor_tensor(qdec[:, d, h, :], egb[:, h % 2, d, :], qch[:, h, :], ALU.mult).then_inc(S["qd_ready"], 1)

            def decay_argument(h):
                if h == 0:
                    dve.wait_ge(S["dist_in"], 16)
                m = decay[h][:, 512:1024]
                step(V.tensor_scalar(m, dist[:, 512:1024], small_consts[:, 16 + h:17 + h], None, ALU.mult))
                V.scalar_tensor_tensor(out=m, in0=dist[:, 1536:2048], scalar=small_consts[:, 20 + h:21 + h], in1=m,
                                       op0=ALU.mult, op1=ALU.add).then_inc(S["ret_arg"], 1)

            def decay_finish(h):
                dve.wait_ge(S["decay_exp"], h + 1)
                for k in range(2):
                    m = decay[h][:, 512 + 384 * k:640 + 384 * k]
                    V.tensor_tensor(m, m, ident, ALU.add)
                V.tensor_tensor(decay[h][:, 0:512], decay[h][:, 0:512], decayB[:, h % 2], ALU.add).then_inc(S["decay_ready"], 1)

            n_rope = 0
            for s in range(8):
                use = ("u", s)
                banks.wait_filled(dve, use)
                for d in range(2):
                    t, c = where(d, s)
                    p = slice(64 * c, 64 * c + 64)
                    ins = V.tensor_copy(usav[p, d, t % 2], banks[use][p, :].rearrange("p (h e) -> p h e", h=H))
                banks.read(ins, use)
                for f in filler()[s]:
                    if f[0] in ("rk", "rq"):
                        banks.wait_read(dve, f)
                        r, dst = raw[:, n_rope % 2, :], (rk[:, f[1], 256:512] if f[0] == "rk" else rq[:, f[1], :])
                        V.tensor_tensor(r[0:64, 256:512], r[64:128, 0:256], cst["sin"][64:128, :], ALU.mult)
                        V.tensor_tensor(r[64:128, 256:512], r[0:64, 0:256], cst["sin"][0:64, :], ALU.mult)
                        step(V.tensor_tensor(dst, r[:, 0:256], cst["cos"], ALU.mult))
                        V.tensor_tensor(dst, dst, r[:, 256:512], ALU.add).then_inc(S["rope_done"], 1)
                        n_rope += 1
                if s < 7:
                    for d in range(2):
                        use = ("S", d, s)
                        banks.wait_filled(dve, use)
                        b = banks[use][:, :].rearrange("p (h e) -> p h e", h=H)
                        nxt = state[:, (s + 1) % 4, d]
                        if s == 0:
                            banks.read(V.tensor_copy(nxt, b), use)
                        else:
                            dve.wait_ge(S["s_scaled"], 2 * (s - 1) + d + 1)
                            banks.read(V.tensor_tensor(nxt, nxt, b, ALU.add), use)
                if s >= 4:
                    decay_argument(s - 4)
                if s >= 5:
                    decay_finish(s - 5)
            decay_finish(3)
            dve.wait_ge(S["gains_ready"], 4)
            for t in range(2):
                use = ("o", t)
                r = ssq[:, 4 * t:4 * t + 4]
                rooted(r)
                m = mix[:, t, 0:512]
                m4 = m.rearrange("p (h e) -> p h e", h=H)
                banks.read(V.tensor_tensor(m4, banks[use][:, :].rearrange("p (h e) -> p h e", h=H), bct(r, 4, 128), ALU.mult), use)
                banks.wait_read(dve, use)
                V.tensor_tensor(m, m, zs[:, t, :], ALU.mult).then_inc(S["mix_ready"], 1)
            for h in range(H):
                dve.wait_ge(S["decay_ready"], h + 1)
                for q in range(2):
                    use = ("sc", h, q)
                    banks.wait_filled(dve, use)
                    m = decay[h][:, 512 * q:512 * q + 512]
                    banks.read(V.scalar_tensor_tensor(out=m, in0=banks[use][:, :], scalar=DK ** -0.5, in1=m, op0=ALU.mult, op1=ALU.mult), use)
            for t in range(2):
                use = ("ro", t)
                banks.wait_filled(dve, use)
                b = banks[use]
                for h in range(H):
                    ins = V.bn_stats(st[:, 6 * h:6 * h + 6], b[:, 128 * h:128 * h + 128])
                step(ins)
                for h in range(H):
                    ins = V.bn_aggr(mv[:, 2 * h:2 * h + 2], st[:, 6 * h:6 * h + 6])
                step(ins)
                V.tensor_copy(mv[:, 8:12], mv[:, 1:8:2]).then_inc(S["root_in"], 1)
                rooted(mv[:, 8:12])
                for h in range(H):
                    ins = V.tensor_scalar(mix[:, t, 512 + 128 * h:640 + 128 * h], b[:, 128 * h:128 * h + 128],
                                          mv[:, 2 * h:2 * h + 1], mv[:, 8 + h:9 + h], ALU.subtract, ALU.mult)
                banks.read(ins, use)
                banks.wait_read(dve, use)
                m = mix[:, t, 512:1024]
                V.tensor_tensor(m, m, gs[:, t, :], ALU.mult).then_inc(S["mix_ready"], 1)
            use = ("mT", 2)
            banks.wait_filled(dve, use)
            banks.read(V.tensor_copy(mixT[:, 4:6, :], banks[use][:, :].rearrange("p (k t) -> p k t", k=2)), use)
            for i in range(2):
                banks.wait_read(dve, ("g1", i))
            for half in range(2):
                for t in range(2):
                    use = ("y", half, t)
                    banks.wait_filled(dve, use)
                    cols = slice(512 * half, 512 * half + 512)
                    banks.read(V.tensor_tensor(h_t[:, t, cols], banks[use][:, :], g1b[:, cols], ALU.mult), use)
            banks.wait_read(dve, ("y", 1, 1))
            dve.wait_ge(S["xres_in"], 32)
            dve.wait_ge(S["lnrows_in"], 32)

            def var(t):
                return mv[:, 18 + t:19 + t]

            def statistics(t, src):
                s0 = st[:, 12 * t:12 * t + 12].rearrange("p (a n) -> p a n", a=2)
                for i in range(2):
                    ins = V.bn_stats(s0[:, i, :], src[:, 512 * i:512 * i + 512])
                step(ins)
                step(V.bn_aggr(mv[:, 2 * t:2 * t + 2], s0))
                V.tensor_copy(var(t), mv[:, 2 * t + 1:2 * t + 2]).then_inc(S["root_in"], 1)

            def residual_norm(t, res, dst):
                m = h_t[:, t, :]
                step(V.scalar_tensor_tensor(out=m, in0=res, scalar=ALPHA, in1=m, op0=ALU.mult, op1=ALU.add))
                statistics(t, m)
                step(V.scalar_tensor_tensor(out=m, in0=m, scalar=mv[:, 2 * t:2 * t + 1], in1=lnr[:, 0:1024], op0=ALU.subtract, op1=ALU.mult))
                rooted(var(t))
                return V.scalar_tensor_tensor(out=dst, in0=m, scalar=var(t), in1=lnr[:, 1024:2048], op0=ALU.mult, op1=ALU.add)

            for t in range(2):
                step(residual_norm(t, xres[:, t, :], x1[:, t, :]))
                statistics(t, x1[:, t, :])
                rooted(var(t))
                V.scalar_tensor_tensor(out=mv[:, 16 + t:17 + t], in0=mv[:, 2 * t:2 * t + 1], scalar=-1.0, in1=var(t),
                                       op0=ALU.mult, op1=ALU.mult).then_inc(S["ln_ready"], 1)
            for k in (0, 2):
                hT_out(dve, k, lambda o, i, sc, bi: V.tensor_scalar(o, i, sc, bi, ALU.mult, ALU.add))

            s_, sb, masked, work, sel, gate, posx, max8 = (rt[n] for n in ("s", "sb", "masked", "work", "sel", "gate", "posx", "max8"))
            banks.wait_read(dve, "lg")
            dve.wait_ge(S["rbias_in"], 16)
            step(V.tensor_scalar(s_, s_, 1.0, None, ALU.add))
            step(V.reciprocal(s_, s_))
            step(V.tensor_tensor(sb, s_, rbias.unsqueeze(1).to_broadcast([128, 2, 64]), ALU.add))
            for t in range(2):
                for g in range(GROUPS):
                    ins = V.max(max8[:, t, 8 * g:8 * g + 8], sb[:, t, 8 * g:8 * g + 8])
            step(ins)
            gsc, gm8, gwork, gpen = (g8[:, 16 * i:16 * i + 16].rearrange("p (t g) -> p t g", t=2) for i in range(4))
            step(V.tensor_tensor(gsc, max8[:, :, 0:64:8], max8[:, :, 1:64:8], ALU.add))
            for t in range(2):
                ins = V.max(gm8[:, t, :], gsc[:, t, :])
            step(ins)
            step(V.memset(gm8[:, :, TOPG:8], 1e30))
            for t in range(2):
                ins = V.match_replace(gwork[:, t, :], gm8[:, t, :], gsc[:, t, :], -1e30)
            step(ins)
            step(V.tensor_scalar(gwork, gwork, -1e29, None, ALU.is_lt))
            step(V.tensor_scalar(gpen, gwork, -1.0, 1e30, ALU.add, ALU.mult))

            def by_expert(m, t):
                return m[:, t, :].rearrange("p (g e) -> p g e", g=GROUPS)

            for t in range(2):
                ins = V.tensor_tensor(by_expert(masked, t), by_expert(sb, t), gwork[:, t, :].unsqueeze(2).to_broadcast([128, 8, 8]), ALU.mult)
            step(ins)
            for t in range(2):
                ins = V.tensor_tensor(by_expert(masked, t), by_expert(masked, t), gpen[:, t, :].unsqueeze(2).to_broadcast([128, 8, 8]), ALU.add)
            step(ins)
            for t in range(2):
                ins = V.max(gm8[:, t, :], masked[:, t, :])
            step(ins)
            for t in range(2):
                ins = V.match_replace(work[:, t, :], gm8[:, t, :], masked[:, t, :], -3e38)
            step(ins)
            step(V.tensor_scalar(sel, work, -2e38, None, ALU.is_lt))
            V.memset(st[:, 60:61], 0.0).then_inc(S["sel_ready"], 1)
            V.tensor_tensor(gate, s_, sel, ALU.mult)
            banks.wait_filled(dve, "cnt")
            banks.read(V.tensor_copy(route[0:64, 0:1], banks["cnt"][0:64, 0:1]), "cnt")
            banks.wait_read(dve, "cnt")
            for r in range(T // CAP):
                ins = V.tensor_scalar(route[0:64, 1 + r:2 + r], route[0:64, 0:1], float(CAP * r), None, ALU.is_gt)
            step(ins)
            V.tensor_reduce(route[0:64, 8:9], route[0:64, 1:5], mybir.AxisListType.X, ALU.add).then_inc(S["counts_ready"], 1)
            dve.wait_ge(S["counts_ready"], 1)
            step(V.tensor_reduce(st[:, 40:42], gate, mybir.AxisListType.X, ALU.add))
            V.reciprocal(st[:, 42:44], st[:, 40:42]).then_inc(S["vstep"], 1)
            n_done[0] += 1
            banks.wait_filled(dve, "start")
            banks.read(V.tensor_copy(route[0:64, 9:10], banks["start"][0:64, 0:1]), "start")
            banks.wait_read(dve, "start")
            V.tensor_scalar(route[0:64, 11:12], route[0:64, 9:10], float(CAP), None, ALU.mult)
            V.tensor_tensor(route[0:64, 10:11], route[0:64, 9:10], route[0:64, 8:9], ALU.add)
            step(V.tensor_scalar(onehot, cst["item"][0:64, :], route[0:64, 9:10], None, ALU.is_ge))
            V.scalar_tensor_tensor(out=onehot, in0=cst["item"][0:64, :], scalar=route[0:64, 10:11], in1=onehot,
                                   op0=ALU.is_lt, op1=ALU.mult).then_inc(S["onehot_ready"], 1)
            V.scalar_tensor_tensor(out=gate, in0=gate, scalar=2.5, in1=bct(st[:, 42:44], 2, 64), op0=ALU.mult, op1=ALU.mult)
            banks.wait_filled(dve, "rank")
            banks.read(V.scalar_tensor_tensor(out=posx, in0=banks["rank"][:, 0:128].rearrange("p (t e) -> p t e", t=2), scalar=BIG,
                                              in1=sel, op0=ALU.add, op1=ALU.mult), "rank")
            banks.wait_read(dve, "rank")
            V.tensor_scalar(posx, posx, -BIG, None, ALU.add).then_inc(S["posx_ready"], 1)
            banks.wait_filled(dve, "itrow")
            banks.read(V.tensor_copy(eidx[0:1, 0:ITEMS + 1], banks["itrow"][0:1, 0:ITEMS + 1]), "itrow")
            banks.wait_read(dve, "itrow")
            V.memset(st[:, 62:63], 0.0).then_inc(S["eidx_ready"], 1)
            banks.wait_filled(dve, "selT")
            b = banks["selT"]
            V.tensor_scalar(itemT[:, 0:256], b[0:64, 0:256], route[0:64, 11:12], None, ALU.add)
            banks.read(V.tensor_copy(itemT[:, 256:512], b[0:64, 256:512]), "selT")
            banks.wait_read(dve, "selT")
            V.memset(st[:, 61:62], 0.0).then_inc(S["items_ready"], 1)
            banks.wait_filled(dve, "item")
            b = banks["item"][:, 0:4 * ITEMS].rearrange("p (w t i) -> p w t i", w=2, t=2)
            V.tensor_tensor(tabv[:, 0], b[:, 0], cst["item64"].unsqueeze(1).to_broadcast([128, 2, ITEMS]), ALU.subtract)
            banks.read(V.tensor_copy(tabv[:, 1], b[:, 1]), "item")
            banks.wait_read(dve, "item")
            V.memset(st[:, 63:64], 0.0).then_inc(S["table_ready"], 1)
            for t in range(2):
                use = ("sh", t)
                dve.wait_ge(S["sh_silu"], t + 1)
                V.tensor_tensor(sa[:, t, :], sa[:, t, :], banks[use][:, 256:512], ALU.mult).then_inc(emptied[banks.at[use][0]], 1)
                banks.wait_read(dve, use)
                V.memset(st[:, 60 + t:61 + t], 0.0).then_inc(S["sh_gated"], 1)

            def choose(buf, col):
                rank = tabv[:, 0, :, col].unsqueeze(3).to_broadcast([128, 2, 2, 64])
                wgt = tabv[:, 1, :, col].unsqueeze(3).to_broadcast([128, 2, 2, 64])
                io = cst["iota64"].unsqueeze(1).unsqueeze(1).to_broadcast([128, 2, 2, 64])
                o = pick[:, buf].rearrange("p t (j s) -> p t j s", j=2)
                og = pickg[:, buf].rearrange("p t (j s) -> p t j s", j=2)
                ins = V.tensor_tensor(o, io, rank, ALU.is_equal)
                return ins, lambda: V.tensor_tensor(og, o, wgt, ALU.mult)

            V.memset(flip[:, 1, :], 0.0).then_inc(S["gated"], 1)
            V.memset(ybuf[:, 0:512], 0.0).then_inc(S["outA"], 1)
            V.memset(ybuf[:, 512:1024], 0.0).then_inc(S["outB"], 1)
            ins, weigh = choose(0, slice(0, 2))
            step(ins)
            weigh().then_inc(S["pick_ready"], 1)
            trips = trips_of(dve)
            dve.wait_ge(S["gatherB"], 1)
            V.tensor_copy(hid[:, 0, 4:8, :], psum[5][:, :].rearrange("p (k s) -> p k s", k=4)).then_inc(S["hidB"], 1)
            chosen = n_done[0]
            with dve.Fori(0, trips) as it:
                for u in range(2):
                    ins, weigh = choose(1 - u, bass.ds(it * 4 + (2 * u + 2), 2))
                    ins.then_inc(S["vstep"], 1)
                    dve.wait_ge(S["vstep"], it * 2 + (u + 1 + chosen))
                    weigh().then_inc(S["pick_ready"], 1)
                    dve.wait_ge(S["silu_done"], it * 2 + (u + 1))
                    V.tensor_tensor(gbuf[:, u, :], sa[:, 0, :], psum[6][:, 256:512], ALU.mult).then_inc(S["gated"], 1)
                    dve.wait_ge(S["flip_done"], it * 2 + (u + 1))
                    V.tensor_copy(flip[:, u, :], psum[7][:, :]).then_inc(S["flipped"], 1)
                    dve.wait_ge(S["yB"], it * 2 + (u + 1))
                    dve.wait_ge(S["scattered"], it * 2 + (u + 1))
                    V.tensor_copy(ybuf[:, 512:1024], psum[7][:, :]).then_inc(S["outB"], 1)
                    dve.wait_ge(S["gatherB"], it * 2 + (u + 2))
                    V.tensor_copy(hid[:, 1 - u, 4:8, :], psum[5][:, :].rearrange("p (k s) -> p k s", k=4)).then_inc(S["hidB"], 1)

            n_done[0] = 0
            dve.wait_ge(S["scattered"], trips * 2 + 1)
            dve.wait_ge(S["ln2_in"], 32)
            for i in range(2):
                banks.wait_read(dve, ("g2", i))

            def last_step(ins):
                n_done[0] += 1
                ins.then_inc(S["final_norm"], 1)
                dve.wait_ge(S["final_norm"], n_done[0])
            step = last_step
            for t in range(2):
                for half in range(2):
                    cols = slice(512 * half, 512 * half + 512)
                    step(V.tensor_tensor(h_t[:, t, cols], psum[2 * t + half][:, :], g2b[:, cols], ALU.mult))
                residual_norm(t, x1[:, t, :], h_t[:, t, :]).then_inc(S["out_ready"], 1)

        @block.gpsimd
        def _(pool):
            G = nc.gpsimd
            n_done = [0]

            def step(ins):
                n_done[0] += 1
                ins.then_inc(S["pstep"], 1)
                pool.wait_ge(S["pstep"], n_done[0])

            def inputs(s):
                if s == 0:
                    banks.wait_filled(pool, ("X", LEVELS - 1, 3))
                    banks.wait_read(pool, ("toTok", 7))
                if s >= 2:
                    banks.wait_filled(pool, ("S", 1, s - 2))
                for n, (src, w, dst) in enumerate(((vtok, BETA, vbeta), (ktok, NBEG, kbeta), (ktok, KEND, kend))):
                    for d in range(2):
                        t, c = where(d, s)
                        p = slice(64 * c, 64 * c + 64)
                        o = 16 * d + 4 * t
                        ins = G.tensor_tensor(dst[p, s % 2], src[p, t], gcol(w)[p, o:o + 4].unsqueeze(2).to_broadcast([64, 4, 128]), ALU.mult)
                        if (n, d) != (2, 1):
                            step(ins)
                ins.then_inc(S["step_in"], 1)
                pool.wait_ge(S["step_in"], s + 1)

            banks.wait_filled(pool, ("xT", KB - 1))
            G.memset(A(12288, 4096), 0.0).then_inc(S["zeroed"], 1)
            G.memset(A(28672, 4096), 0.0).then_inc(S["zeroed"], 1)
            banks.wait_read(pool, ("toTok", 11))
            G.memset(A(41984, 3072), 0.0)
            G.memset(Ybd[3], 0.0).then_inc(S["zeroed"], 1)
            inputs(0)
            inputs(1)
            for s in range(1, 8):
                if s < 7:
                    for d in range(2):
                        banks.wait_read(pool, ("S", d, s - 1))
                        t, c = where(d, s)
                        o = 32 * c + 16 * d + 4 * t
                        G.tensor_tensor(state[:, (s + 1) % 4, d], state[:, s % 4, d], ge[:, o:o + 4].unsqueeze(2).to_broadcast([128, 4, 128]),
                                        ALU.mult).then_inc(S["s_scaled"], 1)
                    pool.wait_ge(S["s_scaled"], 2 * s)
                    inputs(s + 1)
            pool.wait_ge(S["norms_in"], 32)
            for t in range(2):
                banks.wait_read(pool, ("z", t))
                m4 = zs[:, t, :].rearrange("p (h e) -> p h e", h=H)
                G.tensor_tensor(m4, m4, norms[:, 0:128].unsqueeze(1).to_broadcast([128, 4, 128]), ALU.mult).then_inc(S["gains_ready"], 1)
            for t in range(2):
                banks.wait_read(pool, ("gt", t))
                G.tensor_tensor(gs[:, t, :], gs[:, t, :], norms[:, 128:640], ALU.mult).then_inc(S["gains_ready"], 1)


NAMES = ["x", "c", "ctx", "c_ctx", "w_mod", "b_mod", "w_in", "conv_w", "gdn_a_log", "gdn_dt_bias", "gdn_norm_g",
         "ret_log_gamma", "ret_norm_g", "w_out", "ln1_g", "ln1_b", "w_router", "router_bias", "w_gate_up", "w_down",
         "w_shared_gate_up", "w_shared_down", "ln2_g", "ln2_b"]


def build(nc, shapes):
    a = {n: nc.dram_tensor(n, s, F32, kind="ExternalInput").ap() for n, s in shapes.items()}
    out = nc.dram_tensor("out", (1, T, D), F32, kind="ExternalOutput").ap()
    program(nc, a, out)


def kernel(**inputs):
    import concourse.bacc as bacc
    from concourse.bass_utils import run_bass_kernel_spmd

    arrays = {n: np.ascontiguousarray(inputs[n]) for n in NAMES}
    arrays["const"], arrays["dist"] = constants()
    nc = bacc.Bacc("TRN2", target_bir_lowering=False, num_devices=1)
    build(nc, {n: v.shape for n, v in arrays.items()})
    r = run_bass_kernel_spmd(nc, [arrays], core_ids=[0])
    return r.results[0]["out"]
```

```python
import math
from contextlib import ExitStack

import numpy as np

import concourse.bass as bass
from concourse import mybir

F32 = mybir.dt.float32
I32 = mybir.dt.int32
BF16 = mybir.dt.bfloat16
ALU = mybir.AluOpType
ACT = mybir.ActivationFunctionType

D, T, CTX, H, DK = 1024, 256, 256, 4, 128
NT = (T + CTX) // 128
KB = D // 128
C = 64
E, TOPK, GROUPS, TOPG, FF = 64, 8, 8, 4, 256
CAP = 64
ITEMS = 100
LEVELS = 6
EPS = 1e-6
ALPHA = 2.0 ** 0.25
BIG = 1048576.0
BETA_G = 8
Q0, K0, V0, Z0, BA0, RQ0, RK0, RV0, RG0 = 0, 512, 1024, 1536, 2048, 2064, 2576, 3088, 3600
CHUNKCOLS = 512

CONST = {}
_at = 0
for _n, _w in [("ident", 128), ("two", 2), ("trif", 128), ("trib", 128), ("blk", 128), ("strict", 128), ("ones", 128),
               ("ymask", LEVELS * 2 * 64), ("u1mask", 2 * 64), ("neg", 2 * 64), ("i64", 64), ("iota64", 64),
               ("item", ITEMS), ("item64", ITEMS), ("cos", 256), ("sin", 256), ("part", 1)]:
    CONST[_n] = (_at, _w)
    _at += _w
NCONST = _at
UNITS = (0, 2, 1, 3)
NDIST = 2 * 1024


def constants():
    c = np.zeros((128, NCONST), np.float32)

    def put(name, a):
        o, w = CONST[name]
        c[:, o:o + w] = a

    p = np.arange(128)[:, None]
    f = np.arange(128)[None, :]
    same = (p // C) == (f // C)
    put("ident", p == f)
    put("two", np.concatenate([p % 32 == 0, p % 32 == 1], 1))
    put("trif", same & (p <= f))
    put("trib", same & (p >= f))
    put("blk", same)
    put("strict", p < f)
    put("ones", 1.0)
    i = p % C
    j = np.arange(C)[None, :]
    eye = (i == j).astype(np.float32)

    def lower(b):
        return ((i // (2 * b)) == (j // (2 * b))) & ((i // b) % 2 == 1) & ((j // b) % 2 == 0)

    def upper(b):
        return ((i // (2 * b)) == (j // (2 * b))) & ((i // b) % 2 == 0) & ((j // b) % 2 == 1)

    put("ymask", np.concatenate([eye - m(1 << l) for l in range(LEVELS) for m in (lower, upper)], 1))
    put("u1mask", np.concatenate([eye - upper(1), eye - lower(1)], 1))
    put("neg", np.concatenate([np.where(j > i, 0.0, -1e30), np.where(j < i, 0.0, -1e30)], 1))
    put("i64", eye)
    put("iota64", j)
    it = np.arange(ITEMS)[None, :]
    put("item", it)
    put("item64", it * float(CAP))
    t = np.arange(T)
    quarter = DK // 4
    inv = (np.float32(10000.0) ** (-np.arange(quarter, dtype=np.float32) / np.float32(quarter))).astype(np.float32)
    row, col = (t // 64).astype(np.float32), (t % 64).astype(np.float32)
    ang = np.concatenate([row[:, None] * inv, col[:, None] * inv], -1).astype(np.float32).T
    cos, sin = np.cos(ang), np.sin(ang)
    put("cos", np.concatenate([cos, cos], 0))
    put("sin", np.concatenate([sin, -sin], 0))
    put("part", p)
    d = np.zeros((128, NDIST), np.float32)
    q = np.arange(T)[None, :]
    for k in range(4):
        key = p + 128 * (k % 2)
        if k < 2:
            fwd, bwd = CTX + q - key, T - q + key
        else:
            fwd, bwd = np.maximum(q - key, 0), np.maximum(key - q, 0)
        d[:, 256 * k:256 * k + 256] = fwd
        d[:, 1024 + 256 * k:1024 + 256 * k + 256] = bwd
    return c, d


def bank_uses():
    u = ["small"]
    for i in range(4):
        u += [("mod", i)] + ([("modT", i - 1)] if i else [])
    u += [("modT", 3), "convw"] + [("xT", k) for k in range(KB)]
    for g in range(12):
        u.append(("gdn", g))
        if g == 3:
            u.append("ba")
        if g >= 2:
            u.append(("toTok", g - 2))
        if g >= 4 and g - 4 not in range(4, 8):
            u.append(("toChan", g - 4))
        if 2 <= g <= 7:
            u.append(("mod", g + 2))
            if g > 2:
                u.append(("modT", g + 1))
        if g == 5:
            u.append("gcum")
        if g == 6:
            u += ["rows", "gend"]
        if g == 8:
            u.append(("modT", 9))
    u += [("toTok", 10), ("mod", 10), ("toTok", 11), ("mod", 11), ("modT", 10), ("modT", 11)] + [("toChan", g) for g in (8, 9, 10, 11)]
    for h in range(H):
        u += [("kk", h), ("bc", 0, h), ("bc", 1, h)]
    for two in (UNITS[:2], UNITS[2:]):
        u += [("T1", g) for g in two] + [("X", 1, g) for g in two]
    for l in range(1, LEVELS):
        if l > 1:
            u += [("X", l, g) for g in UNITS]
        for g in UNITS:
            u += ([("T", l, g)] if l < LEVELS - 1 else []) + [("U", l, g)]
    u += [("eg", h) for h in range(H)]
    fill = filler()
    for s in range(8):
        u += [("nw", 0, s), ("nw", 1, s)] if s else []
        u.append(("u", s))
        u += fill[s]
        u += [("S", 0, s), ("S", 1, s)] if s < 7 else []
    u += [("o", 0), ("o", 1)]
    u += fill[8]
    u += [("g1", 0), ("g1", 1), ("mT", 0), ("mT", 1)]
    u += [("y", half, t) for t in range(2) for half in range(2)]
    u += [("mT", 2), ("mT", 3)]
    u += [("hT", k) for k in range(4)] + ["lg"] + [("hk", k) for k in range(4)] + [("sh", 0)]
    u += ["rank", "cnt", ("g2", 0), ("g2", 1), "start", "itrow", "selT", "item", ("sh", 1), ("shT", 0), ("shT", 1)]
    return u


def filler():
    f = [[] for _ in range(9)]
    rk = [("rk", h) for h in range(4)]
    rq = [("rq", h) for h in range(4)]
    rv = [("rv", t) for t in range(4)]
    z = [("z", t) for t in range(2)]
    gt = [("gt", t) for t in range(2)]
    f[0], f[1], f[2] = rk[:2], rk[2:], rq
    f[3], f[4] = rv[:2], rv[2:]
    f[5], f[6], f[7] = z, gt[:1], gt[1:]
    sc = [("sc", h, a) for h in range(H) for a in range(2)]
    f[8] = sc[:2] + [("ro", 0), ("ro", 1)] + sc[2:]
    return f


class Banks:

    def __init__(self, psum, filled, emptied):
        self.at, nth, held, b = {}, [0] * 8, set(), 7
        for name in bank_uses():
            if name == ("mT", 2):
                held.clear()
            b = (b + 1) % 8
            while b in held:
                b = (b + 1) % 8
            self.at[name] = (b, nth[b])
            nth[b] += 1
            if name[0] == "ro":
                held.add(b)
        self.psum, self.filled, self.emptied = psum, filled, emptied
        self.total = nth

    def __getitem__(self, name):
        return self.psum[self.at[name][0]]

    def open(self, pe, name):
        b, n = self.at[name]
        if n:
            pe.wait_ge(self.emptied[b], n)

    def close(self, ins, name):
        ins.then_inc(self.filled[self.at[name][0]], 1)

    def wait_filled(self, eng, name):
        b, n = self.at[name]
        eng.wait_ge(self.filled[b], n + 1)

    def read(self, ins, name):
        ins.then_inc(self.emptied[self.at[name][0]], 1)

    def wait_read(self, eng, name):
        b, n = self.at[name]
        eng.wait_ge(self.emptied[b], n + 1)


SEMS = """ident_in consts_in small_in x_in dist_in rows_in ba_in router_in lnrows_in xres_in ln2_in norms_in rbias_in
root_in root_out sil xn modcols conv_acc conv_silu gate_raw gate_exp gates_ready decay_arg gexp u1_ready
u1_early lt_ready zeroed dt_arg dt_exp at_ready qd_ready step_in s_scaled rope_done ret_arg decay_exp
decay_ready mix_ready x1n_ready sel_ready posx_ready counts_ready items_ready onehot_ready htok_ready
parts_ready eidx_ready table_ready shgu_in shdn_in gains_ready ln_ready sh_silu sh_gated final_norm acc_ready
last_ready last_normed out_ready out_in vstep astep pstep gu_in0 gu_in1 dn_in0 dn_in1 gu_free dn_free
pick_ready gatherA gatherB hidA hidB gu_done silu_done gated flip_done flipped yA yB outA outB scattered""".split()


def chunks(a):
    def cols(w, c0, n=CHUNKCOLS):
        return w[:, c0:c0 + n].rearrange("(k p) n -> p k n", p=128)
    wm, wi, wo = a["w_mod"][0], a["w_in"][0], a["w_out"][0]
    def mod(i):
        return ("mod", i), cols(wm, 512 * i)
    w_in = {"gk": K0, "gv": V0, "gq": Q0, "rk": RK0, "rq": RQ0, "rv": RV0, "z": Z0, "gt": RG0}
    w_in = {n: (n, cols(wi, c0)) for n, c0 in w_in.items()}
    out = [mod(i) for i in range(4)] + [w_in["gk"], w_in["gv"], mod(4), mod(5), w_in["gq"], mod(6), mod(7), w_in["rk"],
                                        mod(8), mod(9), mod(10), mod(11), w_in["rq"], w_in["rv"], w_in["z"], w_in["gt"]]
    out += [(("wo", i), cols(wo, 512 * i)) for i in range(2)]
    return out


def slots(names):
    slot, order, nth = {}, [2, 0, 1], {}
    for n in names:
        if n[0] == "mod":
            slot[n] = {2: 0, 3: 1}.get(n[1], 3 + n[1] % 2)
        else:
            slot[n] = order[0]
            order = order[1:] + order[:1]
    seen = [0] * SLOTS
    for n in names:
        nth[n] = seen[slot[n]]
        seen[slot[n]] += 1
    return slot, nth


SLOTS = 5
LAST_USE = {"gk": ("gdn", 3), "gv": ("gdn", 7), "gq": ("gdn", 11), "rk": ("rk", 3), "rq": ("rq", 3), "rv": ("rv", 3),
            "z": ("z", 1), "gt": ("gt", 1), ("wo", 0): ("y", 0, 1), ("wo", 1): ("y", 1, 1)}


def program(nc, a, out):
    with ExitStack() as ctx:
        arena = ctx.enter_context(nc.sbuf_tensor("arena", [128, 49152], F32))
        const = ctx.enter_context(nc.sbuf_tensor("constants", [128, NCONST], F32))
        psum = [ctx.enter_context(nc.psum_tensor(f"bank{i}", [128, 512], F32)) for i in range(8)]
        S = {n: ctx.enter_context(nc.semaphore(n)) for n in SEMS}
        ring_in = [ctx.enter_context(nc.semaphore(f"ring_in{i}")) for i in range(SLOTS)]
        filled = [ctx.enter_context(nc.semaphore(f"filled{i}")) for i in range(8)]
        emptied = [ctx.enter_context(nc.semaphore(f"emptied{i}")) for i in range(8)]
        banks = Banks(psum, filled, emptied)

        def small(name, shape, dt=F32):
            return ctx.enter_context(nc.sbuf_tensor(name, shape, dt))

        rows64 = small("rows64", [64, 128])
        colsT = small("colsT", [128, 64])
        convw = small("convw", [128, 60])
        modc = small("modc", [128, 96])
        st = small("st", [128, 64])
        mv = small("mv", [128, 32])
        GB = small("GB", [128, 64])
        GBt = small("GBt", [128, 64])
        gates = small("gates", [128, 8 * 32])
        ssq = small("ssq", [128, 48])
        ge = small("ge", [128, 64])
        small_consts = small("small_consts", [128, 32])
        eidx = small("eidx", [1, ITEMS + 4], I32)
        route = small("route", [128, 64])
        cst = {n: const[:, o:o + w] for n, (o, w) in CONST.items()}
        ident = cst["ident"]

        def A(off, n):
            return arena[:, off:off + n]

        slot_at = [0, 4096, 8192, 32768, 36864]
        ringbuf = [A(o, 4096).rearrange("p (k n) -> p k n", k=KB) for o in slot_at]
        dist = A(12288, 2048)
        decayB = A(15360, 1024).rearrange("p (b n) -> p b n", b=2)
        ktok = A(16384, 2048).rearrange("p (t h d) -> p t h d", t=NT, h=H)
        vtok = A(18432, 2048).rearrange("p (t h d) -> p t h d", t=NT, h=H)
        kch = A(20480, 2048).rearrange("p (h t) -> p h t", h=H)
        decay = [A(o, 1024) for o in (20480, 21504, 14336, 33792)]
        kend = A(22528, 1024).rearrange("p (b h d) -> p b h d", b=2, h=H)
        nwT = A(23552, 1024).rearrange("p (b d h i) -> p b d h i", b=2, d=2, h=H)
        xmT = A(24576, 4096).rearrange("p (k t) -> p k t", k=KB)
        xall = A(28672, 4096).rearrange("p (t n) -> p t n", t=NT)
        state = A(28672, 4096).rearrange("p (s d h e) -> p s d h e", s=4, d=2, h=H)
        LT = A(32768, 2048).rearrange("p (d h t i) -> p d h t i", d=2, h=H, t=NT)
        Tbd = [A(12288 + 1024 * g, 1024) for g in range(4)]
        Ubd = [A(28672 + 1024 * g, 1024) for g in range(4)]
        Ybd = [A(o, 1024) for o in (41984, 43008, 44032, 47104)]
        vbeta = A(32768, 1024).rearrange("p (b h d) -> p b h d", b=2, h=H)
        kbeta = A(33792, 1024).rearrange("p (b h d) -> p b h d", b=2, h=H)
        usav = A(34816, 2048).rearrange("p (d t h e) -> p d t h e", d=2, t=2, h=H)
        Ym = A(36864, 2048).rearrange("p (d h t i) -> p d h t i", d=2, h=H, t=NT)
        qdec = A(36864, 2048).rearrange("p (d h t) -> p d h t", d=2, h=H)
        Um = A(38912, 2048).rearrange("p (d h t i) -> p d h t i", d=2, h=H, t=NT)
        AT = A(40960, 1024).rearrange("p (d h t i) -> p d h t i", d=2, h=H, t=2)
        convbuf = A(41984, 1040).rearrange("p (b s n) -> p b s n", b=2, s=2)
        convout = A(43024, 1024).rearrange("p (b n) -> p b n", b=2)
        rch = A(41984, 3072)
        rk = rch[:, 0:2048].rearrange("p (h t) -> p h t", h=H)
        rq = rch[:, 2048:3072].rearrange("p (h t) -> p h t", h=H)
        qch = A(45056, 1024).rearrange("p (h t) -> p h t", h=H)
        zs = A(45056, 1024).rearrange("p (t n) -> p t n", t=2)
        tmp = A(46080, 1024)
        raw = tmp.rearrange("p (b n) -> p b n", b=2)
        gs = tmp.rearrange("p (t n) -> p t n", t=2)
        rv = A(47104, 2048).rearrange("p (t n) -> p t n", t=NT)
        rowsT = A(23936, 512)[0:16, :]
        wba = A(47104, 128).rearrange("p (k n) -> p k n", k=KB)
        cwrows = A(16384, 1536)
        modrow = A(22528, 1024).rearrange("p (b n) -> p b n", b=2)
        sil = A(23680, 256).rearrange("p (k m) -> p k m", k=KB)
        qtok = A(46080, 512).rearrange("p (b t d) -> p b t d", b=2, t=2)
        dtmp = A(46592, 512).rearrange("p (b t i) -> p b t i", b=2, t=NT)
        egb = A(46080, 1024).rearrange("p (b d n) -> p b d n", b=2, d=2)
        norms = A(38912, 640)
        junk = A(47360, 512)
        mix = A(24576, 2048).rearrange("p (t n) -> p t n", t=2)
        mixT = A(26624, 2048).rearrange("p (k t) -> p k t", k=KB)
        xres = A(28672, 2048).rearrange("p (t n) -> p t n", t=2)
        g1b = A(30720, 1024)
        lnr = A(34816, 2048)
        h_t = A(36864, 2048).rearrange("p (t n) -> p t n", t=2)
        x1 = A(38912, 2048).rearrange("p (t n) -> p t n", t=2)
        hT = A(41984, 2048).rearrange("p (k t) -> p k t", k=KB)
        htok = A(24576, 2048).rearrange("p (b n) -> p b n", b=4)
        hparts = [A(o, 1024).bitcast(BF16).rearrange("p (t n) -> p t n", t=2) for o in (47104, 48128, 36864)]
        g2b = A(46080, 1024)
        wr = A(32768, 512).rearrange("p (k n) -> p k n", k=KB)
        rt = {n: A(33280 + 128 * i, 128).rearrange("p (t e) -> p t e", t=2)
              for i, n in enumerate(["s", "sb", "masked", "work", "sel", "gate", "posx", "max8"])}
        itemT = A(31232, 512)[0:64, :]
        onehot = A(31744, ITEMS)[0:64, :]
        rbias = A(31844, 64)
        g8 = A(31908, 64)
        tab = A(34304, 4 * ITEMS)
        wsgu = A(20480, 4096).rearrange("p (k n) -> p k n", k=KB)
        wsd = A(44032, 2048).rearrange("p (k n) -> p k n", k=2)
        gu_w = [A(8192 * i, 8192).rearrange("p (j k n) -> p j k n", j=2, k=KB) for i in range(2)]
        dn_w = [A(16384 + 4096 * i, 4096).rearrange("p (j k n) -> p j k n", j=2, k=2) for i in range(2)]
        pick = A(24576, 256).bitcast(BF16).rearrange("p (b t s) -> p b t s", b=2, t=2)
        pickg = A(25088, 512).rearrange("p (b t s) -> p b t s", b=2, t=2)
        flip = A(25600, 1024).rearrange("p (b n) -> p b n", b=2)
        hid = A(26624, 2048).rearrange("p (b k s) -> p b k s", b=2, k=KB)
        ybuf = A(28672, 1024)
        sa = A(29696, 512).rearrange("p (t n) -> p t n", t=2)
        gbuf = A(30208, 512).rearrange("p (b n) -> p b n", b=2)
        shgT = A(30720, 512).rearrange("p (k t) -> p k t", k=2)
        tabv = tab.rearrange("p (w t i) -> p w t i", w=2, t=2)
        gcol = lambda w: gates[:, 32 * w:32 * w + 32]
        BETA, GRAW, EG, NBEG, KEND, GT, EGT, SCR = range(8)
        junk2 = A(22528, 512)

        def unit(m, g):
            return m[:, g // 2, 2 * (g % 2):2 * (g % 2) + 2].rearrange("p h t i -> p (h t) i")

        def first_U(eng, g, step):
            o = 64 * (g // 2)
            for x in range(2):
                for c in range(2):
                    p = slice(64 * c, 64 * c + 64)
                    ins = eng.tensor_tensor(unit(Um, g)[64 * x:64 * x + 64, c::2, :], unit(LT, g)[p, x::2, :],
                                            cst["u1mask"][p, o:o + 64].unsqueeze(1).to_broadcast([64, 4, 64]), ALU.mult)
                    if (x, c) != (1, 1):
                        step(ins)
            ins.then_inc(S["u1_ready" if g == UNITS[3] else "u1_early"], 1)

        def corners(bd):
            m = bd.rearrange("p (n i) -> p n i", n=8)
            return [(slice(64 * c, 64 * c + 64), m[64 * c:64 * c + 64, :, 64 * c:64 * c + 64]) for c in range(2)]

        def hT_out(eng, k, modulate):
            use = ("hT", k)
            banks.wait_read(eng, ("modT", 11))
            banks.wait_filled(eng, use)
            for i in range(2):
                m = 2 * k + i
                ins = modulate(hT[:, m, :], banks[use][:, 256 * i:256 * i + 256], modc[:, 64 + 2 * m:65 + 2 * m], modc[:, 48 + 2 * m:49 + 2 * m])
            banks.read(ins, use)

        CH = chunks(a)
        slot, nth = slots([n for n, _ in CH])
        block = ctx.enter_context(nc.Block())

        def rowcol(m, d, h):
            return m[:, 16 * d + h:16 * d + 16:4]

        def where(d, s):
            n = s if d == 0 else (3 - s if s < 4 else 11 - s)
            return n // 2, n % 2

        def trips_of(eng):
            before_last = eng.value_load(eidx[0:1, ITEMS:ITEMS + 1], min_val=T * TOPK // CAP - 1, max_val=95)
            trips = eng.snap(before_last // 4)
            return trips, eng.snap(before_last % 4 // 2 + 1)

        def over_pairs(eng, trips, rest, pair):
            with eng.Fori(0, trips) as it:
                for u in range(2):
                    pair(it * 2 + u, it, u, None)
            with eng.Fori(0, rest) as r:
                pair(trips * 2 + r, trips + r, 0, r)

        @block.sync
        def _(sp):
            x2, ctx2 = a["x"][0], a["ctx"][0]
            sp.dma_start(rows64[0:8, :], a["c"].rearrange("a (k p) -> (a k) p", p=128)).then_inc(S["small_in"], 16)
            sp.dma_start(rows64[8:16, :], a["c_ctx"].rearrange("(k p) -> k p", p=128)).then_inc(S["small_in"], 16)
            sp.dma_start(rows64[16:64, :], a["b_mod"].rearrange("a (k p) -> (a k) p", p=128)).then_inc(S["small_in"], 16)
            early = CONST["two"][0] + CONST["two"][1]
            sp.dma_start(const[:, 0:early], a["const"][:, 0:early]).then_inc(S["ident_in"], 16)
            last = {}

            def load_chunk(n):
                name, src = CH[n]
                s = slot[name]
                if s in last:
                    banks.wait_filled(sp, LAST_USE.get(last[s], last[s]))
                last[s] = name
                sp.dma_start(ringbuf[s], src).then_inc(ring_in[s], 16)

            for t in range(NT):
                src = ctx2 if t < 2 else x2
                sp.dma_start(xall[:, t, :], src[128 * (t % 2):128 * (t % 2) + 128, :]).then_inc(S["x_in"], 16)
            for n in range(4):
                load_chunk(n)
            sp.dma_start(cwrows[0:5, :], a["conv_w"][0]).then_inc(S["rows_in"], 16)
            sp.dma_start(small_consts[:, 0:8], a["gdn_a_log"].to_broadcast([128, 8])).then_inc(S["rows_in"], 16)
            sp.dma_start(small_consts[:, 8:16], a["gdn_dt_bias"].to_broadcast([128, 8])).then_inc(S["rows_in"], 16)
            sp.dma_start(small_consts[:, 16:24], a["ret_log_gamma"][0].rearrange("d h -> (d h)").unsqueeze(0).to_broadcast([128, 8])).then_inc(S["rows_in"], 16)
            sp.dma_start(wba, a["w_in"][0][:, BA0:BA0 + 16].rearrange("(k p) n -> p k n", p=128)).then_inc(S["ba_in"], 16)
            load_chunk(4)
            sp.dma_start(const[:, early:], a["const"][:, early:]).then_inc(S["consts_in"], 16)
            for n in range(5, len(CH)):
                name = CH[n][0]
                if name == "z":
                    banks.wait_filled(sp, ("X", LEVELS - 1, 3))
                    sp.dma_start(dist, a["dist"]).then_inc(S["dist_in"], 16)
                load_chunk(n)
            banks.wait_filled(sp, ("u", 7))
            sp.dma_start(norms[:, 0:128], a["gdn_norm_g"].to_broadcast([128, 128])).then_inc(S["norms_in"], 16)
            sp.dma_start(norms[:, 128:640], a["ret_norm_g"].to_broadcast([128, 512])).then_inc(S["norms_in"], 16)
            banks.wait_filled(sp, ("o", 1))
            for t in range(2):
                sp.dma_start(xres[:, t, :], x2[128 * t:128 * t + 128, :]).then_inc(S["xres_in"], 16)
            sp.dma_start(lnr[:, 0:1024], a["ln1_g"].to_broadcast([128, D])).then_inc(S["lnrows_in"], 16)
            sp.dma_start(lnr[:, 1024:2048], a["ln1_b"].to_broadcast([128, D])).then_inc(S["lnrows_in"], 16)
            sp.dma_start(wr, a["w_router"][0].rearrange("(k p) n -> p k n", p=128)).then_inc(S["router_in"], 16)
            sp.dma_start(rbias, a["router_bias"].to_broadcast([128, E])).then_inc(S["rbias_in"], 16)
            banks.wait_filled(sp, ("ro", 1))
            sp.dma_start(wsgu, a["w_shared_gate_up"][0].rearrange("(k p) n -> p k n", p=128)).then_inc(S["shgu_in"], 16)
            sp.wait_ge(S["mix_ready"], 4)
            sp.dma_start(wsd, a["w_shared_down"][0].rearrange("(k p) n -> p k n", p=128)).then_inc(S["shdn_in"], 16)
            sp.wait_ge(S["x1n_ready"], 2)
            sp.dma_start(lnr[:, 0:1024], a["ln2_g"].to_broadcast([128, D])).then_inc(S["ln2_in"], 16)
            sp.dma_start(lnr[:, 1024:2048], a["ln2_b"].to_broadcast([128, D])).then_inc(S["ln2_in"], 16)
            sp.wait_ge(S["eidx_ready"], 1)
            trips, rest = trips_of(sp)
            def pair(p, uses, u, r):
                es = [sp.value_load(eidx[0:1, bass.ds(p * 2 + j, 1)], min_val=0, max_val=E - 1) for j in range(2)]
                sp.wait_ge(S["gu_free"], p + 1 if r is None else p + r + 1)
                for j in range(2):
                    src = a["w_gate_up"][0, bass.ds(es[j], 1)].rearrange("a (k p) n -> p (a k) n", p=128)
                    sp.dma_start(gu_w[u][:, j], src).then_inc(S[f"gu_in{u}"], 16)
                sp.wait_ge(S["dn_free"], p + 1 if r is None else p + r + 1)
                for j in range(2):
                    src = a["w_down"][0, bass.ds(es[j], 1)].rearrange("a (k p) n -> p (a k) n", p=128)
                    sp.dma_start(dn_w[u][:, j], src).then_inc(S[f"dn_in{u}"], 16)

            over_pairs(sp, trips, rest, pair)
            for t in range(2):
                sp.wait_ge(S["out_ready" if t else "last_ready"], 1 if t else 2)
                sp.dma_start(out[0, 128 * t:128 * t + 128, :], h_t[:, t, :]).then_inc(S["out_in"], 16)
            sp.wait_ge(S["out_in"], 32)

        @block.tensor
        def _(pe):
            mm, tr = nc.tensor.matmul, nc.tensor.transpose

            def chunk(name):
                pe.wait_ge(ring_in[slot[name]], 16 * (nth[name] + 1))
                return ringbuf[slot[name]]

            pe.wait_ge(S["ident_in"], 16)
            pe.wait_ge(S["small_in"], 48)
            b = banks["small"]
            banks.close(tr(b[:, 0:64], rows64[:, :], ident[0:64, 0:64]), "small")

            def mod_rows(i):
                use = ("mod", i)
                w = chunk(use)
                banks.open(pe, use)
                b = banks[use]
                for r in range(2):
                    for j in range(4):
                        k = 4 * r + j
                        ins = mm(b[32 * j:32 * j + 32, :], sil[:, k, :], w[:, k, :], start=(r == 0), stop=(r == 1))
                banks.close(ins, use)

            def mod_cols(i):
                use = ("modT", i)
                banks.open(pe, use)
                banks.wait_read(pe, ("mod", i))
                b = banks[use]
                for m in range(4):
                    ins = mm(b[:, 2 * m:2 * m + 2], modrow[:, i % 2, 128 * m:128 * m + 128], cst["two"])
                banks.close(ins, use)

            pe.wait_ge(S["sil"], 1)
            for i in range(4):
                mod_rows(i)
                if i:
                    mod_cols(i - 1)
            mod_cols(3)
            pe.wait_ge(S["rows_in"], 64)
            b = banks["convw"]
            for i in range(12):
                ins = tr(b[:, 5 * i:5 * i + 5], cwrows[0:5, 128 * i:128 * i + 128], ident[0:5, 0:5])
            banks.close(ins, "convw")
            for k in range(KB):
                banks.open(pe, ("xT", k))
                b = banks[("xT", k)]
                for t in range(NT):
                    if k == 0:
                        pe.wait_ge(S["xn"], t + 1)
                    ins = tr(b[:, 128 * t:128 * t + 128], xall[:, t, 128 * k:128 * k + 128], ident)
                banks.close(ins, ("xT", k))

            def channel(use, name, h, cols):
                w = chunk(name)
                banks.open(pe, use)
                b = banks[use]
                n = cols.stop - cols.start
                for k in range(KB):
                    ins = mm(b[:, 0:n], w[:, k, 128 * h:128 * h + 128], xmT[:, k, cols], start=(k == 0), stop=(k == KB - 1))
                banks.close(ins, use)

            def tokens(use, name, t):
                w = chunk(name)
                banks.open(pe, use)
                b = banks[use]
                for k in range(KB):
                    ins = mm(b[:, :], xmT[:, k, 128 * t:128 * t + 128], w[:, k, :], start=(k == 0), stop=(k == KB - 1))
                banks.close(ins, use)

            def to_tok(g):
                use = ("toTok", g)
                banks.open(pe, use)
                pe.wait_ge(S["conv_silu"], g + 1)
                b = banks[use]
                for t in range(4 if g < 8 else 2):
                    ins = tr(b[:, 128 * t:128 * t + 128], convout[:, g % 2, 128 * t:128 * t + 128], ident)
                banks.close(ins, use)

            def to_chan(g):
                use = ("toChan", g)
                banks.open(pe, use)
                banks.wait_read(pe, ("toTok", g))
                b = banks[use]
                for t in range(4 if g < 8 else 2):
                    src = ktok[:, t, g, :] if g < 8 else qtok[:, g % 2, t, :]
                    ins = tr(b[:, 128 * t:128 * t + 128], src, ident)
                banks.close(ins, use)

            for k in range(KB):
                banks.wait_read(pe, ("xT", k))
            pe.wait_ge(S["ba_in"], 16)
            for g in range(12):
                channel(("gdn", g), ("gk", "gv", "gq")[g // 4], g % 4, slice(0, 512) if g < 8 else slice(256, 512))
                if g == 3:
                    banks.open(pe, "ba")
                    b = banks["ba"]
                    for t in range(NT):
                        for k in range(KB):
                            ins = mm(b[:, 16 * t:16 * t + 16], xmT[:, k, 128 * t:128 * t + 128], wba[:, k, :],
                                     start=(k == 0), stop=(k == KB - 1))
                    banks.close(ins, "ba")
                if g >= 2:
                    to_tok(g - 2)
                if g >= 4 and g - 4 not in range(4, 8):
                    to_chan(g - 4)
                if 2 <= g <= 7:
                    mod_rows(g + 2)
                    if g > 2:
                        mod_cols(g + 1)
                if g == 5:
                    pe.wait_ge(S["consts_in"], 16)
                    pe.wait_ge(S["gates_ready"], 1)
                    banks.open(pe, "gcum")
                    b = banks["gcum"]
                    mm(b[:, 0:16], cst["trif"], gcol(GRAW)[:, 0:16])
                    mm(b[:, 16:32], cst["trib"], gcol(GRAW)[:, 16:32])
                    banks.close(mm(b[:, 32:64], cst["blk"], gcol(GRAW)), "gcum")
                if g == 6:
                    banks.wait_read(pe, "gcum")
                    banks.open(pe, "rows")
                    b = banks["rows"]
                    pe.wait_ge(S["gexp"], 1)
                    for t in range(NT):
                        ins = tr(b[0:16, 128 * t:128 * t + 128], GBt[:, 16 * t:16 * t + 16], ident)
                    banks.close(ins, "rows")
                    banks.open(pe, "gend")
                    b = banks["gend"]
                    for c in range(2):
                        ins = mm(b[:, 32 * c:32 * c + 32], ident[:, 64 * c:64 * c + 1].to_broadcast([128, 128]), gcol(EGT))
                    banks.close(ins, "gend")
                if g == 8:
                    mod_cols(9)
            to_tok(10)
            mod_rows(10)
            to_tok(11)
            mod_rows(11)
            mod_cols(10)
            mod_cols(11)
            for g in (8, 9, 10, 11):
                to_chan(g)

            def spread(out_ap, w, d, h, cols, m):
                row = 8 * w + 4 * d + h
                return mm(out_ap, ident[0:16, row:row + 1].to_broadcast([16, m]), cols)

            banks.wait_read(pe, "rows")
            for h in range(H):
                use = ("kk", h)
                banks.open(pe, use)
                banks.wait_read(pe, ("toChan", h))
                banks.wait_read(pe, ("toChan", 8 + h))
                b = banks[use]
                for t in range(NT):
                    for c in range(2):
                        s = slice(128 * t + 64 * c, 128 * t + 64 * c + 64)
                        mm(b[64 * c:64 * c + 64, 64 * t:64 * t + 64], kch[:, h, s], kch[:, h, s])
                for t in range(2):
                    for c in range(2):
                        o = 128 * t + 64 * c
                        ins = mm(b[64 * c:64 * c + 64, 256 + 64 * t:320 + 64 * t], kch[:, h, 256 + o:320 + o], qch[:, h, o:o + 64])
                banks.close(ins, use)
                for d in range(2):
                    use = ("bc", d, h)
                    banks.open(pe, use)
                    b = banks[use]
                    for w in range(2):
                        for c in range(2):
                            ins = spread(b[64 * c:64 * c + 64, 256 * w:256 * w + 256], w, d, h,
                                         rowsT.rearrange("p (t c i) -> p t c i", t=NT, c=2)[:, :, c, :], 64)
                    banks.close(ins, use)

            def cross(use, stacked, bd):
                banks.open(pe, use)
                b = banks[use]
                for n in range(8):
                    x = 64 * (n % 2)
                    ins = mm(b[x:x + 64, 128 * (n // 2):128 * (n // 2) + 128], stacked[:, n, :], bd[:, 128 * n:128 * n + 128])
                banks.close(ins, use)

            def straight(use, lhs, rhs):
                banks.open(pe, use)
                b = banks[use]
                for n in range(8):
                    for x in range(2):
                        p = slice(64 * x, 64 * x + 64)
                        ins = mm(b[p, 64 * n:64 * n + 64], lhs[p, n, :], rhs[p, n, :])
                banks.close(ins, use)

            def transpose_first(g):
                use = ("T1", g)
                if g == UNITS[3]:
                    pe.wait_ge(S["u1_ready"], 1)
                else:
                    pe.wait_ge(S["u1_early"], UNITS.index(g) + 1)
                banks.open(pe, use)
                b = banks[use]
                for n in range(4):
                    ins = tr(b[:, 128 * n:128 * n + 128], unit(Um, g)[:, 2 * n:2 * n + 2, :].rearrange("p n i -> p (n i)"), ident)
                banks.close(ins, use)

            def times_L(l, g):
                banks.wait_read(pe, ("T1", g) if l == 1 else ("T", l - 1, g))
                cross(("X", l, g), unit(LT, g), Tbd[g])

            for two in (UNITS[:2], UNITS[2:]):
                for g in two:
                    transpose_first(g)
                for g in two:
                    times_L(1, g)
            for l in range(1, LEVELS):
                if l > 1:
                    for g in UNITS:
                        times_L(l, g)
                for g in UNITS:
                    banks.wait_read(pe, ("X", l, g))
                    if l > 1:
                        banks.wait_read(pe, ("U", l - 1, g))
                    if l < LEVELS - 1:
                        cross(("T", l, g), unit(Um, g), Ybd[g])
                        straight(("U", l, g), unit(Ym, g), unit(Um, g))
                    else:
                        cross(("U", l, g), unit(Ym, g), Ubd[g])

            for h in range(H):
                use = ("eg", h)
                banks.open(pe, use)
                b = banks[use]
                for d in range(2):
                    ins = spread(b[:, 256 * d:256 * d + 256], 0, d, h, rowsT[:, 256:512], 128)
                banks.close(ins, use)

            def fill(use):
                kind, n = use
                if kind == "rk":
                    channel(use, "rk", n, slice(0, 512))
                elif kind == "rq":
                    channel(use, "rq", n, slice(256, 512))
                elif kind == "rv":
                    tokens(use, "rv", n)
                else:
                    tokens(use, kind, 2 + n)

            for g in range(4):
                banks.wait_read(pe, ("U", LEVELS - 1, g))
            for s in range(8):
                pe.wait_ge(S["step_in"], s + 1)
                at = [where(d, s) for d in range(2)]
                part = [slice(64 * c, 64 * c + 64) for _, c in at]
                if s:
                    for d in range(2):
                        use = ("nw", d, s)
                        banks.open(pe, use)
                        b = banks[use]
                        for h in range(H):
                            ins = mm(b[:, 64 * h:64 * h + 64], kbeta[part[d], s % 2, h, :], Um[part[d], d, h, at[d][0], :])
                        banks.close(ins, use)
                use = ("u", s)
                banks.open(pe, use)
                b = banks[use]
                if s:
                    for d in range(2):
                        banks.wait_read(pe, ("nw", d, s))
                        banks.wait_read(pe, ("S", d, s - 1))
                for h in range(H):
                    o = [b[part[d], 128 * h:128 * h + 128] for d in range(2)]
                    for d in range(2):
                        ins = mm(o[d], Um[part[d], d, h, at[d][0], :], vbeta[part[d], s % 2, h, :], start=True, stop=(s == 0))
                    if s:
                        for d in range(2):
                            ins = mm(o[d], nwT[:, s % 2, d, h, :], state[:, s % 4, d, h, :], start=False, stop=True)
                banks.close(ins, use)
                for f in filler()[s]:
                    fill(f)
                if s < 7:
                    banks.wait_read(pe, ("u", s))
                    for d in range(2):
                        use = ("S", d, s)
                        banks.open(pe, use)
                        b = banks[use]
                        for h in range(H):
                            ins = mm(b[:, 128 * h:128 * h + 128], kend[part[d], s % 2, h, :], usav[part[d], d, at[d][0] % 2, h, :])
                        banks.close(ins, use)
            banks.wait_read(pe, ("u", 7))
            pe.wait_ge(S["qd_ready"], 8)
            pe.wait_ge(S["at_ready"], 8)
            for t in range(2):
                use = ("o", t)
                banks.open(pe, use)
                b = banks[use]
                for h in range(H):
                    halves = [(c, slice(64 * c, 64 * c + 64), 2 * t + c) for c in range(2)]
                    o = [b[p, 128 * h:128 * h + 128] for _, p, _ in halves]
                    for c, p, m in halves:
                        mm(o[c], qdec[:, 0, h, 64 * m:64 * m + 64], state[:, m, 0, h, :], start=True, stop=False)
                    for c, p, m in halves:
                        mm(o[c], qdec[:, 1, h, 64 * m:64 * m + 64], state[:, 3 - m, 1, h, :], start=False, stop=False)
                    for c, p, m in halves:
                        mm(o[c], AT[p, 0, h, t, :], usav[p, 0, t, h, :], start=False, stop=False)
                    for c, p, m in halves:
                        ins = mm(o[c], AT[p, 1, h, t, :], usav[p, 1, t, h, :], start=False, stop=True)
                banks.close(ins, use)

            def ret_out(h):
                for q in range(2):
                    banks.wait_read(pe, ("sc", h, q))
                for t in range(2):
                    b = banks[("ro", t)]
                    for kt in range(NT):
                        ins = mm(b[:, 128 * h:128 * h + 128], decay[h][:, 256 * kt + 128 * t:256 * kt + 128 * t + 128],
                                 rv[:, kt, 128 * h:128 * h + 128], start=(kt == 0), stop=(kt == NT - 1))
                    if h == H - 1:
                        banks.close(ins, ("ro", t))

            for t in range(2):
                banks.open(pe, ("ro", t))
            for n in range(NT):
                banks.wait_read(pe, ("rv", n))
            pe.wait_ge(S["rope_done"], 8)
            for h in range(H):
                for q in range(2):
                    use = ("sc", h, q)
                    banks.open(pe, use)
                    b = banks[use]
                    for k in range(2):
                        kt = 2 * q + k
                        ins = mm(b[:, 256 * k:256 * k + 256], rk[:, h, 128 * kt:128 * kt + 128], rq[:, h, :])
                    banks.close(ins, use)
                if h:
                    ret_out(h - 1)

            def to_mixT(k):
                use = ("mT", k)
                banks.open(pe, use)
                pe.wait_ge(S["mix_ready"], 2 if k < 2 else 4)
                b = banks[use]
                for i in range(2):
                    for t in range(2):
                        ins = tr(b[:, 256 * i + 128 * t:256 * i + 128 * t + 128], mix[:, t, 128 * (2 * k + i):128 * (2 * k + i) + 128], ident)
                banks.close(ins, use)

            def wide(use, block):
                banks.open(pe, use)
                b = banks[use]
                for m in range(4):
                    c = 2 * (block + m)
                    ins = mm(b[:, 128 * m:128 * m + 128], modc[:, c:c + 1].to_broadcast([128, 128]), ident)
                banks.close(ins, use)

            for i in range(2):
                wide(("g1", i), 16 + 4 * i)
            to_mixT(0)
            to_mixT(1)
            ret_out(H - 1)
            for part in range(2):
                if part == 1:
                    to_mixT(2)
                    to_mixT(3)
                for k in range(2 * part, 2 * part + 2):
                    banks.wait_read(pe, ("mT", k))
                for t in range(2):
                    for half in range(2):
                        w = chunk(("wo", half))
                        use = ("y", half, t)
                        if part == 0:
                            banks.open(pe, use)
                        b = banks[use]
                        for k in range(4 * part, 4 * part + 4):
                            ins = mm(b[:, :], mixT[:, k, 128 * t:128 * t + 128], w[:, k, :], start=(k == 0), stop=(k == KB - 1))
                        if part == 1:
                            banks.close(ins, use)
            for t in range(2):
                pe.wait_ge(S["x1n_ready"], t + 1)
                for k in range(4):
                    use = ("hT", k)
                    if t == 0:
                        banks.open(pe, use)
                    b = banks[use]
                    for i in range(2):
                        ins = tr(b[:, 256 * i + 128 * t:256 * i + 128 * t + 128], h_t[:, t, 128 * (2 * k + i):128 * (2 * k + i) + 128], ident)
                    if t == 1:
                        banks.close(ins, use)
            banks.open(pe, "lg")
            b = banks["lg"]
            for k in range(4):
                banks.wait_read(pe, ("hT", k))
            pe.wait_ge(S["router_in"], 16)
            for t in range(2):
                for k in range(KB):
                    ins = mm(b[:, 64 * t:64 * t + 64], hT[:, k, 128 * t:128 * t + 128], wr[:, k, :], start=(k == 0), stop=(k == KB - 1))
            banks.close(ins, "lg")
            for n in range(4):
                use = ("hk", n)
                t, half = n // 2, n % 2
                banks.open(pe, use)
                b = banks[use]
                for i in range(4):
                    ins = tr(b[:, 128 * i:128 * i + 128], hT[:, 4 * half + i, 128 * t:128 * t + 128], ident)
                banks.close(ins, use)
            def shared_up(t):
                use = ("sh", t)
                banks.open(pe, use)
                b = banks[use]
                for k in range(KB):
                    ins = mm(b[:, :], hT[:, k, 128 * t:128 * t + 128], wsgu[:, k, :], start=(k == 0), stop=(k == KB - 1))
                banks.close(ins, use)

            pe.wait_ge(S["shgu_in"], 16)
            shared_up(0)
            pe.wait_ge(S["sel_ready"], 1)
            banks.open(pe, "rank")
            b = banks["rank"]
            sel = rt["sel"]
            mm(b[:, 0:64], cst["strict"], sel[:, 0, :]).then_inc(S["gu_free"], 2)
            mm(b[:, 64:128], cst["ones"], sel[:, 0, :], start=True, stop=False)
            banks.close(mm(b[:, 64:128], cst["strict"], sel[:, 1, :], start=False, stop=True), "rank")
            banks.open(pe, "cnt")
            b = banks["cnt"]
            mm(b[0:64, 0:1], sel[:, 0, :], cst["ones"][:, 0:1], start=True, stop=False).then_inc(S["dn_free"], 1)
            banks.close(mm(b[0:64, 0:1], sel[:, 1, :], cst["ones"][:, 0:1], start=False, stop=True), "cnt")
            for i in range(2):
                wide(("g2", i), 40 + 4 * i)
            banks.open(pe, "start")
            b = banks["start"]
            pe.wait_ge(S["counts_ready"], 1)
            banks.close(mm(b[0:64, 0:1], cst["strict"][0:64, 0:64], route[0:64, 8:9]), "start")
            banks.open(pe, "itrow")
            b = banks["itrow"]
            pe.wait_ge(S["onehot_ready"], 1)
            mm(b[0:1, 0:ITEMS], cst["part"][0:64, :], onehot)
            banks.close(mm(b[0:1, ITEMS:ITEMS + 1], route[0:64, 8:9], cst["ones"][0:64, 0:1]), "itrow")
            banks.open(pe, "selT")
            b = banks["selT"]
            pe.wait_ge(S["posx_ready"], 1)
            for n, m in enumerate(("posx", "gate")):
                for t in range(2):
                    ins = tr(b[0:64, 256 * n + 128 * t:256 * n + 128 * t + 128], rt[m][:, t, :], ident)
            banks.close(ins, "selT")

            banks.open(pe, "item")
            b = banks["item"]
            pe.wait_ge(S["items_ready"], 1)
            for n in range(4):
                ins = mm(b[:, n * ITEMS:(n + 1) * ITEMS], itemT[:, 128 * n:128 * n + 128], onehot)
            banks.close(ins, "item")
            shared_up(1)
            for t in range(2):
                use = ("shT", t)
                banks.open(pe, use)
                pe.wait_ge(S["sh_gated"], t + 1)
                b = banks[use]
                for k in range(2):
                    ins = tr(b[:, 128 * k:128 * k + 128], sa[:, t, 128 * k:128 * k + 128], ident)
                    if t == 0 and k == 0:
                        ins.then_inc(S["dn_free"], 1)
                banks.close(ins, use)
            pe.wait_ge(S["shdn_in"], 16)
            for k in range(8):
                pe.wait_ge(emptied[k], banks.total[k])

            def acc(t, half):
                return psum[2 * t + half]

            for t in range(2):
                for half in range(2):
                    for k in range(2):
                        mm(acc(t, half)[:, :], shgT[:, k, 128 * t:128 * t + 128], wsd[:, k, 512 * half:512 * half + 512],
                           start=(k == 0), stop=False)

            gA, gB, gU, gF = psum[4], psum[5], psum[6], psum[7]

            def gather(half, buf, free, by):
                b = (gA, gB)[half]
                for k in range(4):
                    for n in range(6):
                        t, part = n // 3, hparts[n % 3]
                        ins = mm(b[:, 128 * k:128 * k + 128], part[:, t, 128 * (4 * half + k):128 * (4 * half + k) + 128],
                                 pick[:, buf, t, :], start=(n == 0), stop=(n == 5))
                        if free is not None and k == 0 and n == 0:
                            ins.then_inc(free, by)
                ins.then_inc(S[("gatherA", "gatherB")[half]], 1)

            def scatter(buf, last):
                for t in range(2):
                    for half in range(2):
                        ins = mm(acc(t, half)[:, :], flip[:, buf, 256 + 128 * t:256 + 128 * t + 128],
                                 ybuf[:, 512 * half:512 * half + 512], start=False, stop=last)
                        if last:
                            ins.then_inc(S["acc_ready"], 1)
                        elif t == 0 and half == 0:
                            ins.then_inc(S["gu_free"], 1)
                if not last:
                    ins.then_inc(S["scattered"], 1)

            pe.wait_ge(S["table_ready"], 1)
            trips, rest = trips_of(pe)
            pe.wait_ge(S["parts_ready"], 4)
            pe.wait_ge(S["pick_ready"], 1)
            gather(0, 0, None, 0)
            gather(1, 0, None, 0)
            def pair(p, uses, u, r):
                f = 1 if r is not None else u
                pe.wait_ge(S[f"gu_in{u}"], uses * 32 + 32)
                pe.wait_ge(S["hidA"], p + 1)
                pe.wait_ge(S["outA"], p + 1)
                for k in range(KB):
                    if k == 4:
                        pe.wait_ge(S["hidB"], p + 1)
                    for j in range(2):
                        ins = mm(gU[64 * j:64 * j + 64, :], hid[:, u, k, 64 * j:64 * j + 64], gu_w[u][:, j, k, :],
                                 start=(k == 0), stop=(k == KB - 1))
                ins.then_inc(S["gu_done"], 1)
                pe.wait_ge(S["outB"], p + 1)
                scatter(1 - u, False)
                pe.wait_ge(S["gated"], p + 2)
                for n in range(2):
                    tr(gF[:, 128 * n:128 * n + 128], gbuf[:, u, 128 * n:128 * n + 128], ident)
                for n in range(2):
                    ins = tr(gF[:, 256 + 128 * n:256 + 128 * n + 128], pickg[:, u, n, :], ident)
                ins.then_inc(S["flip_done"], 1)
                pe.wait_ge(S["pick_ready"], p + 2)
                gather(0, 0 if r is not None else 1 - u, None, 0)
                pe.wait_ge(S["flipped"], p + 1)
                pe.wait_ge(S[f"dn_in{u}"], uses * 32 + 32)
                for half in range(2):
                    b = (gU, gF)[half]
                    for k in range(2):
                        for j in range(2):
                            ins = mm(b[64 * j:64 * j + 64, :], flip[:, f, 128 * k + 64 * j:128 * k + 64 * j + 64],
                                     dn_w[u][:, j, k, 512 * half:512 * half + 512], start=(k == 0), stop=(k == 1))
                    ins.then_inc(S[("yA", "yB")[half]], 1)
                gather(1, 0 if r is not None else 1 - u, S["dn_free"], 1)

            over_pairs(pe, trips, rest, pair)
            pe.wait_ge(S["outA"], trips * 2 + rest + 1)
            pe.wait_ge(S["outB"], trips * 2 + rest + 1)
            scatter(1, True)

        @block.scalar
        def _(act):
            n_done = [0]

            def act_fn(out_ap, in_ap, f, **kw):
                return nc.scalar.activation(out_ap, in_ap, f, **kw)

            def step(ins):
                n_done[0] += 1
                ins.then_inc(S["astep"], 1)
                act.wait_ge(S["astep"], n_done[0])

            def sqrt(dst, src, scale=1.0, add=EPS):
                act_fn(dst, src, ACT.Sqrt, scale=scale, bias=add).then_inc(S["root_out"], 1)

            roots_in = [0]

            def sqrt_var(ap):
                roots_in[0] += 1
                act.wait_ge(S["root_in"], roots_in[0])
                sqrt(ap, ap)

            def var(t):
                return mv[:, 18 + t:19 + t]

            banks.wait_read(act, "small")
            act_fn(sil[:, :, 0:2], colsT[:, 0:16].rearrange("p (v k) -> p k v", v=2), ACT.Silu).then_inc(S["sil"], 1)
            for t in range(NT):
                sqrt_var(mv[:, 2:3])

            def mod_rows_out(i):
                use = ("mod", i)
                banks.wait_filled(act, use)
                if i >= 2:
                    banks.wait_filled(act, ("modT", i - 2))
                banks.read(act_fn(modrow[:, i % 2, :], banks[use][:, :], ACT.Copy), use)

            for i in range(4):
                mod_rows_out(i)
            act.wait_ge(S["modcols"], 1)
            for k in range(1, KB, 2):
                use = ("xT", k)
                banks.wait_filled(act, use)
                b = banks[use]
                for v, cols in ((1, slice(0, 256)), (0, slice(256, 512))):
                    ins = act_fn(xmT[:, k, cols], b[:, cols], ACT.Identity, bias=modc[:, 2 * k + v:2 * k + v + 1],
                                 scale=modc[:, 16 + 2 * k + v:16 + 2 * k + v + 1])
                banks.read(ins, use)

            def square(g):
                use = ("toTok", g)
                banks.wait_filled(act, use)
                b = banks[use]
                for t in range(4 if g < 8 else 2):
                    ins = act_fn(junk[:, 128 * t:128 * t + 128], b[:, 128 * t:128 * t + 128], ACT.Square, accum_out=ssq[:, 4 * g + t:4 * g + t + 1])
                step(ins)
                r = ssq[:, 4 * g:4 * g + (4 if g < 8 else 2)]
                sqrt(r, r, *((1.0, EPS) if g < 8 else (float(DK), DK * EPS)))

            def copy_out(use, dst, src):
                banks.wait_filled(act, use)
                banks.read(act_fn(dst, src, ACT.Copy), use)

            def tok_part(g):
                if 4 <= g < 8:
                    copy_out(("toTok", g), vtok[:, :, g - 4, :], banks[("toTok", g)][:, :].rearrange("p (t d) -> p t d", t=4))
                else:
                    square(g)

            def chan_part(g):
                if g < 4:
                    copy_out(("toChan", g), kch[:, g, :], banks[("toChan", g)][:, :])
                else:
                    copy_out(("toChan", g), qch[:, g - 8, :], banks[("toChan", g)][:, 0:256])

            act.wait_ge(S["vstep"], 1)
            for g in range(12):
                use = ("gdn", g)
                banks.wait_filled(act, use)
                b = banks[use]
                if g >= 2:
                    act.wait_ge(S["conv_acc"], g - 1)
                if g < 8:
                    ins = act_fn(convbuf[:, g % 2, :, 2:258], b[:, :].rearrange("p (s n) -> p s n", s=2), ACT.Copy)
                else:
                    ins = act_fn(convbuf[:, g % 2, 1, 2:258], b[:, 0:256], ACT.Copy)
                banks.read(ins, use)
                act.wait_ge(S["conv_acc"], g + 1)
                n = 512 if g < 8 else 256
                act_fn(convout[:, g % 2, 0:n], convout[:, g % 2, 0:n], ACT.Silu).then_inc(S["conv_silu"], 1)
                if g >= 2:
                    tok_part(g - 2)
                if g >= 4 and g - 4 not in range(4, 8):
                    chan_part(g - 4)
                if 2 <= g <= 7:
                    mod_rows_out(g + 2)
                if g == 3:
                    act.wait_ge(S["gate_raw"], 1)
                    act_fn(gcol(BETA), gcol(BETA), ACT.Exp, scale=-1.0)
                    act_fn(small_consts[:, 24:32], small_consts[:, 0:8], ACT.Exp)
                    step(act_fn(gcol(SCR), gcol(SCR), ACT.Exp, scale=-1.0))
                    act_fn(gcol(SCR), gcol(SCR), ACT.Ln, bias=1.0).then_inc(S["gate_exp"], 1)
                if g == 5:
                    act.wait_ge(S["decay_arg"], 1)
                    act_fn(gcol(EG), GB[:, 0:32], ACT.Exp)
                    act_fn(gcol(KEND), gcol(SCR), ACT.Exp)
                    act_fn(gcol(EGT), gcol(GT), ACT.Exp).then_inc(S["gexp"], 1)
            tok_part(10)
            mod_rows_out(10)
            tok_part(11)
            mod_rows_out(11)
            for g in (8, 9, 10, 11):
                chan_part(g)
            for n in range(8):
                h, d = n // 2, n % 2
                act.wait_ge(S["dt_arg"], n + 1)
                for t in range(NT):
                    m, col = dtmp[:, n % 2, t, :], 16 * d + 4 * t + h
                    ins = act_fn(m, m, ACT.Exp, bias=gcol(SCR)[:, col:col + 1])
                ins.then_inc(S["dt_exp"], 1)

            def places(use):
                return banks[use][:, :].rearrange("p (n i) -> p n i", n=8)

            def block_diagonal(bd, use):
                banks.wait_filled(act, use)
                for p, corner in corners(bd):
                    ins = act_fn(corner, places(use)[p], ACT.Copy)
                banks.read(ins, use)

            act.wait_ge(S["zeroed"], 2)
            for g in UNITS:
                block_diagonal(Tbd[g], ("T1", g))
            for l in range(1, LEVELS):
                for g in UNITS:
                    if l < LEVELS - 1:
                        block_diagonal(Tbd[g], ("T", l, g))
                    if l == LEVELS - 2:
                        block_diagonal(Ubd[g], ("U", l, g))
                    else:
                        copy_out(("U", l, g), unit(Um, g), places(("U", l, g)))
            for h in range(H):
                use = ("eg", h)
                if h >= 2:
                    act.wait_ge(S["qd_ready"], 2 * (h - 1))
                else:
                    act.wait_ge(S["at_ready"], 8)
                banks.wait_filled(act, use)
                banks.read(act_fn(egb[:, h % 2], banks[use][:, :].rearrange("p (d n) -> p d n", d=2), ACT.Exp), use)
            n_raw = 0

            def decays(h):
                if h == 0:
                    act.wait_ge(S["dist_in"], 16)
                if h >= 2:
                    act.wait_ge(S["decay_ready"], h - 1)
                act.wait_ge(S["ret_arg"], h + 1)
                act_fn(decay[h][:, 0:512], dist[:, 0:512], ACT.Exp, scale=small_consts[:, 16 + h:17 + h])
                act_fn(decayB[:, h % 2], dist[:, 1024:1536], ACT.Exp, scale=small_consts[:, 20 + h:21 + h])
                act_fn(decay[h][:, 512:1024], decay[h][:, 512:1024], ACT.Exp).then_inc(S["decay_exp"], 1)

            for s in range(8):
                if s:
                    for d in range(2):
                        use = ("nw", d, s)
                        copy_out(use, nwT[:, s % 2, d], banks[use][:, 0:256].rearrange("p (h i) -> p h i", h=H))
                if 4 <= s <= 6:
                    decays(s - 4)
                for use in filler()[s]:
                    kind, n = use
                    banks.wait_filled(act, use)
                    b = banks[use]
                    if kind in ("rk", "rq"):
                        if n_raw == 0:
                            act.wait_ge(S["qd_ready"], 8)
                        if n_raw >= 2:
                            act.wait_ge(S["rope_done"], n_raw - 1)
                        if kind == "rk":
                            act_fn(rk[:, n, 0:256], b[:, 0:256], ACT.Copy)
                            ins = act_fn(raw[:, n_raw % 2, 0:256], b[:, 256:512], ACT.Copy)
                        else:
                            ins = act_fn(raw[:, n_raw % 2, 0:256], b[:, 0:256], ACT.Copy)
                        banks.read(ins, use)
                        n_raw += 1
                    elif kind == "rv":
                        banks.read(act_fn(rv[:, n, :], b[:, :], ACT.Copy), use)
                    elif kind == "z":
                        banks.read(act_fn(zs[:, n, :], b[:, :], ACT.Silu), use)
                    else:
                        act.wait_ge(S["rope_done"], 8)
                        banks.read(act_fn(gs[:, n, :], b[:, :], ACT.Silu), use)
            decays(3)
            for t in range(2):
                use = ("o", t)
                banks.wait_filled(act, use)
                b = banks[use]
                for h in range(H):
                    ins = act_fn(junk2[:, 128 * h:128 * h + 128], b[:, 128 * h:128 * h + 128], ACT.Square, accum_out=ssq[:, 4 * t + h:4 * t + h + 1])
                step(ins)
                sqrt(ssq[:, 4 * t:4 * t + 4], ssq[:, 4 * t:4 * t + 4], 1.0 / DK, EPS)
            for i in range(2):
                copy_out(("g1", i), g1b[:, 512 * i:512 * i + 512], banks[("g1", i)][:, :])

            def mixT_out(k):
                copy_out(("mT", k), mixT[:, 2 * k:2 * k + 2, :], banks[("mT", k)][:, :].rearrange("p (k t) -> p k t", k=2))

            mixT_out(0)
            mixT_out(1)
            sqrt_var(mv[:, 8:12])
            sqrt_var(mv[:, 8:12])
            mixT_out(3)
            for t in range(2):
                for i in range(2):
                    sqrt_var(var(t))
                act.wait_ge(S["ln_ready"], t + 1)
                act_fn(h_t[:, t, :], x1[:, t, :], ACT.Identity, scale=var(t), bias=mv[:, 16 + t:17 + t]).then_inc(S["x1n_ready"], 1)
            for k in range(4):
                if k % 2:
                    hT_out(act, k, lambda o, i, sc, bi: act_fn(o, i, ACT.Identity, scale=sc, bias=bi))
            banks.wait_filled(act, "lg")
            act_fn(rt["s"], banks["lg"][:, 0:128].rearrange("p (t e) -> p t e", t=2), ACT.Exp, scale=-1.0).then_inc(emptied[banks.at["lg"][0]], 1)
            for n in range(4):
                t, half = n // 2, n % 2
                use = ("hk", n)
                banks.wait_filled(act, use)
                act_fn(htok[:, n, :], banks[use][:, :], ACT.Copy).then_inc(S["htok_ready"], 1)
                act_fn(hparts[0][:, t, 512 * half:512 * half + 512], banks[use][:, :], ACT.Copy).then_inc(emptied[banks.at[use][0]], 1)
            for t in range(2):
                if t:
                    for i in range(2):
                        copy_out(("g2", i), g2b[:, 512 * i:512 * i + 512], banks[("g2", i)][:, :])
                banks.wait_filled(act, ("sh", t))
                act_fn(sa[:, t, :], banks[("sh", t)][:, 0:256], ACT.Silu).then_inc(S["sh_silu"], 1)
            for t in range(2):
                use = ("shT", t)
                copy_out(use, shgT[:, :, 128 * t:128 * t + 128], banks[use][:, 0:256].rearrange("p (k t) -> p k t", k=2))

            act.wait_ge(S["table_ready"], 1)
            trips, rest = trips_of(act)
            act.wait_ge(S["gatherA"], 1)
            act_fn(hid[:, 0, 0:4, :], psum[4][:, :].rearrange("p (k s) -> p k s", k=4), ACT.Copy).then_inc(S["hidA"], 1)
            def pair(p, uses, u, r):
                n = 1 - u if r is None else 0
                act.wait_ge(S["gu_done"], p + 1)
                act.wait_ge(S["gated"], p + 1)
                act_fn(sa[:, 0, :], psum[6][:, 0:256], ACT.Silu).then_inc(S["silu_done"], 1)
                act.wait_ge(S["gatherA"], p + 2)
                act_fn(hid[:, n, 0:4, :], psum[4][:, :].rearrange("p (k s) -> p k s", k=4), ACT.Copy).then_inc(S["hidA"], 1)
                act.wait_ge(S["yA"], p + 1)
                act.wait_ge(S["scattered"], p + 1)
                act_fn(ybuf[:, 0:512], psum[6][:, :], ACT.Copy).then_inc(S["outA"], 1)

            over_pairs(act, trips, rest, pair)
            for t in range(2):
                sqrt_var(var(t))
                if t == 0:
                    act.wait_ge(S["last_ready"], 1)
                    act_fn(h_t[:, 0, :], h_t[:, 0, :], ACT.Identity, scale=var(0), bias=mv[:, 16:17]).then_inc(S["last_normed"], 1)

        @block.vector
        def _(dve):
            V = nc.vector
            n_done = [0]

            def step(ins):
                n_done[0] += 1
                ins.then_inc(S["vstep"], 1)
                dve.wait_ge(S["vstep"], n_done[0])

            n_roots = [0]

            def rooted(ap):
                n_roots[0] += 1
                dve.wait_ge(S["root_out"], n_roots[0])
                step(V.reciprocal(ap, ap))

            def layernorm(dst, src):
                s0 = st[:, 0:12].rearrange("p (a n) -> p a n", a=2)
                for i in range(2):
                    ins = V.bn_stats(s0[:, i, :], src[:, 512 * i:512 * i + 512])
                step(ins)
                step(V.bn_aggr(mv[:, 0:2], s0))
                V.tensor_copy(mv[:, 2:3], mv[:, 1:2]).then_inc(S["root_in"], 1)
                rooted(mv[:, 2:3])
                return V.tensor_scalar(dst, src, mv[:, 0:1], mv[:, 2:3], ALU.subtract, ALU.mult)

            def bct(ap, n, m):
                return ap.unsqueeze(2).to_broadcast([ap.shape[0], n, m])

            V.memset(sil, 0.0)
            step(V.memset(A(41984, 1040), 0.0))
            banks.wait_filled(dve, "small")
            banks.read(V.tensor_copy(colsT[:, :], banks["small"][:, 0:64]), "small")
            for t in range(NT):
                dve.wait_ge(S["x_in"], 64)
                layernorm(xall[:, t, :], xall[:, t, :]).then_inc(S["xn"], 1)
            banks.wait_filled(dve, "convw")
            banks.read(V.tensor_copy(convw[:, :], banks["convw"][:, 0:60]), "convw")
            banks.wait_read(dve, "small")

            def mod_bias(i):
                use = ("modT", i)
                banks.wait_filled(dve, use)
                banks.read(V.scalar_tensor_tensor(
                    out=modc[:, 8 * i:8 * i + 8].rearrange("p (m v) -> p m v", v=2),
                    in0=banks[use][:, 0:8].rearrange("p (m v) -> p m v", v=2), scalar=1.0 if i in (2, 3, 8, 9) else 0.0,
                    in1=bct(colsT[:, 16 + 4 * i:20 + 4 * i], 4, 2), op0=ALU.add, op1=ALU.add), use)

            for i in range(4):
                mod_bias(i)
            banks.wait_read(dve, ("modT", 3))
            V.memset(st[:, 60:61], 0.0).then_inc(S["modcols"], 1)
            for k in range(0, KB, 2):
                use = ("xT", k)
                banks.wait_filled(dve, use)
                b = banks[use]
                for v, cols in ((1, slice(0, 256)), (0, slice(256, 512))):
                    ins = V.tensor_scalar(xmT[:, k, cols], b[:, cols], modc[:, 16 + 2 * k + v:17 + 2 * k + v],
                                          modc[:, 2 * k + v:2 * k + v + 1], ALU.mult, ALU.add)
                banks.read(ins, use)

            def conv(g):
                dve_in = convbuf[:, g % 2, :, :] if g < 8 else convbuf[:, g % 2, 1:2, :]
                banks.wait_read(dve, ("gdn", g))
                if g >= 2:
                    banks.wait_filled(dve, ("toTok", g - 2))
                n = 2 if g < 8 else 1
                o = convout[:, g % 2, 0:256 * n].rearrange("p (s n) -> p s n", s=n)
                tile = {0: 4, 1: 8, 2: 0}[g // 4] + g % 4
                for j in range(5):
                    src, w = dve_in[:, :, j:j + 256], convw[:, 5 * tile + j:5 * tile + j + 1]
                    if j == 0:
                        ins = V.tensor_scalar(o, src, w, None, ALU.mult)
                    else:
                        ins = V.scalar_tensor_tensor(out=o, in0=src, scalar=w, in1=o, op0=ALU.mult, op1=ALU.add)
                    if j < 4:
                        step(ins)
                ins.then_inc(S["conv_acc"], 1)

            def tok_part(g):
                if 4 <= g < 8:
                    return
                use = ("toTok", g)
                n = 4 if g < 8 else 2
                r = ssq[:, 4 * g:4 * g + n]
                rooted(r)
                if g < 8:
                    dst = ktok[:, :, g, :]
                else:
                    if g >= 10:
                        banks.wait_filled(dve, ("toChan", g - 2))
                    dst = qtok[:, g % 2, :, :]
                banks.read(V.tensor_tensor(dst, banks[use][:, 0:128 * n].rearrange("p (t d) -> p t d", t=n), bct(r, n, 128), ALU.mult), use)

            for g in range(12):
                conv(g)
                if g >= 2:
                    tok_part(g - 2)
                if 3 <= g <= 8:
                    mod_bias(g + 1)
                if g == 3:
                    banks.wait_filled(dve, "ba")
                    b = banks["ba"][:, 0:64].rearrange("p (t w d h) -> p w t d h", t=4, w=2, d=2)

                    def dth(m, d):
                        return m.rearrange("p (d t h) -> p d t h", d=2, t=4)[:, d]
                    for d in range(2):
                        V.tensor_copy(dth(gcol(BETA), d), b[:, 0, :, d, :])
                        ins = V.tensor_tensor(dth(gcol(GRAW), d), b[:, 1, :, d, :],
                                              small_consts[:, 8 + 4 * d:12 + 4 * d].unsqueeze(1).to_broadcast([128, 4, 4]), ALU.add)
                    banks.read(ins, "ba")
                    banks.wait_read(dve, "ba")
                    V.scalar_tensor_tensor(out=gcol(SCR), in0=gcol(GRAW), scalar=-1.0, in1=gcol(GRAW), op0=ALU.mult, op1=ALU.max).then_inc(S["gate_raw"], 1)
                if g == 4:
                    dve.wait_ge(S["gate_exp"], 1)
                    V.tensor_scalar(gcol(BETA), gcol(BETA), 1.0, None, ALU.add)
                    step(V.scalar_tensor_tensor(out=gcol(GRAW), in0=gcol(GRAW), scalar=0.0, in1=gcol(SCR), op0=ALU.max, op1=ALU.add))
                    step(V.reciprocal(GB[:, 32:64], gcol(BETA)))
                    V.tensor_copy(gcol(BETA), GB[:, 32:64])
                    for d in range(2):
                        m = gcol(GRAW).rearrange("p (d t h) -> p d t h", d=2, t=4)[:, d]
                        ins = V.scalar_tensor_tensor(out=m, in0=m, scalar=-1.0,
                                                     in1=small_consts[:, 24 + 4 * d:28 + 4 * d].unsqueeze(1).to_broadcast([128, 4, 4]),
                                                     op0=ALU.mult, op1=ALU.mult)
                    ins.then_inc(S["gates_ready"], 1)
                if g == 5:
                    banks.wait_filled(dve, "gcum")
                    V.tensor_copy(GB[:, 0:32], banks["gcum"][:, 0:32])
                    banks.read(V.tensor_copy(gcol(GT), banks["gcum"][:, 32:64]), "gcum")
                    banks.wait_read(dve, "gcum")
                    V.tensor_copy(GBt[:, :].rearrange("p (t x h) -> p x t h", x=4, h=H), GB[:, :].rearrange("p (x t h) -> p x t h", x=4, h=H))
                    V.tensor_tensor(gcol(SCR), gcol(GT), GB[:, 0:32], ALU.subtract).then_inc(S["decay_arg"], 1)
                if g == 6:
                    dve.wait_ge(S["gexp"], 1)
                    V.tensor_scalar(gcol(SCR), GB[:, 0:32], -1.0, None, ALU.mult)
                    V.scalar_tensor_tensor(out=gcol(NBEG), in0=gcol(BETA), scalar=-1.0, in1=gcol(EG), op0=ALU.mult, op1=ALU.mult)
                    banks.wait_filled(dve, "rows")
                    banks.read(V.tensor_copy(rowsT, banks["rows"][0:16, :]), "rows")
                    banks.wait_filled(dve, "gend")
                    banks.read(V.tensor_copy(ge[:, :], banks["gend"][:, 0:64]), "gend")
            tok_part(10)
            tok_part(11)
            mod_bias(10)
            mod_bias(11)


            def dt_argument(n):
                h, d = n // 2, n % 2
                use = ("bc", d, h)
                banks.wait_filled(dve, use)
                m = dtmp[:, n % 2]
                V.tensor_tensor(m, banks[use][:, 0:256].rearrange("p (t i) -> p t i", t=4), cst["neg"][:, 64 * d:64 * d + 64].unsqueeze(1).to_broadcast([128, 4, 64]), ALU.add).then_inc(S["dt_arg"], 1)

            def i64(n):
                return cst["i64"].unsqueeze(1).to_broadcast([128, n, 64])

            def dt_finish(n):
                h, d = n // 2, n % 2
                use = ("bc", d, h)
                dve.wait_ge(S["dt_exp"], n + 1)
                m = dtmp[:, n % 2]
                L, At = LT[:, d, h], AT[:, d, h]
                kk = banks[("kk", h)]
                step(V.tensor_tensor(At, m[:, 2:4, :], i64(2), ALU.add))
                ins = V.tensor_tensor(L, m, banks[use][:, 256:512].rearrange("p (t i) -> p t i", t=4), ALU.mult)
                banks.read(ins, use)
                ins = V.tensor_tensor(At, At, kk[:, 256:384].rearrange("p (t i) -> p t i", t=2), ALU.mult)
                ins.then_inc(S["at_ready"], 1)
                banks.wait_read(dve, use)
                ins = V.tensor_tensor(L, L, kk[:, 0:256].rearrange("p (t i) -> p t i", t=4), ALU.mult)
                if d:
                    banks.read(ins, ("kk", h))
                    banks.wait_read(dve, ("kk", h))
                else:
                    step(ins)
                step(V.tensor_tensor(L, L, i64(4), ALU.add))

            for n in range(9):
                if n < 8:
                    if n % 2 == 0:
                        banks.wait_filled(dve, ("kk", n // 2))
                    dt_argument(n)
                if n:
                    dt_finish(n - 1)
                if n in (4, 8):
                    V.memset(st[:, 62:63], 0.0).then_inc(S["lt_ready"], 1)
            first_U(V, UNITS[3], lambda ins: None)
            dve.wait_ge(S["zeroed"], 3)
            for l in range(1, LEVELS):
                for g in UNITS:
                    use = ("X", l, g)
                    banks.wait_filled(dve, use)
                    b = banks[use][:, :].rearrange("p (n i) -> p n i", n=8)
                    o = 64 * (2 * l + g // 2)
                    mask = cst["ymask"][:, o:o + 64].unsqueeze(1).to_broadcast([128, 8, 64])
                    if l < LEVELS - 1:
                        for p, corner in corners(Ybd[g]):
                            V.tensor_tensor(corner, b[p], mask[p], ALU.mult)
                    banks.read(V.tensor_tensor(unit(Ym, g), b, mask, ALU.mult), use)
            for h in range(H):
                banks.wait_read(dve, ("eg", h))
                for d in range(2):
                    V.tensor_tensor(qdec[:, d, h, :], egb[:, h % 2, d, :], qch[:, h, :], ALU.mult).then_inc(S["qd_ready"], 1)

            def decay_argument(h):
                if h == 0:
                    dve.wait_ge(S["dist_in"], 16)
                m = decay[h][:, 512:1024]
                step(V.tensor_scalar(m, dist[:, 512:1024], small_consts[:, 16 + h:17 + h], None, ALU.mult))
                V.scalar_tensor_tensor(out=m, in0=dist[:, 1536:2048], scalar=small_consts[:, 20 + h:21 + h], in1=m,
                                       op0=ALU.mult, op1=ALU.add).then_inc(S["ret_arg"], 1)

            def decay_finish(h):
                dve.wait_ge(S["decay_exp"], h + 1)
                for k in range(2):
                    m = decay[h][:, 512 + 384 * k:640 + 384 * k]
                    V.tensor_tensor(m, m, ident, ALU.add)
                V.tensor_tensor(decay[h][:, 0:512], decay[h][:, 0:512], decayB[:, h % 2], ALU.add).then_inc(S["decay_ready"], 1)

            n_rope = 0
            for s in range(8):
                use = ("u", s)
                banks.wait_filled(dve, use)
                for d in range(2):
                    t, c = where(d, s)
                    p = slice(64 * c, 64 * c + 64)
                    ins = V.tensor_copy(usav[p, d, t % 2], banks[use][p, :].rearrange("p (h e) -> p h e", h=H))
                banks.read(ins, use)
                for f in filler()[s]:
                    if f[0] in ("rk", "rq"):
                        banks.wait_read(dve, f)
                        r, dst = raw[:, n_rope % 2, :], (rk[:, f[1], 256:512] if f[0] == "rk" else rq[:, f[1], :])
                        V.tensor_tensor(r[0:64, 256:512], r[64:128, 0:256], cst["sin"][64:128, :], ALU.mult)
                        V.tensor_tensor(r[64:128, 256:512], r[0:64, 0:256], cst["sin"][0:64, :], ALU.mult)
                        step(V.tensor_tensor(dst, r[:, 0:256], cst["cos"], ALU.mult))
                        V.tensor_tensor(dst, dst, r[:, 256:512], ALU.add).then_inc(S["rope_done"], 1)
                        n_rope += 1
                if s < 7:
                    for d in range(2):
                        use = ("S", d, s)
                        banks.wait_filled(dve, use)
                        b = banks[use][:, :].rearrange("p (h e) -> p h e", h=H)
                        nxt = state[:, (s + 1) % 4, d]
                        if s == 0:
                            banks.read(V.tensor_copy(nxt, b), use)
                        else:
                            dve.wait_ge(S["s_scaled"], 2 * (s - 1) + d + 1)
                            banks.read(V.tensor_tensor(nxt, nxt, b, ALU.add), use)
                if 3 <= s <= 5:
                    decay_argument(s - 3)
                if 4 <= s <= 6:
                    decay_finish(s - 4)
            decay_argument(3)
            decay_finish(3)
            dve.wait_ge(S["gains_ready"], 4)
            def delta_out(t):
                use = ("o", t)
                r = ssq[:, 4 * t:4 * t + 4]
                rooted(r)
                m = mix[:, t, 0:512]
                m4 = m.rearrange("p (h e) -> p h e", h=H)
                banks.read(V.tensor_tensor(m4, banks[use][:, :].rearrange("p (h e) -> p h e", h=H), bct(r, 4, 128), ALU.mult), use)
                banks.wait_read(dve, use)
                V.tensor_tensor(m, m, zs[:, t, :], ALU.mult).then_inc(S["mix_ready"], 1)
            def scores(h):
                dve.wait_ge(S["decay_ready"], h + 1)
                for q in range(2):
                    use = ("sc", h, q)
                    banks.wait_filled(dve, use)
                    m = decay[h][:, 512 * q:512 * q + 512]
                    banks.read(V.scalar_tensor_tensor(out=m, in0=banks[use][:, :], scalar=DK ** -0.5, in1=m, op0=ALU.mult, op1=ALU.mult), use)

            delta_out(0)
            scores(0)
            delta_out(1)
            for h in range(1, H):
                scores(h)
            for t in range(2):
                use = ("ro", t)
                banks.wait_filled(dve, use)
                b = banks[use]
                for h in range(H):
                    ins = V.bn_stats(st[:, 6 * h:6 * h + 6], b[:, 128 * h:128 * h + 128])
                step(ins)
                for h in range(H):
                    ins = V.bn_aggr(mv[:, 2 * h:2 * h + 2], st[:, 6 * h:6 * h + 6])
                step(ins)
                V.tensor_copy(mv[:, 8:12], mv[:, 1:8:2]).then_inc(S["root_in"], 1)
                rooted(mv[:, 8:12])
                for h in range(H):
                    ins = V.tensor_scalar(mix[:, t, 512 + 128 * h:640 + 128 * h], b[:, 128 * h:128 * h + 128],
                                          mv[:, 2 * h:2 * h + 1], mv[:, 8 + h:9 + h], ALU.subtract, ALU.mult)
                banks.read(ins, use)
                banks.wait_read(dve, use)
                m = mix[:, t, 512:1024]
                V.tensor_tensor(m, m, gs[:, t, :], ALU.mult).then_inc(S["mix_ready"], 1)
            use = ("mT", 2)
            banks.wait_filled(dve, use)
            banks.read(V.tensor_copy(mixT[:, 4:6, :], banks[use][:, :].rearrange("p (k t) -> p k t", k=2)), use)
            for i in range(2):
                banks.wait_read(dve, ("g1", i))
            dve.wait_ge(S["xres_in"], 32)
            dve.wait_ge(S["lnrows_in"], 32)

            def var(t):
                return mv[:, 18 + t:19 + t]

            def halves(t):
                return [(half, slice(512 * half, 512 * half + 512), st[:, 12 * t + 6 * half:12 * t + 6 * half + 6]) for half in range(2)]

            def variance(t):
                step(V.bn_aggr(mv[:, 2 * t:2 * t + 2], st[:, 12 * t:12 * t + 12].rearrange("p (a n) -> p a n", a=2)))
                V.tensor_copy(var(t), mv[:, 2 * t + 1:2 * t + 2]).then_inc(S["root_in"], 1)

            def residual(t, arrived, y, used, gate, res):
                for half, cols, stat in halves(t):
                    arrived(half)
                    used(V.tensor_tensor(h_t[:, t, cols], y(half), gate[:, cols], ALU.mult), half)
                    step(V.scalar_tensor_tensor(out=h_t[:, t, cols], in0=res[:, cols], scalar=ALPHA, in1=h_t[:, t, cols],
                                                op0=ALU.mult, op1=ALU.add))
                    ins = V.bn_stats(stat, h_t[:, t, cols])
                step(ins)
                variance(t)

            def affine(t, dst):
                m = h_t[:, t, :]
                step(V.scalar_tensor_tensor(out=m, in0=m, scalar=mv[:, 2 * t:2 * t + 1], in1=lnr[:, 0:1024], op0=ALU.subtract, op1=ALU.mult))
                rooted(var(t))
                return V.scalar_tensor_tensor(out=dst, in0=m, scalar=var(t), in1=lnr[:, 1024:2048], op0=ALU.mult, op1=ALU.add)

            def shift(t):
                rooted(var(t))
                return V.scalar_tensor_tensor(out=mv[:, 16 + t:17 + t], in0=mv[:, 2 * t:2 * t + 1], scalar=-1.0, in1=var(t),
                                              op0=ALU.mult, op1=ALU.mult)

            for t in range(2):
                def y_used(ins, half):
                    banks.read(ins, ("y", half, t))
                    banks.wait_read(dve, ("y", half, t))

                residual(t, lambda half: banks.wait_filled(dve, ("y", half, t)), lambda half: banks[("y", half, t)][:, :],
                         y_used, g1b, xres[:, t, :])
                step(affine(t, x1[:, t, :]))
                for half, cols, stat in halves(t):
                    ins = V.bn_stats(stat, x1[:, t, cols])
                step(ins)
                variance(t)
                shift(t).then_inc(S["ln_ready"], 1)
            for k in (0, 2):
                hT_out(dve, k, lambda o, i, sc, bi: V.tensor_scalar(o, i, sc, bi, ALU.mult, ALU.add))

            def shared_gate(t):
                use = ("sh", t)
                dve.wait_ge(S["sh_silu"], t + 1)
                V.tensor_tensor(sa[:, t, :], sa[:, t, :], banks[use][:, 256:512], ALU.mult).then_inc(emptied[banks.at[use][0]], 1)
                banks.wait_read(dve, use)
                V.memset(st[:, 60 + t:61 + t], 0.0).then_inc(S["sh_gated"], 1)

            s_, sb, masked, work, sel, gate, posx, max8 = (rt[n] for n in ("s", "sb", "masked", "work", "sel", "gate", "posx", "max8"))
            banks.wait_read(dve, "lg")
            dve.wait_ge(S["rbias_in"], 16)
            step(V.tensor_scalar(s_, s_, 1.0, None, ALU.add))
            step(V.reciprocal(s_, s_))
            step(V.tensor_tensor(sb, s_, rbias.unsqueeze(1).to_broadcast([128, 2, 64]), ALU.add))
            for t in range(2):
                for g in range(GROUPS):
                    ins = V.max(max8[:, t, 8 * g:8 * g + 8], sb[:, t, 8 * g:8 * g + 8])
            step(ins)
            gsc, gm8, gwork, gpen = (g8[:, 16 * i:16 * i + 16].rearrange("p (t g) -> p t g", t=2) for i in range(4))
            step(V.tensor_tensor(gsc, max8[:, :, 0:64:8], max8[:, :, 1:64:8], ALU.add))
            for t in range(2):
                ins = V.max(gm8[:, t, :], gsc[:, t, :])
            step(ins)
            step(V.memset(gm8[:, :, TOPG:8], 1e30))
            for t in range(2):
                ins = V.match_replace(gwork[:, t, :], gm8[:, t, :], gsc[:, t, :], -1e30)
            step(ins)
            step(V.tensor_scalar(gwork, gwork, -1e29, None, ALU.is_lt))
            step(V.tensor_scalar(gpen, gwork, -1.0, 1e30, ALU.add, ALU.mult))

            def by_expert(m, t):
                return m[:, t, :].rearrange("p (g e) -> p g e", g=GROUPS)

            for t in range(2):
                ins = V.tensor_tensor(by_expert(masked, t), by_expert(sb, t), gwork[:, t, :].unsqueeze(2).to_broadcast([128, 8, 8]), ALU.mult)
            step(ins)
            for t in range(2):
                ins = V.tensor_tensor(by_expert(masked, t), by_expert(masked, t), gpen[:, t, :].unsqueeze(2).to_broadcast([128, 8, 8]), ALU.add)
            step(ins)
            for t in range(2):
                ins = V.max(gm8[:, t, :], masked[:, t, :])
            step(ins)
            for t in range(2):
                ins = V.match_replace(work[:, t, :], gm8[:, t, :], masked[:, t, :], -3e38)
            step(ins)
            step(V.tensor_scalar(sel, work, -2e38, None, ALU.is_lt))
            V.memset(st[:, 60:61], 0.0).then_inc(S["sel_ready"], 1)
            V.tensor_tensor(gate, s_, sel, ALU.mult)
            banks.wait_filled(dve, "cnt")
            banks.read(V.tensor_copy(route[0:64, 0:1], banks["cnt"][0:64, 0:1]), "cnt")
            banks.wait_read(dve, "cnt")
            for r in range(T // CAP):
                ins = V.tensor_scalar(route[0:64, 1 + r:2 + r], route[0:64, 0:1], float(CAP * r), None, ALU.is_gt)
            step(ins)
            V.tensor_reduce(route[0:64, 8:9], route[0:64, 1:5], mybir.AxisListType.X, ALU.add).then_inc(S["counts_ready"], 1)
            dve.wait_ge(S["counts_ready"], 1)
            step(V.tensor_reduce(st[:, 40:42], gate, mybir.AxisListType.X, ALU.add))
            V.reciprocal(st[:, 42:44], st[:, 40:42]).then_inc(S["vstep"], 1)
            n_done[0] += 1
            banks.wait_filled(dve, "start")
            banks.read(V.tensor_copy(route[0:64, 9:10], banks["start"][0:64, 0:1]), "start")
            banks.wait_read(dve, "start")
            V.tensor_scalar(route[0:64, 11:12], route[0:64, 9:10], float(CAP), None, ALU.mult)
            V.tensor_tensor(route[0:64, 10:11], route[0:64, 9:10], route[0:64, 8:9], ALU.add)
            step(V.tensor_scalar(onehot, cst["item"][0:64, :], route[0:64, 9:10], None, ALU.is_ge))
            V.scalar_tensor_tensor(out=onehot, in0=cst["item"][0:64, :], scalar=route[0:64, 10:11], in1=onehot,
                                   op0=ALU.is_lt, op1=ALU.mult).then_inc(S["onehot_ready"], 1)
            V.scalar_tensor_tensor(out=gate, in0=gate, scalar=2.5, in1=bct(st[:, 42:44], 2, 64), op0=ALU.mult, op1=ALU.mult)
            banks.wait_filled(dve, "rank")
            banks.read(V.scalar_tensor_tensor(out=posx, in0=banks["rank"][:, 0:128].rearrange("p (t e) -> p t e", t=2), scalar=BIG,
                                              in1=sel, op0=ALU.add, op1=ALU.mult), "rank")
            banks.wait_read(dve, "rank")
            V.tensor_scalar(posx, posx, -BIG, None, ALU.add).then_inc(S["posx_ready"], 1)
            banks.wait_filled(dve, "itrow")
            V.tensor_copy(eidx[0:1, 0:ITEMS], banks["itrow"][0:1, 0:ITEMS])
            banks.read(V.tensor_scalar(eidx[0:1, ITEMS:ITEMS + 1], banks["itrow"][0:1, ITEMS:ITEMS + 1], -1.0, None, ALU.add), "itrow")
            banks.wait_read(dve, "itrow")
            V.memset(st[:, 62:63], 0.0).then_inc(S["eidx_ready"], 1)
            shared_gate(0)
            banks.wait_filled(dve, "selT")
            b = banks["selT"]
            V.tensor_scalar(itemT[:, 0:256], b[0:64, 0:256], route[0:64, 11:12], None, ALU.add)
            banks.read(V.tensor_copy(itemT[:, 256:512], b[0:64, 256:512]), "selT")
            banks.wait_read(dve, "selT")
            V.memset(st[:, 61:62], 0.0).then_inc(S["items_ready"], 1)
            banks.wait_filled(dve, "item")
            b = banks["item"][:, 0:4 * ITEMS].rearrange("p (w t i) -> p w t i", w=2, t=2)
            V.tensor_tensor(tabv[:, 0], b[:, 0], cst["item64"].unsqueeze(1).to_broadcast([128, 2, ITEMS]), ALU.subtract)
            banks.read(V.tensor_copy(tabv[:, 1], b[:, 1]), "item")
            banks.wait_read(dve, "item")
            V.memset(st[:, 63:64], 0.0).then_inc(S["table_ready"], 1)
            shared_gate(1)

            def choose(buf, col):
                rank = tabv[:, 0, :, col].unsqueeze(3).to_broadcast([128, 2, 2, 64])
                wgt = tabv[:, 1, :, col].unsqueeze(3).to_broadcast([128, 2, 2, 64])
                io = cst["iota64"].unsqueeze(1).unsqueeze(1).to_broadcast([128, 2, 2, 64])
                o = pick[:, buf].rearrange("p t (j s) -> p t j s", j=2)
                og = pickg[:, buf].rearrange("p t (j s) -> p t j s", j=2)
                ins = V.tensor_tensor(o, io, rank, ALU.is_equal)
                return ins, lambda: V.tensor_tensor(og, o, wgt, ALU.mult)

            dve.wait_ge(S["parts_ready"], 4)
            V.memset(flip[:, 1, :], 0.0).then_inc(S["gated"], 1)
            V.memset(ybuf[:, 0:512], 0.0).then_inc(S["outA"], 1)
            V.memset(ybuf[:, 512:1024], 0.0).then_inc(S["outB"], 1)
            ins, weigh = choose(0, slice(0, 2))
            step(ins)
            weigh().then_inc(S["pick_ready"], 1)
            trips, rest = trips_of(dve)
            dve.wait_ge(S["gatherB"], 1)
            V.tensor_copy(hid[:, 0, 4:8, :], psum[5][:, :].rearrange("p (k s) -> p k s", k=4)).then_inc(S["hidB"], 1)
            chosen = n_done[0]
            def pair(p, uses, u, r):
                n = 1 - u if r is None else 0

                def next_picks():
                    ins, weigh = choose(n, bass.ds(p * 2 + 2, 2))
                    ins.then_inc(S["vstep"], 1)
                    dve.wait_ge(S["vstep"], p + (1 + chosen))
                    weigh().then_inc(S["pick_ready"], 1)

                if r is None:
                    next_picks()
                dve.wait_ge(S["silu_done"], p + 1)
                V.tensor_tensor(gbuf[:, u, :], sa[:, 0, :], psum[6][:, 256:512], ALU.mult).then_inc(S["gated"], 1)
                dve.wait_ge(S["flip_done"], p + 1)
                V.tensor_copy(flip[:, 1 if r is not None else u, :], psum[7][:, :]).then_inc(S["flipped"], 1)
                if r is not None:
                    next_picks()
                dve.wait_ge(S["yB"], p + 1)
                dve.wait_ge(S["scattered"], p + 1)
                V.tensor_copy(ybuf[:, 512:1024], psum[7][:, :]).then_inc(S["outB"], 1)
                dve.wait_ge(S["gatherB"], p + 2)
                V.tensor_copy(hid[:, n, 4:8, :], psum[5][:, :].rearrange("p (k s) -> p k s", k=4)).then_inc(S["hidB"], 1)

            over_pairs(dve, trips, rest, pair)
            n_done[0] = 0
            dve.wait_ge(S["acc_ready"], 1)
            dve.wait_ge(S["ln2_in"], 32)
            for i in range(2):
                banks.wait_read(dve, ("g2", i))

            def last_step(ins):
                n_done[0] += 1
                ins.then_inc(S["final_norm"], 1)
                dve.wait_ge(S["final_norm"], n_done[0])
            step = last_step
            for t in range(2):
                residual(t, lambda half: dve.wait_ge(S["acc_ready"], 2 * t + half + 1), lambda half: psum[2 * t + half][:, :],
                         lambda ins, half: step(ins), g2b, x1[:, t, :])
                if t == 0:
                    shift(t).then_inc(S["last_ready"], 1)
                else:
                    affine(t, h_t[:, t, :]).then_inc(S["out_ready"], 1)

        @block.gpsimd
        def _(pool):
            G = nc.gpsimd
            n_done = [0]

            def step(ins):
                n_done[0] += 1
                ins.then_inc(S["pstep"], 1)
                pool.wait_ge(S["pstep"], n_done[0])

            def inputs(s):
                if s == 0:
                    banks.wait_filled(pool, ("X", LEVELS - 1, 3))
                    banks.wait_read(pool, ("toTok", 7))
                if s >= 2:
                    banks.wait_filled(pool, ("S", 1, s - 2))
                for n, (src, w, dst) in enumerate(((vtok, BETA, vbeta), (ktok, NBEG, kbeta), (ktok, KEND, kend))):
                    for d in range(2):
                        t, c = where(d, s)
                        p = slice(64 * c, 64 * c + 64)
                        o = 16 * d + 4 * t
                        ins = G.tensor_tensor(dst[p, s % 2], src[p, t], gcol(w)[p, o:o + 4].unsqueeze(2).to_broadcast([64, 4, 128]), ALU.mult)
                        if (n, d) != (2, 1):
                            step(ins)
                ins.then_inc(S["step_in"], 1)
                pool.wait_ge(S["step_in"], s + 1)

            banks.wait_filled(pool, ("xT", KB - 1))
            G.memset(A(12288, 4096), 0.0).then_inc(S["zeroed"], 1)
            G.memset(A(28672, 4096), 0.0).then_inc(S["zeroed"], 1)
            banks.wait_read(pool, ("toTok", 11))
            G.memset(A(41984, 3072), 0.0)
            G.memset(Ybd[3], 0.0).then_inc(S["zeroed"], 1)
            for n in range(3):
                pool.wait_ge(S["lt_ready"], n // 2 + 1)
                first_U(G, UNITS[n], step)
            inputs(0)
            inputs(1)
            for s in range(1, 8):
                if s < 7:
                    for d in range(2):
                        banks.wait_read(pool, ("S", d, s - 1))
                        t, c = where(d, s)
                        o = 32 * c + 16 * d + 4 * t
                        G.tensor_tensor(state[:, (s + 1) % 4, d], state[:, s % 4, d], ge[:, o:o + 4].unsqueeze(2).to_broadcast([128, 4, 128]),
                                        ALU.mult).then_inc(S["s_scaled"], 1)
                    pool.wait_ge(S["s_scaled"], 2 * s)
                    inputs(s + 1)
            pool.wait_ge(S["norms_in"], 32)
            for t in range(2):
                banks.wait_read(pool, ("z", t))
                m4 = zs[:, t, :].rearrange("p (h e) -> p h e", h=H)
                G.tensor_tensor(m4, m4, norms[:, 0:128].unsqueeze(1).to_broadcast([128, 4, 128]), ALU.mult).then_inc(S["gains_ready"], 1)
            for t in range(2):
                banks.wait_read(pool, ("gt", t))
                G.tensor_tensor(gs[:, t, :], gs[:, t, :], norms[:, 128:640], ALU.mult).then_inc(S["gains_ready"], 1)
            for n in range(4):
                t, cols = n // 2, slice(512 * (n % 2), 512 * (n % 2) + 512)
                m = htok[:, n, :]
                pool.wait_ge(S["htok_ready"], n + 1)
                banks.wait_read(pool, ("hk", n))
                step(G.tensor_tensor(m, m, hparts[0][:, t, cols], ALU.subtract))
                step(G.tensor_copy(hparts[1][:, t, cols], m))
                G.tensor_tensor(hparts[2][:, t, cols], m, hparts[1][:, t, cols], ALU.subtract).then_inc(S["parts_ready"], 1)
            pool.wait_ge(S["last_normed"], 1)
            step(G.tensor_tensor(h_t[:, 0, :], h_t[:, 0, :], lnr[:, 0:1024], ALU.mult))
            G.tensor_tensor(h_t[:, 0, :], h_t[:, 0, :], lnr[:, 1024:2048], ALU.add).then_inc(S["last_ready"], 1)



NAMES = ["x", "c", "ctx", "c_ctx", "w_mod", "b_mod", "w_in", "conv_w", "gdn_a_log", "gdn_dt_bias", "gdn_norm_g",
         "ret_log_gamma", "ret_norm_g", "w_out", "ln1_g", "ln1_b", "w_router", "router_bias", "w_gate_up", "w_down",
         "w_shared_gate_up", "w_shared_down", "ln2_g", "ln2_b"]


def build(nc, shapes):
    a = {n: nc.dram_tensor(n, s, F32, kind="ExternalInput").ap() for n, s in shapes.items()}
    out = nc.dram_tensor("out", (1, T, D), F32, kind="ExternalOutput").ap()
    program(nc, a, out)


def kernel(**inputs):
    import concourse.bacc as bacc
    from concourse.bass_utils import run_bass_kernel_spmd

    arrays = {n: np.ascontiguousarray(inputs[n]) for n in NAMES}
    arrays["const"], arrays["dist"] = constants()
    nc = bacc.Bacc("TRN2", target_bir_lowering=False, num_devices=1)
    build(nc, {n: v.shape for n, v in arrays.items()})
    r = run_bass_kernel_spmd(nc, [arrays], core_ids=[0])
    return r.results[0]["out"]
```
